# Optimizing a Trainium2 kernel written in Bass

```python
import math
import jax, jax.numpy as jnp
from jax import lax
import numpy as np

D_MODEL = 1024
BATCH = 1
SEQ = 1024
DEPTH = 1

D_MIX = D_MODEL
POOL_WINDOWS = (2, 4, 8, 16)
POOL_GROUPS = len(POOL_WINDOWS)
POOL_CH = 64
POOL_WIDTH = POOL_GROUPS * POOL_CH
MAX_WIN = max(POOL_WINDOWS)
HGRN_WIDTH = D_MIX - POOL_WIDTH
HGRN_HEAD_DIM = 128
HGRN_HEADS = HGRN_WIDTH // HGRN_HEAD_DIM
CHUNK = 64
D_FF = 4 * D_MODEL
RMS_EPS = 1e-5
IN_WIDTH = POOL_WIDTH + 4 * HGRN_WIDTH


def rms_norm(x, g, eps=RMS_EPS):
    xf = x.astype(jnp.float32)
    y = xf * lax.rsqrt(jnp.mean(xf * xf, axis=-1, keepdims=True) + eps)
    return (y * g.astype(jnp.float32)).astype(x.dtype)

def pool_mixer(u, w, scale):
    B, S, _ = u.shape
    uf = u.astype(jnp.float32)
    c = jnp.cumsum(uf, axis=1)
    cp = jnp.pad(c, ((0, 0), (MAX_WIN, 0), (0, 0)))
    t = jnp.arange(S)
    groups = []
    for gi, win in enumerate(POOL_WINDOWS):
        lo, hi = gi * POOL_CH, (gi + 1) * POOL_CH
        win_sum = c[:, :, lo:hi] - cp[:, MAX_WIN - win:MAX_WIN - win + S, lo:hi]
        cnt = jnp.minimum(t + 1, win).astype(jnp.float32)[None, :, None]
        groups.append(win_sum / cnt - uf[:, :, lo:hi])
    p = jnp.stack(groups, axis=2)
    y = jnp.einsum('bsgc,gcd->bsgd', p, w.astype(jnp.float32)).reshape(B, S, POOL_WIDTH)
    return (y * scale.astype(jnp.float32)).astype(u.dtype)

def _to_chunks(t, B, S):
    return t.reshape(B, S // CHUNK, CHUNK, HGRN_HEADS, HGRN_HEAD_DIM).transpose(1, 0, 3, 2, 4)

def hgrn2_mixer(q_raw, f_raw, i_raw, g_raw, lb, norm_g):
    B, S, _ = q_raw.shape
    z = f_raw.astype(jnp.float32)
    lbf = lb.astype(jnp.float32)
    log_f = jnp.logaddexp(jnp.log(lbf), jnp.log1p(-lbf) + jax.nn.log_sigmoid(z))
    k = (1.0 - lbf) * jax.nn.sigmoid(-z)
    q = jax.nn.silu(q_raw.astype(jnp.float32))
    v = i_raw.astype(jnp.float32)
    qc, kc, vc, fc = (_to_chunks(a, B, S) for a in (q, k, v, log_f))
    causal = jnp.tril(jnp.ones((CHUNK, CHUNK), dtype=bool))[None, None, :, :, None]

    def chunk_step(state, inp):
        qb, kb, vb, lfb = inp
        b = jnp.cumsum(lfb, axis=2)
        diff = jnp.where(causal, b[:, :, :, None, :] - b[:, :, None, :, :], -jnp.inf)
        scores = jnp.einsum('bhtk,bhsk,bhtsk->bhts', qb, kb, jnp.exp(diff))
        o = (jnp.einsum('bhts,bhsv->bhtv', scores, vb)
             + jnp.einsum('bhtk,bhkv->bhtv', qb * jnp.exp(b), state))
        b_last = b[:, :, -1:, :]
        new_state = (jnp.exp(b_last[:, :, 0, :])[..., None] * state
                     + jnp.einsum('bhsk,bhsv->bhkv', kb * jnp.exp(b_last - b), vb))
        return new_state, o

    s0 = jnp.zeros((B, HGRN_HEADS, HGRN_HEAD_DIM, HGRN_HEAD_DIM), jnp.float32)
    _, o = lax.scan(chunk_step, s0, (qc, kc, vc, fc))
    o = o.transpose(1, 0, 3, 2, 4).reshape(B, S, HGRN_HEADS, HGRN_HEAD_DIM)
    o = o * lax.rsqrt(jnp.mean(o * o, axis=-1, keepdims=True) + RMS_EPS)
    o = o.reshape(B, S, HGRN_WIDTH) * norm_g.astype(jnp.float32)
    o = o * jax.nn.silu(g_raw.astype(jnp.float32))
    return o.astype(q_raw.dtype)

def first_inputs(seed: int = 0) -> dict:
    key = jax.random.key(seed)
    ks = jax.random.split(key, 12)
    f32 = jnp.float32
    x = jax.random.normal(ks[0], (BATCH, SEQ, D_MODEL), f32)
    norm_mix_g = 1.0 + 0.05 * jax.random.normal(ks[1], (DEPTH, D_MODEL), f32)
    w_in = jax.random.normal(ks[2], (DEPTH, D_MODEL, IN_WIDTH), f32) * D_MODEL ** -0.5
    pool_w = jax.random.normal(ks[3], (DEPTH, POOL_GROUPS, POOL_CH, POOL_CH), f32) * POOL_CH ** -0.5
    pool_scale = 1.0 + 0.1 * jax.random.normal(ks[4], (DEPTH, POOL_WIDTH), f32)
    hgrn_lb_logits = 0.5 * jax.random.normal(ks[5], (DEPTH, HGRN_WIDTH), f32)
    hgrn_norm_g = 1.0 + 0.05 * jax.random.normal(ks[6], (DEPTH, HGRN_WIDTH), f32)
    w_out = jax.random.normal(ks[7], (DEPTH, D_MIX, D_MODEL), f32) * D_MIX ** -0.5
    norm_mlp_g = 1.0 + 0.05 * jax.random.normal(ks[8], (DEPTH, D_MODEL), f32)
    w_up = jax.random.normal(ks[9], (DEPTH, D_MODEL, D_FF), f32) * D_MODEL ** -0.5
    w_down = jax.random.normal(ks[10], (DEPTH, D_FF, D_MODEL), f32) * D_FF ** -0.5
    final_norm_g = 1.0 + 0.05 * jax.random.normal(ks[11], (D_MODEL,), f32)
    return {"x": x, "norm_mix_g": norm_mix_g, "w_in": w_in, "pool_w": pool_w,
            "pool_scale": pool_scale, "hgrn_lb_logits": hgrn_lb_logits,
            "hgrn_norm_g": hgrn_norm_g, "w_out": w_out, "norm_mlp_g": norm_mlp_g,
            "w_up": w_up, "w_down": w_down, "final_norm_g": final_norm_g}

def first_block(x, norm_mix_g, w_in, pool_w, pool_scale, hgrn_lb_logits, hgrn_norm_g,
              w_out, norm_mlp_g, w_up, w_down, final_norm_g):
    lb_cum = jnp.cumsum(jax.nn.softmax(hgrn_lb_logits.astype(jnp.float32), axis=0), axis=0)
    lower_bounds = lb_cum - lb_cum[0:1]
    splits = [POOL_WIDTH + j * HGRN_WIDTH for j in range(4)]
    for l in range(DEPTH):
        h = rms_norm(x, norm_mix_g[l])
        u = h @ w_in[l]
        u_pool, q_raw, f_raw, i_raw, g_raw = jnp.split(u, splits, axis=-1)
        y_pool = pool_mixer(u_pool, pool_w[l], pool_scale[l])
        y_hgrn = hgrn2_mixer(q_raw, f_raw, i_raw, g_raw, lower_bounds[l], hgrn_norm_g[l])
        x = x + jnp.concatenate([y_pool, y_hgrn], axis=-1) @ w_out[l]
        h2 = rms_norm(x, norm_mlp_g[l])
        x = x + jnp.square(jax.nn.relu(h2 @ w_up[l])) @ w_down[l]
    return rms_norm(x, final_norm_g)


GRID_W = 64
NA_HEADS = 8
NA_HEAD_DIM = 64
D_ATTN = NA_HEADS * NA_HEAD_DIM
NA_KH = 8
NA_KW = 16
Q_BLOCK_W = 16
K_BLOCK_W = 2 * NA_KW
N_COL_BLOCKS = GRID_W // Q_BLOCK_W
CONV_CH = 512
CONV_K = 31
D_FF_2 = 2816
FFN_CONV_K = 3
D_IN = 3 * D_ATTN + 2 * CONV_CH + 2 * D_MODEL
EPS = 1e-6
NEG = -1e30


def _rmsnorm(x, g):
    xf = x.astype(jnp.float32)
    y = xf * lax.rsqrt(jnp.mean(xf * xf, axis=-1, keepdims=True) + EPS)
    return (y * g.astype(jnp.float32)).astype(x.dtype)

def _layernorm(x, g, b):
    xf = x.astype(jnp.float32)
    mu = jnp.mean(xf, axis=-1, keepdims=True)
    var = jnp.mean(jnp.square(xf - mu), axis=-1, keepdims=True)
    y = (xf - mu) * lax.rsqrt(var + EPS)
    return (y * g.astype(jnp.float32) + b.astype(jnp.float32)).astype(x.dtype)

def _dwconv_centred(x, w, b):
    k = w.shape[0]
    pad = k // 2
    y = lax.conv_general_dilated(
        x, w[:, None, :].astype(x.dtype), window_strides=(1,), padding=[(pad, pad)],
        dimension_numbers=("NWC", "WIO", "NWC"), feature_group_count=x.shape[-1])
    return y + b.astype(x.dtype)

def _neighbourhood_attention(q, k, v, rpb):
    bsz, s, h, dh = q.shape
    rows = s // GRID_W
    kh = min(NA_KH, rows)
    scale = NA_HEAD_DIM ** -0.5
    qg = q.reshape(bsz, rows, GRID_W, h, dh)
    kg = k.reshape(bsz, rows, GRID_W, h, dh)
    vg = v.reshape(bsz, rows, GRID_W, h, dh)

    col = jnp.arange(GRID_W)
    col_start = jnp.clip(col - NA_KW // 2, 0, GRID_W - NA_KW)
    blk_start = jnp.minimum(col_start[jnp.arange(N_COL_BLOCKS) * Q_BLOCK_W],
                            GRID_W - K_BLOCK_W)
    key_col = blk_start[:, None] + jnp.arange(K_BLOCK_W)
    q_col = col.reshape(N_COL_BLOCKS, Q_BLOCK_W)
    cs = col_start.reshape(N_COL_BLOCKS, Q_BLOCK_W)
    kc = key_col[:, None, :]
    in_win = (kc >= cs[..., None]) & (kc < cs[..., None] + NA_KW)
    col_off = jnp.clip(kc - q_col[..., None] + NA_KW - 1, 0, 2 * NA_KW - 2)
    rpb_col = rpb.astype(jnp.float32)[:, :, col_off]
    mask = in_win[None, None, :, :, None, :]

    def one_row(r):
        rs = jnp.clip(r - kh // 2, 0, rows - kh)
        q_r = lax.dynamic_index_in_dim(qg, r, axis=1, keepdims=False)
        q_r = q_r.reshape(bsz, N_COL_BLOCKS, Q_BLOCK_W, h, dh)
        k_r = lax.dynamic_slice_in_dim(kg, rs, kh, axis=1)[:, :, key_col]
        v_r = lax.dynamic_slice_in_dim(vg, rs, kh, axis=1)[:, :, key_col]
        row_off = rs + jnp.arange(kh) - r + NA_KH - 1
        bias = jnp.take(rpb_col, row_off, axis=1).transpose(0, 2, 3, 1, 4)
        sc = jnp.einsum("bnqhd,bknjhd->bhnqkj", q_r, k_r).astype(jnp.float32) * scale
        sc = jnp.where(mask, sc + bias[None], NEG)
        p = jax.nn.softmax(sc.reshape(bsz, h, N_COL_BLOCKS, Q_BLOCK_W, kh * K_BLOCK_W), axis=-1)
        p = p.reshape(sc.shape).astype(v.dtype)
        o = jnp.einsum("bhnqkj,bknjhd->bnqhd", p, v_r)
        return o.reshape(bsz, GRID_W, h * dh)

    out = lax.map(one_row, jnp.arange(rows))
    return out.transpose(1, 0, 2, 3).reshape(bsz, s, h * dh)

def second_inputs(seed: int = 0) -> dict:
    key = jax.random.key(seed)
    ks = jax.random.split(key, 20)
    n = jax.random.normal
    f32 = jnp.float32
    L = DEPTH
    return {
        "x": n(ks[0], (BATCH, SEQ, D_MODEL), f32),
        "norm1_g": 1.0 + 0.05 * n(ks[1], (L, D_MODEL), f32),
        "w_in": n(ks[2], (L, D_MODEL, D_IN), f32) * D_MODEL ** -0.5,
        "b_in": 0.01 * n(ks[3], (L, D_IN), f32),
        "rpb": 0.1 * n(ks[4], (L, NA_HEADS, 2 * NA_KH - 1, 2 * NA_KW - 1), f32),
        "w_na_out": n(ks[5], (L, D_ATTN, D_MODEL), f32) * D_ATTN ** -0.5,
        "conv_dw_w": n(ks[6], (L, CONV_K, CONV_CH), f32) * CONV_K ** -0.5,
        "conv_dw_b": 0.01 * n(ks[7], (L, CONV_CH), f32),
        "conv_ln_g": 1.0 + 0.05 * n(ks[8], (L, CONV_CH), f32),
        "conv_ln_b": 0.01 * n(ks[9], (L, CONV_CH), f32),
        "w_conv_out": n(ks[10], (L, CONV_CH, D_MODEL), f32) * CONV_CH ** -0.5,
        "w_out": n(ks[11], (L, D_MODEL, D_MODEL), f32) * D_MODEL ** -0.5,
        "norm2_g": 1.0 + 0.05 * n(ks[12], (L, D_MODEL), f32),
        "w_up": n(ks[13], (L, D_MODEL, 2 * D_FF_2), f32) * D_MODEL ** -0.5,
        "ffn_dw_w": n(ks[14], (L, FFN_CONV_K, 2 * D_FF_2), f32) * FFN_CONV_K ** -0.5,
        "ffn_dw_b": 0.01 * n(ks[15], (L, 2 * D_FF_2), f32),
        "w_down": n(ks[16], (L, D_FF_2, D_MODEL), f32) * D_FF_2 ** -0.5,
        "norm_f_g": 1.0 + 0.05 * n(ks[17], (D_MODEL,), f32),
    }

def second_block(x, norm1_g, w_in, b_in, rpb, w_na_out, conv_dw_w, conv_dw_b, conv_ln_g,
              conv_ln_b, w_conv_out, w_out, norm2_g, w_up, ffn_dw_w, ffn_dw_b, w_down,
              norm_f_g):
    bsz, s, _ = x.shape
    splits = np.cumsum([D_ATTN, D_ATTN, D_ATTN, CONV_CH, CONV_CH, D_MODEL]).tolist()
    for l in range(DEPTH):
        h = _rmsnorm(x, norm1_g[l])
        z = h @ w_in[l] + b_in[l]
        q, k, v, c_a, c_b, g_a, g_b = jnp.split(z, splits, axis=-1)
        qh = q.reshape(bsz, s, NA_HEADS, NA_HEAD_DIM)
        kh = k.reshape(bsz, s, NA_HEADS, NA_HEAD_DIM)
        vh = v.reshape(bsz, s, NA_HEADS, NA_HEAD_DIM)
        br_a = _neighbourhood_attention(qh, kh, vh, rpb[l]) @ w_na_out[l]
        u = c_a * jax.nn.sigmoid(c_b)
        u = _dwconv_centred(u, conv_dw_w[l], conv_dw_b[l])
        u = jax.nn.silu(_layernorm(u, conv_ln_g[l], conv_ln_b[l]))
        br_b = u @ w_conv_out[l]
        merged = jax.nn.sigmoid(g_a) * br_a + jax.nn.sigmoid(g_b) * br_b
        x = x + merged @ w_out[l]
        h2 = _rmsnorm(x, norm2_g[l])
        up = _dwconv_centred(h2 @ w_up[l], ffn_dw_w[l], ffn_dw_b[l])
        gate, val = jnp.split(up, 2, axis=-1)
        x = x + (jax.nn.gelu(gate, approximate=False) * val) @ w_down[l]
    return _rmsnorm(x, norm_f_g)


def setup_inputs(seed=0):
    out = dict(first_inputs(seed))
    for name, value in second_inputs(seed + 1).items():
        if name != "x":
            out[name + "_2"] = value
    return out


def reference(
    x, norm_mix_g, w_in, pool_w, pool_scale, hgrn_lb_logits, hgrn_norm_g, w_out, norm_mlp_g,
    w_up, w_down, final_norm_g, norm1_g_2, w_in_2, b_in_2, rpb_2, w_na_out_2, conv_dw_w_2,
    conv_dw_b_2, conv_ln_g_2, conv_ln_b_2, w_conv_out_2, w_out_2, norm2_g_2, w_up_2, ffn_dw_w_2,
    ffn_dw_b_2, w_down_2, norm_f_g_2,
):
    x = first_block(
        x, norm_mix_g, w_in, pool_w, pool_scale, hgrn_lb_logits, hgrn_norm_g, w_out, norm_mlp_g,
        w_up, w_down, final_norm_g,
    )
    return second_block(
        x, norm1_g_2, w_in_2, b_in_2, rpb_2, w_na_out_2, conv_dw_w_2, conv_dw_b_2, conv_ln_g_2,
        conv_ln_b_2, w_conv_out_2, w_out_2, norm2_g_2, w_up_2, ffn_dw_w_2, ffn_dw_b_2, w_down_2,
        norm_f_g_2,
    )


_drawn_inputs = setup_inputs


def setup_inputs(seed=0):
    import zlib

    import numpy as np

    out = dict(_drawn_inputs(seed))
    spreads = {}
    factors = {'b_in_2': 7.935,
     'rpb_2': 7.892,
     'conv_dw_b_2': 8.0,
     'conv_ln_b_2': 21.567,
     'ffn_dw_b_2': 7.827,
     'conv_ln_g_2': 2.672}
    for name, (base, spread) in spreads.items():
        noise = np.random.default_rng([zlib.crc32(name.encode()), seed]).standard_normal(out[name].shape)
        drawn = base * np.exp(spread * noise) if base else spread * noise
        out[name] = __import__('jax').numpy.asarray(drawn.astype(out[name].dtype))
    for name, factor in factors.items():
        out[name] = (out[name] * factor).astype(out[name].dtype)
    return out
```

```python
import concourse.bass as bass
from concourse import mybir
from contextlib import ExitStack

F32 = mybir.dt.float32
F32R = mybir.dt.float32r
U32 = mybir.dt.uint32
ACT = mybir.ActivationFunctionType
ALU = mybir.AluOpType
AX = mybir.AxisListType

P = 128
SEQ = 1024
D = 1024
KT = D // P
HALF = 512
BANKS = 8
POOL_W = 256
POOL_WINDOWS = (2, 4, 8, 16)
POOL_PAD = 16
HEADS = 6
HG_W = HEADS * P
CHUNK = 128
NC = SEQ // CHUNK
LEVELS = 7
D_FF = 4096
GRID_W = 64
ROWS = SEQ // GRID_W
NA_HEADS = 8
DH = 64
D_ATTN = NA_HEADS * DH
KH, KW = 8, 16
WIN = KH * GRID_W
PAIRS = NA_HEADS // 2
RPB_H, RPB_W = 2 * KH - 1, 2 * KW - 1
RPB_PAD = 128
NEG = -1e30
CONV_CH = 512
CT = CONV_CH // P
CONV_K = 31
CONV_PAD = CONV_K // 2
D_FF2 = 2816
FT2 = D_FF2 // P
FFN_K = 3
MLP_CHUNKS = D_FF // (2 * P)
FFN_CHUNKS = FT2 // 2
EPS1, EPS2 = 1e-5, 1e-6

Q1, F1, I1, G1 = POOL_W, POOL_W + HG_W, POOL_W + 2 * HG_W, POOL_W + 3 * HG_W
Q2, K2, V2 = 0, D_ATTN, 2 * D_ATTN
CA2, CB2 = 3 * D_ATTN, 3 * D_ATTN + CONV_CH
GA2, GB2 = 3 * D_ATTN + 2 * CONV_CH, 3 * D_ATTN + 2 * CONV_CH + D
D_IN2 = GB2 + D

VECTORS = [
    [("norm_mix_g", 8), ("pool_scale", 2), ("hgrn_norm_g", 6), ("norm_mlp_g", 8), ("final_norm_g", 8),
     ("norm1_g_2", 8), ("b_in_2", D_IN2 // P), ("norm2_g_2", 8), ("norm_f_g_2", 8), ("conv_dw_b_2", CT),
     ("conv_ln_g_2", CT), ("conv_ln_b_2", CT)],
    [("ffn_dw_b_2", 2 * FT2), ("ffn_dw_w_2/0", 2 * FT2)],
    [("ffn_dw_w_2/1", 2 * FT2), ("ffn_dw_w_2/2", 2 * FT2)],
    [("conv_dw_w_2", CONV_K * CT)],
]
STACK_ROWS = [sum(n for _, n in stack) for stack in VECTORS]
COL = {}
for _s, _stack in enumerate(VECTORS):
    _at = _s * P
    for _name, _n in _stack:
        COL[_name] = _at
        _at += _n

T_POOL = 0
T_HEADS = T_POOL + POOL_W // P
T_OUT1 = T_HEADS + 4 * HEADS
T_MLP = T_OUT1 + KT
T_CB = T_MLP + 4 * MLP_CHUNKS
T_PAIRS = T_CB + CT
T_MERGE = T_PAIRS + 4 * PAIRS
T_OUT2 = T_MERGE + 3 * KT
T_FFN = T_OUT2 + KT
T_END = T_FFN + 6 * FFN_CHUNKS

BASE = 16512
KB = 1024
A_X = BASE
A_HI = A_X + 32 * KB
A_LO = A_HI + 32 * KB
A_RAW = A_LO + 32 * KB
A_WHI = A_RAW + 8 * KB
A_WLO = A_WHI + 8 * KB
A_CONST = A_WLO + 8 * KB
A_ARENA = A_CONST + 5 * KB


def two_blocks(nc, dram, out):
    ctx = ExitStack()
    with ctx:
        def sem(name):
            return ctx.enter_context(nc.semaphore(name))

        def at(name, shape, address, dtype=F32):
            return nc.alloc_sbuf_tensor_at(name, shape, dtype, offset=address)

        x_t = at("x_t", [P, KT, SEQ], A_X)
        mix1 = at("mix1", [P, KT, SEQ], A_X)
        h_hi = at("h_hi", [P, KT, SEQ], A_HI, F32R)
        h_lo = at("h_lo", [P, KT, SEQ], A_LO, F32R)
        w_raw = at("w_raw", [P, 2, 1024], A_RAW)
        w_hi = at("w_hi", [P, 2, 1024], A_WHI, F32R)
        w_lo = at("w_lo", [P, 2, 1024], A_WLO, F32R)

        ident = at("ident", [P, P], A_CONST)
        ones = at("ones", [P, P], A_CONST + 512)
        cols = at("cols", [P, 4 * P], A_CONST + 1024)
        eps1, eps2, one, decay, row_max, neg_max, row_sum, row_inv = (
            at(name, [P, n], A_CONST + 4096 + 32 * j) for j, (name, n) in enumerate(
                (("eps1", 1), ("eps2", 1), ("one", 1), ("decay", NC), ("row_max", 2), ("neg_max", 2),
                 ("row_sum", 2), ("row_inv", 2))))
        col_mask = at("col_mask", [P, GRID_W], A_CONST + 4352)

        def arena(*shapes):
            got, a = [], A_ARENA
            for name, shape, dtype in shapes:
                size = 4
                for n in shape[1:]:
                    size *= n
                got.append(at(name, shape, a, dtype))
                a += -(-size // 32) * 32
            assert a <= 229344, a
            return got

        x_in, stack_rows, rpb_pad = arena(
            ("x_in", [P, KT, D], F32), ("stack_rows", [P, 4, P], F32), ("rpb_pad", [P, RPB_PAD], F32))
        _, sq, h32, rinv = arena(
            ("norm_hole", [P, 62 * 256], F32), ("sq", [P, 2, SEQ], F32), ("h32", [P, 2, SEQ], F32),
            ("rinv", [P, SEQ], F32))
        (zf, zq, zv, zg, b_t, k_t, q_t, v_tok, sg_t, e_t, s_t, kd_tok, qe_t, states, t1, t2, resets,
         pool_w, pair_mask) = arena(
            ("zf", [P, SEQ], F32), ("zq", [P, SEQ], F32), ("zv", [P, SEQ], F32), ("zg", [P, SEQ], F32),
            ("b_t", [P, SEQ], F32), ("k_t", [P, SEQ], F32), ("q_t", [P, SEQ], F32),
            ("v_tok", [P, NC, P], F32), ("sg_t", [P, SEQ], F32), ("e_t", [P, 2, SEQ], F32),
            ("s_t", [P, NC, CHUNK], F32), ("kd_tok", [P, NC, P], F32), ("qe_t", [P, SEQ], F32),
            ("states", [P, NC, P], F32), ("t1", [P, SEQ], F32), ("t2", [P, SEQ], F32),
            ("resets", [P, SEQ], F32), ("pool_w", [P, 2, P], F32),
            ("pair_mask", [P, LEVELS + 1, P], F32))
        PADDED = POOL_PAD + SEQ
        A_POOL = A_ARENA + 16 * KB
        pool_u = at("pool_u", [P, 2, PADDED], A_POOL)
        pool_a = at("pool_a", [P, PADDED], A_POOL + 2 * 4 * PADDED)
        pool_b = at("pool_b", [P, PADDED], A_POOL + 3 * 4 * PADDED)
        pool_inv = at("pool_inv", [P, 2, SEQ], A_POOL + 4 * 4 * PADDED)
        pool_p = at("pool_p", [P, 2, SEQ], A_POOL + 4 * 4 * PADDED + 8 * KB)
        assert A_POOL + 4 * 4 * PADDED + 16 * KB <= A_ARENA + 64 * KB
        mlp_a, mlp_hi, mlp_lo = arena(
            ("mlp_a", [P, 2, SEQ], F32), ("mlp_hi", [P, 2, SEQ], F32R), ("mlp_lo", [P, 2, SEQ], F32R))
        ffn_gate, ffn_val, ffn_a, ffn_hi, ffn_lo = arena(
            ("ffn_gate", [P, SEQ], F32), ("ffn_val", [P, SEQ], F32), ("ffn_a", [P, 2, SEQ], F32),
            ("ffn_hi", [P, 2, SEQ], F32R), ("ffn_lo", [P, 2, SEQ], F32R))
        conv_t = at("conv_t", [P, CT, SEQ], A_X)
        att_t = at("att_t", [P, PAIRS, SEQ], A_X + 16 * KB)
        conv_lo = at("conv_lo", [P, CT, SEQ], A_X, F32R)
        att_lo = at("att_lo", [P, PAIRS, SEQ], A_X + 16 * KB, F32R)
        U_PAD = CONV_PAD + SEQ + CONV_PAD
        (sig_cb, q_hi, q_lo, k_hi, k_lo, v_t, v_even, v_odd, bias, prob, prob_t, u_t, q32, k32) = arena(
            ("sig_cb", [P, CT, SEQ], F32), ("q_hi", [P, ROWS, P], F32R), ("q_lo", [P, ROWS, P], F32R),
            ("k_hi", [P, SEQ], F32R), ("k_lo", [P, SEQ], F32R), ("v_t", [P, SEQ], F32),
            ("v_even", [P, SEQ // P, P], F32), ("v_odd", [P, SEQ // P, P], F32),
            ("bias", [P, RPB_H, GRID_W], F32), ("prob", [P, 3, WIN], F32), ("prob_t", [P, 2, WIN], F32),
            ("u_t", [P, U_PAD], F32), ("q32", [P, SEQ], F32), ("k32", [P, SEQ], F32))
        conv_hi, att_hi, mix2, sig_a, sig_b, br_a = arena(
            ("conv_hi", [P, CT, SEQ], F32R), ("att_hi", [P, PAIRS, SEQ], F32R), ("mix2", [P, KT, SEQ], F32),
            ("sig_a", [P, SEQ], F32), ("sig_b", [P, SEQ], F32), ("br_a", [P, SEQ], F32))
        A_LN = A_ARENA + 32 * KB
        ln_mean = at("ln_mean", [P, SEQ], A_LN)
        ln_sq = at("ln_sq", [P, CT, SEQ], A_LN + 4 * KB)
        ln_inv = at("ln_inv", [P, SEQ], A_LN + 20 * KB)
        (y_tok,) = arena(("y_tok", [P, KT, D], F32))

        psum = ctx.enter_context(nc.psum_tensor("psum", [P, BANKS, HALF], F32))

        def banks(b, n=2):
            return psum[:, b:b + n, :].rearrange("p b t -> p (b t)")

        def col(name, k=0):
            c = COL[name] + k
            return cols[:, bass.ds(c, 1)] if not isinstance(c, int) else cols[:, c:c + 1]

        x_spill = nc.dram_tensor("x_spill", (P, KT * SEQ), F32, kind="Internal").ap()
        rpb_spill = nc.dram_tensor("rpb_spill", (NA_HEADS * RPB_H, RPB_PAD), F32, kind="Internal").ap()
        bias_rows = nc.dram_tensor("bias_rows", (PAIRS, P, RPB_H, GRID_W), F32, kind="Internal").ap()

        weight_loaded = [sem("weight_loaded_0"), sem("weight_loaded_1")]
        weight_split = sem("weight_split")
        weight_hi = sem("weight_hi")
        tile_done = sem("tile_done")
        sp_passed, pool_passed, dve_passed = (sem(f"{e}_passed") for e in ("sp", "pool", "dve"))
        consts_loaded = sem("consts_loaded")
        x_loaded = [sem(f"x_loaded_{t}") for t in range(KT)]
        rows_loaded = sem("rows_loaded")
        rows_zeroed = sem("rows_zeroed")
        rpb_zeroed = sem("rpb_zeroed")
        rpb_loaded = sem("rpb_loaded")
        rpb_stored = sem("rpb_stored")
        bias_stored = sem("bias_stored")
        memsets = sem("memsets")
        cols_turned = sem("cols_turned")
        cols_ready = sem("cols_ready")
        x_turned = sem("x_turned")
        x_copied = sem("x_copied")
        x_spilled = sem("x_spilled")
        x_back = sem("x_back")
        x_ready = sem("x_ready")
        sq_ready = sem("sq_ready")
        sq_used = sem("sq_used")
        mean_log = sem("mean_log")
        rinv_ready = sem("rinv_ready")
        h32_ready = sem("h32_ready")
        h_hi_ready = sem("h_hi_ready")
        h_ready = sem("h_ready")
        mix_hi_ready = sem("mix_hi_ready")
        mix_split = sem("mix_split")
        x_added = sem("x_added")
        pool_w_zeroed = sem("pool_w_zeroed")
        pool_loaded = sem("pool_loaded")
        pool_u_ready = sem("pool_u_ready")
        pool_step = sem("pool_step")
        pool_p_ready = sem("pool_p_ready")
        pool_mixed = sem("pool_mixed")
        pool_ready = sem("pool_ready")
        zf_ready, zq_ready, zv_ready, zg_ready = (sem(f"z{n}_ready") for n in "fqvg")
        abs_ready = sem("abs_ready")
        exp_ready = sem("exp_ready")
        log1p_ready = sem("log1p_ready")
        logf_ready = sem("logf_ready")
        b_ready = sem("b_ready")
        lk_ready = sem("lk_ready")
        k_ready = sem("k_ready")
        q_ready = sem("q_ready")
        sg_ready = sem("sg_ready")
        v_turned = sem("v_turned")
        v_ready = sem("v_ready")
        kd_arg = sem("kd_arg")
        kd_exp = sem("kd_exp")
        kd_ready = sem("kd_ready")
        kd_turned = sem("kd_turned")
        kd_tok_ready = sem("kd_tok_ready")
        b_exp = sem("b_exp")
        qe_ready = sem("qe_ready")
        decay_ready = sem("decay_ready")
        update_done = sem("update_done")
        state_ready = sem("state_ready")
        level_arg = sem("level_arg")
        level_exp = sem("level_exp")
        level_ready = sem("level_ready")
        level_done = sem("level_done")
        level_merged = sem("level_merged")
        o_done = sem("o_done")
        o_sq = sem("o_sq")
        o_mean = sem("o_mean")
        o_log = sem("o_log")
        o_inv = sem("o_inv")
        o_scaled = sem("o_scaled")
        y_ready = sem("y_ready")
        up_read = sem("up_read")
        act_ready = sem("act_ready")
        act_hi_ready = sem("act_hi_ready")
        act_split = sem("act_split")
        down_done = sem("down_done")
        down_added = sem("down_added")
        ffn_mid = sem("ffn_mid")
        ffn_left = sem("ffn_left")
        ffn_right = sem("ffn_right")
        ffn_gelu = sem("ffn_gelu")
        cb_ready = sem("cb_ready")
        q_zeroed = sem("q_zeroed")
        u_zeroed = sem("u_zeroed")
        bias_loaded = sem("bias_loaded")
        bias_ready = sem("bias_ready")
        vt_ready = sem("vt_ready")
        v_tiles_turned = sem("v_tiles_turned")
        v_tiles_ready = sem("v_tiles_ready")
        q32_ready = sem("q32_ready")
        q_hi_ready = sem("q_hi_ready")
        q_split = sem("q_split")
        k32_ready = sem("k32_ready")
        k_hi_ready = sem("k_hi_ready")
        k_split = sem("k_split")
        u_ready = sem("u_ready")
        conv_step = sem("conv_step")
        scores_done = sem("scores_done")
        scores_max = sem("scores_max")
        neg_max_ready = sem("neg_max_ready")
        prob_exp = sem("prob_exp")
        inv_ready = sem("inv_ready")
        prob_ready = sem("prob_ready")
        prob_turned = sem("prob_turned")
        prob_t_ready = sem("prob_t_ready")
        pv_done = sem("pv_done")
        att_ready = sem("att_ready")
        ln_summed = sem("ln_summed")
        ln_mean_ready = sem("ln_mean_ready")
        ln_centred = sem("ln_centred")
        ln_sq_ready = sem("ln_sq_ready")
        ln_var = sem("ln_var")
        ln_log = sem("ln_log")
        ln_inv_ready = sem("ln_inv_ready")
        ln_scaled = sem("ln_scaled")
        ln_silu = sem("ln_silu")
        branch_hi = sem("branch_hi")
        branch_split = sem("branch_split")
        gate_a_ready = sem("gate_a_ready")
        gate_b_ready = sem("gate_b_ready")
        branch_a = sem("branch_a")
        branch_b = sem("branch_b")
        merged = sem("merged")
        y_turned = sem("y_turned")
        y_copied = sem("y_copied")
        stored = sem("stored")

        block = ctx.enter_context(nc.Block())

        def columns(w, first):
            v = w.rearrange("(k p) n -> p k n", p=P)
            c = slice(first, first + P) if isinstance(first, int) else bass.ds(first, P)
            return [v[:, 0:4, c], v[:, 4:8, c]]

        def rows(w, first, left):
            r = [slice(first + P * k, first + P * k + P) if isinstance(first, int)
                 else bass.ds(first + P * k, P) for k in range(2)]
            return [w[r[k], left:left + HALF] for k in range(2)]

        def branches(first):
            c = slice(first, first + P) if isinstance(first, int) else bass.ds(first, P)
            return [dram[n].rearrange("(k p) n -> p k n", p=P)[:, :, c] for n in ("w_na_out_2", "w_conv_out_2")]

        w_in, w_in2 = dram["w_in"], dram["w_in_2"]

        def head_tiles(h):
            return [columns(w_in, c + h * P) for c in (F1, Q1, I1, G1)]

        def mlp_up(c):
            return [columns(dram["w_up"], c * 2 * P + j * P) for j in range(2)]

        def mlp_down(c):
            return [rows(dram["w_down"], c * 2 * P, j * HALF) for j in range(2)]

        def pair_tiles(p):
            return [columns(w_in2, c + p * P) for c in (CA2, V2, Q2, K2)]

        def merge_tiles(d):
            return [columns(w_in2, GA2 + d * P), columns(w_in2, GB2 + d * P), branches(d * P)]

        def ffn_up(c):
            return [columns(dram["w_up_2"], part + c * 2 * P + j * P) for j in range(2) for part in (0, D_FF2)]

        def ffn_down(c):
            return [rows(dram["w_down_2"], c * 2 * P, j * HALF) for j in range(2)]

        def weight_stream(eng, step):
            parts = [
                ([columns(w_in, j * P) for j in range(2)], 0, None, []),
                (head_tiles(0), HEADS - 1, lambda i: head_tiles(i + 1), []),
                ([], KT // 2, lambda i: [columns(dram["w_out"], i * 2 * P + j * P) for j in range(2)], []),
                (mlp_up(0), MLP_CHUNKS - 1, lambda i: mlp_up(i + 1) + mlp_down(i), mlp_down(MLP_CHUNKS - 1)),
                ([], CT // 2, lambda i: [columns(w_in2, CB2 + i * 2 * P + j * P) for j in range(2)], []),
                ([], PAIRS, pair_tiles, []),
                ([], KT // 2, lambda i: merge_tiles(i * 2) + merge_tiles(i * 2 + 1), []),
                ([], KT // 2, lambda i: [columns(dram["w_out_2"], i * 2 * P + j * P) for j in range(2)], []),
                (ffn_up(0), FFN_CHUNKS - 1, lambda i: ffn_up(i + 1) + ffn_down(i), ffn_down(FFN_CHUNKS - 1)),
            ]
            n = 0
            for ahead, count, body, behind in parts:
                for halves in ahead:
                    step(n, n % 2, halves)
                    n += 1
                if count:
                    size = len(body(0))
                    assert size % 2 == 0 and n % 2 == 0
                    with eng.Fori(0, count) as i:
                        for j, halves in enumerate(body(i)):
                            step(i * size + (n + j), j % 2, halves)
                    n += count * size
                for halves in behind:
                    step(n, n % 2, halves)
                    n += 1
            assert n == T_END

        @block.sync
        def _(sp):
            for t in range(KT):
                sp.dma_start(x_in[:, t, :], dram["x"][0, t * P:(t + 1) * P, :]).then_inc(x_loaded[t], 16)
                if t == 1:
                    sp.dma_start(ident[:, :], dram["c_ident"]).then_inc(consts_loaded, 16)
                    sp.dma_start(col_mask[:, :], dram["c_col_mask"]).then_inc(consts_loaded, 16)
            sp.wait_ge(rows_zeroed, 1)
            for s, stack in enumerate(VECTORS):
                r = 0
                for name, n in stack:
                    if "/" in name:
                        name, tap = name.split("/")
                        src = dram[name][int(tap), :].rearrange("(n c) -> n c", c=P)
                    elif name == "conv_dw_w_2":
                        src = dram[name].rearrange("k (n c) -> (k n) c", c=P)
                    else:
                        src = dram[name].rearrange("(n c) -> n c", c=P)
                    sp.dma_start(stack_rows[r:r + n, s, :], src).then_inc(rows_loaded, 16)
                    r += n
            sp.wait_ge(rpb_zeroed, 1)
            left = GRID_W - KW
            sp.dma_start(rpb_pad[0:NA_HEADS * RPB_H, left:left + RPB_W],
                         dram["rpb_2"].rearrange("h r c -> (h r) c")).then_inc(rpb_loaded, 16)

            def load(n, slot, halves):
                if not isinstance(n, int) or n >= 2:
                    sp.wait_ge(weight_split, n - 1)
                    sp.sem_inc(sp_passed, 1)
                for j, half in enumerate(halves):
                    dst = w_raw[:, slot, j * HALF:(j + 1) * HALF]
                    if len(half.shape) == 3:
                        dst = dst.rearrange("p (k n) -> p k n", n=P)
                    sp.dma_start(dst, half).then_inc(weight_loaded[slot], 16)

            weight_stream(sp, load)

            for t in range(KT):
                sp.wait_ge(y_copied, 2 * t + 2)
                sp.dma_start(out[0, t * P:(t + 1) * P, :], y_tok[:, t, :]).then_inc(stored, 16)
            sp.wait_ge(stored, 16 * KT)

        @block.gpsimd
        def _(pool):
            pool.memset(stack_rows[:, :, :], 0.0).then_inc(rows_zeroed, 1)
            pool.memset(rpb_pad[:, :], 0.0).then_inc(rpb_zeroed, 1)
            pool.memset(ones[:, :], 1.0).then_inc(memsets, 1)
            pool.memset(eps1[:, :], EPS1).then_inc(memsets, 1)
            pool.memset(eps2[:, :], EPS2).then_inc(memsets, 1)
            pool.memset(one[:, :], 1.0).then_inc(memsets, 1)

            def split(n, slot, _):
                pool.wait_ge(weight_loaded[slot], arrived(n, slot))
                if not isinstance(n, int) or n >= 2:
                    pool.wait_ge(tile_done, n - 1)
                pool.sem_inc(pool_passed, 1)
                pool.tensor_copy(w_hi[:, slot, :], w_raw[:, slot, :]).then_inc(weight_hi, 1)
                pool.wait_ge(weight_hi, n + 1)
                pool.tensor_tensor(w_lo[:, slot, :], w_raw[:, slot, :], w_hi[:, slot, :].bitcast(F32),
                                   ALU.subtract).then_inc(weight_split, 1)

            def arrived(n, slot):
                return (n - slot) * 16 + 32

            weight_stream(pool, split)

        def row_window(r):
            first = min(max(r - KH // 2, 0), ROWS - KH)
            return first, first - r + KH - 1

        def level_parts(tile, level):
            return tile.rearrange("p (n two s) -> p n two s", two=2, s=1 << level)

        @block.tensor
        def _(pe):
            def product(n, slot, first_bank, hi, lo):
                pe.wait_ge(weight_split, n + 1)
                for k in range(KT):
                    wh = w_hi[:, slot, k * P:(k + 1) * P]
                    wl = w_lo[:, slot, k * P:(k + 1) * P]
                    for j, (w, a) in enumerate(((wh, hi), (wh, lo), (wl, hi))):
                        for t in range(2):
                            last = pe.matmul(psum[:, first_bank + t, :], w, a[:, k, t * HALF:(t + 1) * HALF],
                                             start=(k == 0 and j == 0), stop=(k == KT - 1 and j == 2))
                last.then_inc(tile_done, 1)

            def down(n, slot, first_group, hi, lo):
                pe.wait_ge(weight_split, n + 1)
                for g in range(8):
                    pe.wait_ge(down_added, first_group + (g + 1))
                    d, t = g // 2, g % 2
                    for k in range(2):
                        at_d = slice(k * HALF + d * P, k * HALF + (d + 1) * P)
                        wh, wl = w_hi[:, slot, at_d], w_lo[:, slot, at_d]
                        for j, (w, a) in enumerate(((wh, hi), (wh, lo), (wl, hi))):
                            last = pe.matmul(psum[:, 4 + g % 4, :], w, a[:, k, t * HALF:(t + 1) * HALF],
                                             start=(k == 0 and j == 0), stop=(k == 1 and j == 2))
                    last.then_inc(down_done if g < 7 else tile_done, 1)

            def sum_squares(m):
                for d in range(KT):
                    pe.wait_ge(sq_ready, KT * m + d + 1)
                    for t in range(2):
                        last = pe.matmul(psum[:, 4 + t, :], ones[:, :], sq[:, d % 2, t * HALF:(t + 1) * HALF],
                                         start=(d == 0), stop=(d == KT - 1))
                    last.then_inc(sq_used, 1)

            def turn(src, dst_bank, tiles, done):
                for c, block_in in enumerate(tiles):
                    last = pe.transpose(psum[:, dst_bank + c // 4, (c % 4) * P:(c % 4 + 1) * P],
                                        block_in, ident[:, :])
                last.then_inc(done, 1)

            pe.wait_ge(consts_loaded, 32)
            for t in range(KT):
                pe.wait_ge(x_loaded[t], 16)
                if t >= 2:
                    pe.wait_ge(x_copied, 2 * (t - 1))
                for d in range(0, KT, 4):
                    turn(x_in, 4 * (t % 2) + d // 4,
                         [x_in[:, t, (d + c) * P:(d + c + 1) * P] for c in range(4)], x_turned)
            pe.wait_ge(rows_loaded, 16 * sum(len(stack) for stack in VECTORS))
            turn(stack_rows, 7, [stack_rows[:, s, :] for s in range(4)], cols_turned)

            pe.wait_ge(memsets, 4)
            sum_squares(0)
            pe.wait_ge(h_ready, KT)
            for j in range(2):
                product(T_POOL + j, j, 2 * j, h_hi, h_lo)

            def project_f(h):
                pe.wait_ge(*((pool_u_ready, 1) if isinstance(h, int) and h == 0 else (zv_ready, h)))
                product(h * 4 + T_HEADS, 0, 0, h_hi, h_lo)

            def project_q(h):
                pe.wait_ge(*((pool_u_ready, 2) if isinstance(h, int) and h == 0 else (zg_ready, h)))
                product(h * 4 + (T_HEADS + 1), 1, 2, h_hi, h_lo)

            def project_i(h):
                pe.wait_ge(zf_ready, h + 1)
                product(h * 4 + (T_HEADS + 2), 0, 0, h_hi, h_lo)

            def project_g(h):
                pe.wait_ge(zq_ready, h + 1)
                product(h * 4 + (T_HEADS + 3), 1, 2, h_hi, h_lo)

            def head(h, following):
                def level(l, first_bank):
                    pe.wait_ge(level_ready, h * LEVELS + (l + 1))
                    for c in range(NC):
                        e = e_t[:, l % 2, c * CHUNK:(c + 1) * CHUNK]
                        last = pe.matmul(psum[:, first_bank + c // 4, (c % 4) * P:(c % 4 + 1) * P], e, e,
                                         start=True, stop=True)
                    last.then_inc(level_done, 1)

                def merged_up_to(l):
                    pe.wait_ge(level_merged, h * (LEVELS + 1) + (l + 1))

                pe.wait_ge(zv_ready, h + 1)
                pe.wait_ge(o_log, h + 1)
                turn(zv, 4, [zv[:, c * P:(c + 1) * P] for c in range(NC)], v_turned)
                if following is not None:
                    project_f(following)
                    project_q(following)
                pe.wait_ge(o_scaled, h + 1)
                level(0, 6)
                pe.wait_ge(kd_ready, h + 1)
                pe.wait_ge(v_ready, h + 1)
                turn(t1, 4, [t1[:, c * P:(c + 1) * P] for c in range(NC)], kd_turned)
                pe.wait_ge(kd_tok_ready, h + 1)
                merged_up_to(0)
                for c in range(NC - 1):
                    last = pe.matmul(psum[:, 6 + c // 4, (c % 4) * P:(c % 4 + 1) * P], kd_tok[:, c, :],
                                     v_tok[:, c, :], start=True, stop=True)
                last.then_inc(update_done, 1)
                if following is not None:
                    project_i(following)
                level(1, 4)
                pe.wait_ge(state_ready, h * (NC - 1) + (NC - 1))
                level(2, 6)
                merged_up_to(1)
                level(3, 4)
                if following is not None:
                    project_g(following)
                merged_up_to(2)
                level(4, 6)
                merged_up_to(3)
                level(5, 4)
                merged_up_to(4)
                level(6, 6)
                merged_up_to(5)
                for c in range(NC):
                    last = pe.matmul(psum[:, 4 + c // 4, (c % 4) * P:(c % 4 + 1) * P],
                                     k_t[:, c * CHUNK:(c + 1) * CHUNK], q_t[:, c * CHUNK:(c + 1) * CHUNK],
                                     start=True, stop=True)
                last.then_inc(level_done, 1)
                merged_up_to(LEVELS)
                pe.wait_ge(qe_ready, h + 1)
                for c in range(NC):
                    o = psum[:, 6 + c // 4, (c % 4) * P:(c % 4 + 1) * P]
                    last = pe.matmul(o, v_tok[:, c, :], s_t[:, c, :], start=True, stop=(c == 0))
                    if c >= 1:
                        last = pe.matmul(o, states[:, c, :], qe_t[:, c * CHUNK:(c + 1) * CHUNK],
                                         start=False, stop=True)
                last.then_inc(o_done, 1)
                pe.wait_ge(o_sq, h + 1)
                for t in range(2):
                    last = pe.matmul(psum[:, 4 + t, :], ones[:, :], t1[:, t * HALF:(t + 1) * HALF],
                                     start=True, stop=True)
                last.then_inc(o_mean, 1)

            project_f(0)
            project_q(0)
            project_i(0)
            project_g(0)
            pe.wait_ge(pool_loaded, 16 * 6)
            for j in range(2):
                pe.wait_ge(pool_p_ready, j + 1)
                for t in range(2):
                    last = pe.matmul(psum[:, 4 + 2 * j + t, :], pool_w[:, j, :],
                                     pool_p[:, j, t * HALF:(t + 1) * HALF], start=True, stop=True)
                last.then_inc(pool_mixed, 1)
            pe.wait_ge(pool_ready, 2)
            with pe.Fori(0, HEADS - 1) as i:
                head(i, i + 1)
            head(HEADS - 1, None)

            def project_out(first_tile, first_split, first_added):
                pe.wait_ge(mix_split, first_split + KT)
                with pe.Fori(0, KT // 2) as i:
                    for s in range(2):
                        pe.wait_ge(x_added, i * 2 + (first_added + s + 1))
                        product(i * 2 + (first_tile + s), s, 2 * s, h_hi, h_lo)

            project_out(T_OUT1, 0, 0)

            def up_product(n, slot, tile, read, first_bank):
                pe.wait_ge(read, tile + 1)
                product(n, slot, first_bank, h_hi, h_lo)

            def mlp_up_part(c, n):
                for j in range(2):
                    up_product(n + j, j, c * 2 + j, up_read, 2 * j)

            def mlp_down_part(c, n):
                pe.wait_ge(act_split, c * 2 + 4)
                for j in range(2):
                    down(n + j, j, c * 16 + 8 * j, mlp_hi, mlp_lo)

            sum_squares(1)
            pe.wait_ge(h_ready, 2 * KT)
            mlp_up_part(0, T_MLP)
            with pe.Fori(0, MLP_CHUNKS - 1) as i:
                mlp_up_part(i + 1, i * 4 + (T_MLP + 2))
                mlp_down_part(i, i * 4 + (T_MLP + 4))
            mlp_down_part(MLP_CHUNKS - 1, T_CB - 2)

            sum_squares(2)
            sum_squares(3)
            pe.wait_ge(h_ready, 3 * KT)

            with pe.Fori(0, CT // 2) as i:
                for s in range(2):
                    pe.wait_ge(cb_ready, i * 2 + (s + 1))
                    product(i * 2 + (T_CB + s), s, 2 * s, h_hi, h_lo)

            def scores(p, s):
                first, _ = row_window(s)
                pe.wait_ge(scores_max, p * ROWS + (s + 1))
                k = slice(first * GRID_W, first * GRID_W + WIN)
                for j, (q, kk) in enumerate(((q_hi, k_hi), (q_hi, k_lo), (q_lo, k_hi))):
                    last = pe.matmul(psum[:, 4 + s % 2, :], q[:, s, :], kk[:, k], start=(j == 0), stop=(j == 2))
                last.then_inc(scores_done, 1)

            def turn_probabilities(p, s):
                pe.wait_ge(prob_ready, p * ROWS + (s + 1))
                pe.wait_ge(prob_t_ready, p * ROWS + (s + 1))
                turn(prob, 6 + s % 2, [prob[:, s % 3, c * P:(c + 1) * P] for c in range(4)], prob_turned)

            def weigh_values(p, s):
                first, _ = row_window(s)
                pe.wait_ge(prob_t_ready, p * ROWS + (s + 3))
                pe.wait_ge(att_ready, p * 4 + (s // 4 + 3))
                v = v_odd if first % 2 else v_even
                for c in range(4):
                    last = pe.matmul(psum[:, (s // 4) % 2, (s % 4) * P:(s % 4 + 1) * P], v[:, first // 2 + c, :],
                                     prob_t[:, s % 2, c * P:(c + 1) * P], start=(c == 0), stop=(c == 3))
                if s % 4 == 3:
                    last.then_inc(pv_done, 1)

            pe.wait_ge(cb_ready, 2 + CT)
            with pe.Fori(0, PAIRS) as p:
                pe.wait_ge(att_ready, p * 4 + 4)
                product(p * 4 + T_PAIRS, 0, 0, h_hi, h_lo)
                pe.wait_ge(k32_ready, p + 1)
                product(p * 4 + (T_PAIRS + 1), 1, 2, h_hi, h_lo)
                pe.wait_ge(u_ready, p + 1)
                product(p * 4 + (T_PAIRS + 2), 0, 0, h_hi, h_lo)
                pe.wait_ge(vt_ready, p + 1)
                pe.wait_ge(scores_max, p * ROWS + 2)
                turn(v_t, 4, [v_t[:, c * P:(c + 1) * P] for c in range(8)], v_tiles_turned)
                pe.wait_ge(prob_t_ready, p * ROWS + 2)
                turn(v_t, 6, [v_t[:, c * P + GRID_W:(c + 1) * P + GRID_W] for c in range(7)], v_tiles_turned)
                product(p * 4 + (T_PAIRS + 3), 1, 2, h_hi, h_lo)
                pe.wait_ge(q_split, p + 1)
                pe.wait_ge(k_split, p + 1)
                pe.wait_ge(v_tiles_ready, p * 2 + 2)
                for s in range(ROWS + 3):
                    if s < ROWS:
                        scores(p, s)
                    if 2 <= s < ROWS + 2:
                        turn_probabilities(p, s - 2)
                    if s >= 3:
                        weigh_values(p, s - 3)

            pe.wait_ge(conv_step, CONV_K * CT)
            for t in range(2):
                for c in range(CT):
                    last = pe.matmul(psum[:, 4 + t, :], ones[:, :], conv_t[:, c, t * HALF:(t + 1) * HALF],
                                     start=(c == 0), stop=(c == CT - 1))
            last.then_inc(ln_summed, 1)
            pe.wait_ge(ln_sq_ready, CT)
            for t in range(2):
                for c in range(CT):
                    last = pe.matmul(psum[:, 6 + t, :], ones[:, :], ln_sq[:, c, t * HALF:(t + 1) * HALF],
                                     start=(c == 0), stop=(c == CT - 1))
            last.then_inc(ln_var, 1)

            pe.wait_ge(att_ready, 4 + 4 * PAIRS)
            with pe.Fori(0, KT // 2) as i:
                for s in range(2):
                    n = i * 6 + (T_MERGE + 3 * s)
                    d1 = i * 2 + (s + 1)
                    pe.wait_ge(gate_a_ready, d1)
                    product(n, s % 2, 0, h_hi, h_lo)
                    pe.wait_ge(gate_b_ready, d1)
                    product(n + 1, (s + 1) % 2, 2, h_hi, h_lo)
                    pe.wait_ge(branch_split, PAIRS + CT)
                    pe.wait_ge(weight_split, n + 3)
                    for branch, read, bank, hi, lo in ((0, branch_a, 4, att_hi, att_lo),
                                                       (1, branch_b, 6, conv_hi, conv_lo)):
                        pe.wait_ge(read, d1)
                        for k in range(4):
                            at_k = slice((4 * branch + k) * P, (4 * branch + k + 1) * P)
                            wh, wl = w_hi[:, s % 2, at_k], w_lo[:, s % 2, at_k]
                            for j, (w, a) in enumerate(((wh, hi), (wh, lo), (wl, hi))):
                                for t in range(2):
                                    last = pe.matmul(psum[:, bank + t, :], w, a[:, k, t * HALF:(t + 1) * HALF],
                                                     start=(k == 0 and j == 0), stop=(k == 3 and j == 2))
                    last.then_inc(tile_done, 1)

            project_out(T_OUT2, KT, KT)

            def ffn_up_part(c, n):
                for j in range(4):
                    up_product(n + j, j % 2, c * 4 + j, ffn_right, 2 * (j % 2))

            def ffn_down_part(c, n):
                pe.wait_ge(act_split, c * 2 + (2 * MLP_CHUNKS + 4))
                for j in range(2):
                    down(n + j, j, c * 16 + (16 * MLP_CHUNKS + 8 * j), ffn_hi, ffn_lo)

            sum_squares(4)
            pe.wait_ge(h_ready, 4 * KT)
            ffn_up_part(0, T_FFN)
            with pe.Fori(0, FFN_CHUNKS - 1) as i:
                ffn_up_part(i + 1, i * 6 + (T_FFN + 4))
                ffn_down_part(i, i * 6 + (T_FFN + 8))
            ffn_down_part(FFN_CHUNKS - 1, T_END - 2)

            sum_squares(5)
            pe.wait_ge(x_ready, 2 * KT)
            for t in range(KT):
                if t >= 2:
                    pe.wait_ge(y_copied, 2 * (t - 1))
                for d in range(0, KT, 4):
                    turn(x_t, 4 * (t % 2) + d // 4,
                         [x_t[:, d + c, t * P:(t + 1) * P] for c in range(4)], y_turned)

        @block.scalar
        def _(act):
            def squares(m, ready, count, eps):
                act.wait_ge(ready, count)
                for d in range(KT):
                    if KT * m + d >= 2:
                        act.wait_ge(sq_used, KT * m + d - 1)
                    act.activation(sq[:, d % 2, :], x_t[:, d, :], ACT.Square).then_inc(sq_ready, 1)
                act.wait_ge(sq_used, KT * (m + 1))
                act.activation(rinv[:, :], banks(4), ACT.Ln, scale=1.0 / D, bias=eps[:, :]).then_inc(mean_log, 1)
                act.wait_ge(mean_log, m + 1)
                act.activation(rinv[:, :], rinv[:, :], ACT.Exp, scale=-0.5).then_inc(rinv_ready, 1)

            def hi_parts(m):
                for d in range(KT):
                    act.wait_ge(h32_ready, KT * m + d + 1)
                    act.activation(h_hi[:, d, :], h32[:, d % 2, :], ACT.Copy).then_inc(h_hi_ready, 1)

            for t in range(KT):
                for j in range(2):
                    act.wait_ge(x_turned, 2 * t + j + 1)
                    act.activation(x_t[:, 4 * j:4 * j + 4, t * P:(t + 1) * P],
                                   psum[:, 4 * (t % 2) + j, :].rearrange("p (d t) -> p d t", t=P),
                                   ACT.Copy).then_inc(x_copied, 1)
            act.wait_ge(x_copied, 2 * KT)
            act.dma_start(x_spill, x_t[:, :, :].rearrange("p d t -> p (d t)")).then_inc(x_spilled, 16)
            act.wait_ge(rpb_loaded, 16)
            act.dma_start(rpb_spill, rpb_pad[0:NA_HEADS * RPB_H, :]).then_inc(rpb_stored, 16)
            act.wait_ge(rpb_stored, 16)
            for h in range(NA_HEADS):
                diagonals = bass.AP(rpb_spill.tensor, h * RPB_H * RPB_PAD + GRID_W - 1,
                                    [[RPB_PAD, RPB_H], [-1, GRID_W], [1, GRID_W]])
                to = bias_rows[h // 2, DH * (h % 2):DH * (h % 2) + GRID_W, :, :].rearrange("q r c -> r q c")
                act.dma_start(to, diagonals).then_inc(bias_stored, 16)
            act.wait_ge(cols_turned, 1)
            act.activation(cols[:, :], psum[:, 7, :], ACT.Copy).then_inc(cols_ready, 1)
            act.wait_ge(memsets, 4)
            squares(0, x_copied, 2 * KT, eps1)
            hi_parts(0)

            for j in range(2):
                act.wait_ge(tile_done, T_POOL + j + 1)
                act.activation(pool_u[:, j, POOL_PAD:], banks(2 * j), ACT.Copy).then_inc(pool_u_ready, 1)
            act.wait_ge(pool_w_zeroed, 1)
            for g in range(4):
                half = slice(64 * (g % 2), 64 * (g % 2) + 64)
                act.dma_start(pool_w[half, g // 2, half], dram["pool_w"][g, :, :]).then_inc(pool_loaded, 16)
            act.dma_start(pool_inv[:, :, :], dram["c_pool_inv"]).then_inc(pool_loaded, 16)
            act.dma_start(pair_mask[:, :, :], dram["c_pair_mask"]).then_inc(pool_loaded, 16)

            def take(z, n, bank, ready):
                act.wait_ge(tile_done, n + 1)
                act.activation(z[:, :], banks(bank), ACT.Copy).then_inc(ready, 1)

            def take_f(h):
                take(zf, h * 4 + T_HEADS, 0, zf_ready)

            def take_q(h):
                take(zq, h * 4 + (T_HEADS + 1), 2, zq_ready)

            def take_i(h):
                take(zv, h * 4 + (T_HEADS + 2), 0, zv_ready)

            def take_g(h):
                take(zg, h * 4 + (T_HEADS + 3), 2, zg_ready)

            for take_z in (take_f, take_q, take_i, take_g):
                take_z(0)
            act.wait_ge(x_spilled, 16)
            for j in range(2):
                act.wait_ge(pool_mixed, j + 1)
                act.activation(mix1[:, j, :], banks(4 + 2 * j), ACT.Copy,
                               scale=col("pool_scale", j)).then_inc(pool_ready, 1)

            def head(h, following):
                def level(l):
                    act.wait_ge(level_arg, h * LEVELS + (l + 1))
                    act.activation(e_t[:, l % 2, :], e_t[:, l % 2, :], ACT.Exp).then_inc(level_exp, 1)

                act.wait_ge(y_ready, h + 1)
                act.wait_ge(zf_ready, h + 1)
                act.activation(t1[:, :], zf[:, :], ACT.Abs).then_inc(abs_ready, 1)
                act.wait_ge(abs_ready, h + 1)
                act.activation(t1[:, :], t1[:, :], ACT.Exp, scale=-1.0).then_inc(exp_ready, 1)
                act.wait_ge(exp_ready, h + 1)
                act.activation(t1[:, :], t1[:, :], ACT.Ln, bias=one[:, :]).then_inc(log1p_ready, 1)
                act.wait_ge(lk_ready, h + 1)
                act.activation(k_t[:, :], t1[:, :], ACT.Exp).then_inc(k_ready, 1)
                act.wait_ge(zq_ready, h + 1)
                act.activation(q_t[:, :], zq[:, :], ACT.Silu).then_inc(q_ready, 1)
                act.wait_ge(zg_ready, h + 1)
                act.activation(sg_t[:, :], zg[:, :], ACT.Silu).then_inc(sg_ready, 1)
                act.wait_ge(v_turned, h + 1)
                act.activation(v_tok[:, :, :].rearrange("p c v -> p (c v)"), banks(4), ACT.Copy).then_inc(v_ready, 1)
                act.wait_ge(kd_arg, h + 1)
                act.activation(t1[:, :], t1[:, :], ACT.Exp).then_inc(kd_exp, 1)
                act.wait_ge(b_ready, h + 1)
                act.activation(t2[:, :], b_t[:, :], ACT.Exp).then_inc(b_exp, 1)
                act.activation(decay[:, :], b_t[:, CHUNK - 1:SEQ:CHUNK], ACT.Exp).then_inc(decay_ready, 1)
                level(0)
                level(1)
                if following is not None:
                    act.wait_ge(lk_ready, h + 1)
                    take_f(following)
                    act.wait_ge(q_ready, h + 1)
                    take_q(following)
                act.wait_ge(kd_turned, h + 1)
                act.activation(kd_tok[:, :, :].rearrange("p c k -> p (c k)"), banks(4), ACT.Copy)\
                   .then_inc(kd_tok_ready, 1)
                level(2)
                if following is not None:
                    act.wait_ge(v_turned, h + 1)
                    take_i(following)
                level(3)
                level(4)
                if following is not None:
                    act.wait_ge(sg_ready, h + 1)
                    take_g(following)
                level(5)
                level(6)
                act.wait_ge(o_done, h + 1)
                act.activation(t1[:, :], banks(6), ACT.Square).then_inc(o_sq, 1)
                act.wait_ge(o_mean, h + 1)
                act.activation(t2[:, :], banks(4), ACT.Ln, scale=1.0 / P, bias=eps1[:, :]).then_inc(o_log, 1)
                act.wait_ge(o_log, h + 2)
                act.activation(t2[:, :], t2[:, :], ACT.Exp, scale=-0.5).then_inc(o_inv, 1)

            with act.Fori(0, HEADS - 1) as i:
                head(i, i + 1)
            head(HEADS - 1, None)

            def split_mix(m, mix, ready, last_use):
                act.wait_ge(tile_done, last_use)
                for d in range(KT):
                    act.wait_ge(*ready(d))
                    act.activation(h_hi[:, d, :], mix[:, d, :], ACT.Copy).then_inc(mix_hi_ready, 1)

            split_mix(0, mix1, lambda d: (pool_ready, d + 1) if d < 2 else (y_ready, d), T_OUT1)
            act.wait_ge(mix_split, KT)
            act.dma_start(x_t[:, :, :].rearrange("p d t -> p (d t)"), x_spill).then_inc(x_back, 16)

            def split_activations(a, hi, first, after):
                if after is not None:
                    act.wait_ge(tile_done, after)
                for j in range(2):
                    act.wait_ge(act_ready, first + (j + 1))
                    act.activation(hi[:, j, :], a[:, j, :], ACT.Copy).then_inc(act_hi_ready, 1)

            def mlp_relu(c, n):
                for j in range(2):
                    act.wait_ge(tile_done, n + (j + 1))
                    act.wait_ge(act_split, c * 2 + (j + 1))
                    act.activation(mlp_a[:, j, :], banks(2 * j), ACT.Relu).then_inc(up_read, 1)

            squares(1, x_added, 2 + KT, eps1)
            hi_parts(1)
            mlp_relu(0, T_MLP)
            split_activations(mlp_a, mlp_hi, 0, None)
            with act.Fori(0, MLP_CHUNKS - 1) as i:
                mlp_relu(i + 1, i * 4 + (T_MLP + 2))
                split_activations(mlp_a, mlp_hi, i * 2 + 2, i * 4 + (T_MLP + 6))

            squares(2, down_added, 4 + 16 * MLP_CHUNKS, eps1)
            squares(3, x_ready, KT, eps2)
            act.dma_start(x_spill, x_t[:, :, :].rearrange("p d t -> p (d t)")).then_inc(x_spilled, 16)
            hi_parts(2)

            with act.Fori(0, CT // 2) as i:
                for s in range(2):
                    act.wait_ge(tile_done, i * 2 + (T_CB + s + 1))
                    act.activation(sig_cb[:, bass.ds(i * 2 + s, 1), :].rearrange("p a t -> p (a t)"), banks(2 * s),
                                   ACT.Sigmoid, bias=col("b_in_2", i * 2 + (CB2 // P + s))).then_inc(cb_ready, 1)

            act.wait_ge(x_spilled, 32)
            act.wait_ge(bias_stored, 16 * NA_HEADS)
            act.wait_ge(h_ready, 3 * KT)
            with act.Fori(0, PAIRS) as p:
                act.wait_ge(scores_max, p * ROWS + 2)
                act.dma_start(bias[:, :, :], bias_rows[bass.ds(p, 1), :, :, :].rearrange("a q r c -> (a q) r c"))\
                   .then_inc(bias_loaded, 16)
                act.wait_ge(tile_done, p * 4 + (T_PAIRS + 2))
                act.activation(v_t[:, :], banks(2), ACT.Identity, bias=col("b_in_2", p + V2 // P)).then_inc(vt_ready, 1)
                act.wait_ge(q32_ready, p + 1)
                for j in range(2):
                    half = slice(DH * j, DH * (j + 1))
                    last = act.activation(q_hi[half, :, half], q32[half, :].rearrange("p (r c) -> p r c", c=GRID_W),
                                          ACT.Copy)
                last.then_inc(q_hi_ready, 1)
                act.wait_ge(v_tiles_turned, p * 2 + 1)
                act.activation(v_even[:, :, :].rearrange("p c v -> p (c v)"), banks(4), ACT.Copy)\
                   .then_inc(v_tiles_ready, 1)
                act.wait_ge(v_tiles_turned, p * 2 + 2)
                act.activation(v_odd[:, 0:7, :].rearrange("p c v -> p (c v)"), banks(6)[:, 0:7 * P], ACT.Copy)\
                   .then_inc(v_tiles_ready, 1)
                act.wait_ge(k32_ready, p + 2)
                act.activation(k_hi[:, :], k32[:, :], ACT.Copy).then_inc(k_hi_ready, 1)
                for s in range(ROWS + 4):
                    if s < ROWS:
                        act.wait_ge(neg_max_ready, p * ROWS + (s + 1))
                        act.activation(prob[:, s % 3, :], prob[:, s % 3, :], ACT.Exp, bias=neg_max[:, s % 2:s % 2 + 1],
                                       accum_out=row_sum[:, s % 2:s % 2 + 1]).then_inc(prob_exp, 1)
                    if 2 <= s < ROWS + 2:
                        u = s - 2
                        act.wait_ge(prob_turned, p * ROWS + (u + 1))
                        act.activation(prob_t[:, u % 2, :], psum[:, 6 + u % 2, :], ACT.Copy).then_inc(prob_t_ready, 1)
                    if s >= 4 and s % 4 == 3:
                        pass
                    if s >= 4 and (s - 4) % 4 == 3:
                        g = (s - 4) // 4
                        act.wait_ge(pv_done, p * 4 + (g + 1))
                        for j in range(2):
                            half = slice(DH * j, DH * (j + 1))
                            dst = att_t[half, bass.ds(p, 1), 4 * g * GRID_W:4 * (g + 1) * GRID_W]
                            last = act.activation(
                                dst.rearrange("p a (r c) -> p (a r) c", c=GRID_W),
                                psum[half, g % 2, :].rearrange("p (r c) -> p r c", c=P)[:, :, half], ACT.Copy)
                        last.then_inc(att_ready, 1)

            act.wait_ge(att_ready, 4 + 4 * PAIRS)
            act.wait_ge(scores_done, ROWS * PAIRS)
            for c in range(PAIRS):
                act.activation(att_hi[:, c, :], att_t[:, c, :], ACT.Copy).then_inc(branch_hi, 1)
            act.wait_ge(ln_summed, 1)
            act.activation(ln_mean[:, :], banks(4), ACT.Copy, scale=1.0 / CONV_CH).then_inc(ln_mean_ready, 1)
            for c in range(CT):
                act.wait_ge(ln_centred, c + 1)
                act.activation(ln_sq[:, c, :], conv_t[:, c, :], ACT.Square).then_inc(ln_sq_ready, 1)
            act.wait_ge(ln_var, 1)
            act.activation(ln_inv[:, :], banks(6), ACT.Ln, scale=1.0 / CONV_CH, bias=eps2[:, :]).then_inc(ln_log, 1)
            act.wait_ge(ln_log, 1)
            act.activation(ln_inv[:, :], ln_inv[:, :], ACT.Exp, scale=-0.5).then_inc(ln_inv_ready, 1)
            for c in range(CT):
                act.wait_ge(ln_scaled, c + 1)
                act.activation(conv_t[:, c, :], conv_t[:, c, :], ACT.Silu, scale=col("conv_ln_g_2", c),
                               bias=col("conv_ln_b_2", c)).then_inc(ln_silu, 1)
                act.wait_ge(ln_silu, c + 1)
                act.activation(conv_hi[:, c, :], conv_t[:, c, :], ACT.Copy).then_inc(branch_hi, 1)

            with act.Fori(0, KT // 2) as i:
                for s in range(2):
                    n = i * 6 + (T_MERGE + 3 * s)
                    d1 = i * 2 + (s + 1)
                    act.wait_ge(tile_done, n + 1)
                    act.wait_ge(branch_a, d1)
                    act.activation(sig_a[:, :], banks(0), ACT.Sigmoid, bias=col("b_in_2", i * 2 + (GA2 // P + s)))\
                       .then_inc(gate_a_ready, 1)
                    act.wait_ge(tile_done, n + 2)
                    act.wait_ge(merged, d1)
                    act.activation(sig_b[:, :], banks(2), ACT.Sigmoid, bias=col("b_in_2", i * 2 + (GB2 // P + s)))\
                       .then_inc(gate_b_ready, 1)

            split_mix(1, mix2, lambda d: (merged, d + 2), T_OUT2)
            act.dma_start(x_t[:, :, :].rearrange("p d t -> p (d t)"), x_spill).then_inc(x_back, 16)

            def ffn_middle(c, n):
                for j in range(2):
                    for part, buf in enumerate((ffn_gate, ffn_val)):
                        act.wait_ge(tile_done, n + (2 * j + part + 1))
                        act.wait_ge(act_ready, c * 2 + (2 * MLP_CHUNKS + j))
                        k = c * 2 + (part * FT2 + j)
                        act.activation(buf[:, :], banks(2 * part), ACT.Identity, scale=col("ffn_dw_w_2/1", k),
                                       bias=col("ffn_dw_b_2", k)).then_inc(ffn_mid, 1)
                        if part == 0:
                            act.wait_ge(ffn_right, c * 4 + (2 + 2 * j + 1))
                            act.activation(ffn_gate[:, :], ffn_gate[:, :], ACT.Gelu).then_inc(ffn_gelu, 1)

            squares(4, x_added, 2 + 2 * KT, eps2)
            hi_parts(3)
            ffn_middle(0, T_FFN)
            split_activations(ffn_a, ffn_hi, 2 * MLP_CHUNKS, None)
            with act.Fori(0, FFN_CHUNKS - 1) as i:
                ffn_middle(i + 1, i * 6 + (T_FFN + 4))
                split_activations(ffn_a, ffn_hi, i * 2 + (2 * MLP_CHUNKS + 2), i * 6 + (T_FFN + 10))

            squares(5, down_added, 4 + 16 * (MLP_CHUNKS + FFN_CHUNKS), eps2)
            for t in range(KT):
                for j in range(2):
                    act.wait_ge(y_turned, 2 * t + j + 1)
                    act.activation(y_tok[:, t, j * HALF:(j + 1) * HALF], psum[:, 4 * (t % 2) + j, :], ACT.Copy)\
                       .then_inc(y_copied, 1)

        @block.vector
        def _(dve):
            dve.sem_inc(down_added, 4)
            dve.sem_inc(x_added, 2)
            dve.sem_inc(o_log, 1)
            dve.sem_inc(o_scaled, 1)
            dve.sem_inc(y_ready, 1)
            dve.sem_inc(up_read, 2)
            dve.sem_inc(act_split, 2)
            dve.sem_inc(cb_ready, 2)
            dve.sem_inc(att_ready, 4)
            dve.sem_inc(k32_ready, 1)
            dve.sem_inc(scores_max, 2)
            dve.sem_inc(prob_t_ready, 2)
            for free in (gate_a_ready, gate_b_ready, branch_a, branch_b, merged):
                dve.sem_inc(free, 1)
            dve.sem_inc(ffn_right, 2)

            def normed(m, k, gain):
                dve.wait_ge(rinv_ready, m + 1)
                for d in range(KT + 1):
                    if d < KT:
                        if d >= 2:
                            dve.wait_ge(h_ready, KT * k + d - 1)
                        dve.scalar_tensor_tensor(h32[:, d % 2, :], x_t[:, d, :], col(gain, d), rinv[:, :],
                                                 ALU.mult, ALU.mult).then_inc(h32_ready, 1)
                    if d >= 1:
                        dve.wait_ge(h_hi_ready, KT * k + d)
                        dve.tensor_tensor(h_lo[:, d - 1, :], h32[:, (d - 1) % 2, :],
                                          h_hi[:, d - 1, :].bitcast(F32), ALU.subtract).then_inc(h_ready, 1)

            def normed_in_place(m, gain):
                dve.wait_ge(rinv_ready, m + 1)
                for d in range(KT):
                    dve.scalar_tensor_tensor(x_t[:, d, :], x_t[:, d, :], col(gain, d), rinv[:, :],
                                             ALU.mult, ALU.mult).then_inc(x_ready, 1)

            dve.wait_ge(cols_ready, 1)
            normed(0, 0, "norm_mix_g")

            dve.wait_ge(h_ready, KT)
            dve.memset(resets[:, :], 1.0).then_inc(pool_step, 1)
            dve.wait_ge(pool_step, 1)
            dve.memset(resets[:, 0:SEQ:CHUNK], 0.0).then_inc(pool_step, 1)
            dve.memset(pool_w[:, :, :], 0.0).then_inc(pool_w_zeroed, 1)
            dve.memset(pool_u[:, :, 0:POOL_PAD], 0.0)
            dve.memset(pool_a[:, 0:POOL_PAD], 0.0)
            dve.memset(pool_b[:, 0:POOL_PAD], 0.0).then_inc(pool_step, 1)
            steps = 3
            dve.wait_ge(pool_loaded, 16 * 6)
            for j in range(2):
                dve.wait_ge(pool_u_ready, j + 1)
                src, sums, shift = pool_u[:, j, :], [], 1
                spare = [pool_a, pool_b]
                for n in range(2 * j + 2):
                    dst = spare[n % 2][:, :]
                    dve.wait_ge(pool_step, steps)
                    dve.tensor_tensor(dst[:, POOL_PAD:], src[:, POOL_PAD:], src[:, POOL_PAD - shift:PADDED - shift],
                                      ALU.add).then_inc(pool_step, 1)
                    steps += 1
                    sums.append(dst)
                    src, shift = dst, 2 * shift
                dve.wait_ge(pool_step, steps)
                for half, window_sum in ((slice(0, 64), sums[-2]), (slice(64, P), sums[-1])):
                    dve.tensor_tensor(pool_p[half, j, :], window_sum[half, POOL_PAD:], pool_inv[half, j, :],
                                      ALU.mult).then_inc(pool_step, 1)
                    steps += 1
                dve.wait_ge(pool_step, steps)
                dve.tensor_tensor(pool_p[:, j, :], pool_p[:, j, :], pool_u[:, j, POOL_PAD:], ALU.subtract)\
                   .then_inc(pool_p_ready, 1)

            dve.wait_ge(x_spilled, 16)
            dve.wait_ge(pool_ready, 2)
            dve.memset(s_t[:, :, :], 0.0).then_inc(pool_step, 1)
            steps += 1
            dve.wait_ge(pool_step, steps)

            def head(h):
                def exponents(l):
                    b, e = level_parts(b_t[:, :], l), level_parts(e_t[:, l % 2, :], l)
                    s = 1 << l
                    n = SEQ // (2 * s)
                    middle = b[:, :, 0, s - 1:s].to_broadcast([P, n, s])
                    dve.tensor_tensor(e[:, :, 0, :], middle, b[:, :, 0, :], ALU.subtract)
                    dve.tensor_tensor(e[:, :, 1, :], b[:, :, 1, :], middle, ALU.subtract).then_inc(level_arg, 1)

                def decayed(l):
                    dve.wait_ge(level_exp, h * LEVELS + (l + 1))
                    e = level_parts(e_t[:, l % 2, :], l)
                    k, q = level_parts(k_t[:, :], l), level_parts(q_t[:, :], l)
                    dve.tensor_tensor(e[:, :, 0, :], e[:, :, 0, :], k[:, :, 0, :], ALU.mult)
                    dve.tensor_tensor(e[:, :, 1, :], e[:, :, 1, :], q[:, :, 1, :], ALU.mult).then_inc(level_ready, 1)

                def merge(l, first_bank):
                    if l >= 1:
                        dve.wait_ge(level_merged, h * (LEVELS + 1) + l)
                    dve.wait_ge(level_done, h * (LEVELS + 1) + (l + 1))
                    dve.sem_inc(dve_passed, 1)
                    mask = pair_mask[:, l:l + 1, :].bitcast(U32).to_broadcast([P, NC, CHUNK])
                    dve.copy_predicated(s_t[:, :, :], mask, banks(first_bank).rearrange("p (c t) -> p c t", t=CHUNK))\
                       .then_inc(level_merged, 1)

                dve.wait_ge(log1p_ready, h + 1)
                dve.scalar_tensor_tensor(t2[:, :], zf[:, :], 0.0, t1[:, :], ALU.min, ALU.subtract).then_inc(logf_ready, 1)
                dve.wait_ge(logf_ready, h + 1)
                dve.tensor_tensor_scan(b_t[:, :], resets[:, :], t2[:, :], 0.0, ALU.mult, ALU.add).then_inc(b_ready, 1)
                dve.tensor_tensor(t1[:, :], t2[:, :], zf[:, :], ALU.subtract).then_inc(lk_ready, 1)
                dve.wait_ge(b_ready, h + 1)
                exponents(0)
                exponents(1)
                dve.wait_ge(k_ready, h + 1)
                ends = b_t[:, :].rearrange("p (c t) -> p c t", t=CHUNK)
                dve.tensor_tensor(t1[:, :].rearrange("p (c t) -> p c t", t=CHUNK),
                                  ends[:, :, CHUNK - 1:CHUNK].to_broadcast([P, NC, CHUNK]), ends,
                                  ALU.subtract).then_inc(kd_arg, 1)
                dve.wait_ge(kd_exp, h + 1)
                dve.tensor_tensor(t1[:, :], t1[:, :], k_t[:, :], ALU.mult).then_inc(kd_ready, 1)
                dve.wait_ge(q_ready, h + 1)
                decayed(0)
                dve.wait_ge(b_exp, h + 1)
                dve.tensor_tensor(qe_t[:, :], q_t[:, :], t2[:, :], ALU.mult).then_inc(qe_ready, 1)
                decayed(1)
                merge(0, 6)
                exponents(2)
                dve.wait_ge(update_done, h + 1)
                dve.wait_ge(decay_ready, h + 1)
                for c in range(NC - 1):
                    update = psum[:, 6 + c // 4, (c % 4) * P:(c % 4 + 1) * P]
                    if c == 0:
                        dve.tensor_copy(states[:, 1, :], update).then_inc(state_ready, 1)
                    else:
                        dve.wait_ge(state_ready, h * (NC - 1) + c)
                        dve.scalar_tensor_tensor(states[:, c + 1, :], states[:, c, :], decay[:, c:c + 1], update,
                                                 ALU.mult, ALU.add).then_inc(state_ready, 1)
                for l in range(2, LEVELS):
                    decayed(l)
                    merge(l - 1, 4 if l % 2 == 0 else 6)
                    if l + 1 < LEVELS:
                        exponents(l + 1)
                merge(LEVELS - 1, 6)
                merge(LEVELS, 4)
                dve.wait_ge(o_inv, h + 1)
                dve.tensor_tensor(t1[:, :], banks(6), t2[:, :], ALU.mult).then_inc(o_scaled, 1)
                dve.wait_ge(o_scaled, h + 2)
                dve.wait_ge(sg_ready, h + 1)
                y = mix1[:, h + 2, :] if isinstance(h, int) else \
                    mix1[:, bass.ds(h + 2, 1), :].rearrange("p a t -> p (a t)")
                dve.scalar_tensor_tensor(y, t1[:, :], col("hgrn_norm_g", h), sg_t[:, :], ALU.mult, ALU.mult)\
                   .then_inc(y_ready, 1)

            with dve.Fori(0, HEADS - 1) as i:
                head(i)
            head(HEADS - 1)

            def project_out(m, mix, first_tile):
                for d in range(KT):
                    dve.wait_ge(mix_hi_ready, KT * m + d + 1)
                    dve.tensor_tensor(h_lo[:, d, :], mix[:, d, :], h_hi[:, d, :].bitcast(F32),
                                      ALU.subtract).then_inc(mix_split, 1)
                dve.wait_ge(x_back, 16 * (m + 1))
                with dve.Fori(0, KT // 2) as i:
                    for s in range(2):
                        dve.wait_ge(tile_done, i * 2 + (first_tile + s + 1))
                        x_d = x_t[:, bass.ds(i * 2 + s, 1), :].rearrange("p a t -> p (a t)")
                        dve.tensor_tensor(x_d, x_d, banks(2 * s), ALU.add).then_inc(x_added, 1)

            project_out(0, mix1, T_OUT1)

            def add_down(c, n, first_chunk):
                for part in range(2):
                    for g in range(8):
                        if g < 7:
                            dve.wait_ge(down_done, c * 14 + (14 * first_chunk + 7 * part + g + 1))
                        else:
                            dve.wait_ge(tile_done, n + (part + 1))
                        x_d = x_t[:, 4 * part + g // 2, (g % 2) * HALF:(g % 2 + 1) * HALF]
                        dve.tensor_tensor(x_d, x_d, psum[:, 4 + g % 4, :], ALU.add).then_inc(down_added, 1)

            def lo_activations(a, hi, lo, first):
                for j in range(2):
                    dve.wait_ge(act_hi_ready, first + (j + 1))
                    dve.tensor_tensor(lo[:, j, :], a[:, j, :], hi[:, j, :].bitcast(F32),
                                      ALU.subtract).then_inc(act_split, 1)

            def mlp_square(c):
                for j in range(2):
                    dve.wait_ge(up_read, c * 2 + (2 + j + 1))
                    dve.tensor_tensor(mlp_a[:, j, :], mlp_a[:, j, :], mlp_a[:, j, :], ALU.mult).then_inc(act_ready, 1)

            normed(1, 1, "norm_mlp_g")
            mlp_square(0)
            lo_activations(mlp_a, mlp_hi, mlp_lo, 0)
            with dve.Fori(0, MLP_CHUNKS - 1) as i:
                mlp_square(i + 1)
                add_down(i, i * 4 + (T_MLP + 4), 0)
                lo_activations(mlp_a, mlp_hi, mlp_lo, i * 2 + 2)
            add_down(MLP_CHUNKS - 1, T_CB - 2, 0)

            normed_in_place(2, "final_norm_g")
            normed(3, 2, "norm1_g_2")

            dve.memset(q_hi[:, :, :].bitcast(F32), 0.0)
            dve.memset(q_lo[:, :, :].bitcast(F32), 0.0).then_inc(q_zeroed, 1)
            dve.memset(u_t[:, 0:CONV_PAD], 0.0)
            dve.memset(u_t[:, CONV_PAD + SEQ:], 0.0).then_inc(u_zeroed, 1)
            dve.wait_ge(q_zeroed, 1)
            dve.wait_ge(u_zeroed, 1)
            dve.wait_ge(x_spilled, 32)

            with dve.Fori(0, PAIRS) as p:
                def convolve(taps):
                    acc = conv_t[:, bass.ds(p, 1), :].rearrange("p a t -> p (a t)")
                    for tap in taps:
                        w = col("conv_dw_w_2", p + tap * CT)
                        if tap == 0:
                            dve.tensor_scalar(acc, u_t[:, 0:SEQ], w, col("conv_dw_b_2", p), ALU.mult, ALU.add)\
                               .then_inc(conv_step, 1)
                        else:
                            dve.wait_ge(conv_step, p * CONV_K + tap)
                            dve.scalar_tensor_tensor(acc, u_t[:, tap:tap + SEQ], w, acc, ALU.mult, ALU.add)\
                               .then_inc(conv_step, 1)

                dve.wait_ge(bias_loaded, p * 16 + 16)
                dve.tensor_tensor(bias[:, :, :], bias[:, :, :],
                                  col_mask[:, :].unsqueeze(1).to_broadcast([P, RPB_H, GRID_W]),
                                  ALU.add).then_inc(bias_ready, 1)
                dve.wait_ge(tile_done, p * 4 + (T_PAIRS + 1))
                dve.scalar_tensor_tensor(u_t[:, CONV_PAD:CONV_PAD + SEQ], banks(0), col("b_in_2", p + CA2 // P),
                                         sig_cb[:, bass.ds(p, 1), :].rearrange("p a t -> p (a t)"),
                                         ALU.add, ALU.mult).then_inc(u_ready, 1)
                dve.wait_ge(u_ready, p + 1)
                convolve(range(0, 14))
                dve.wait_ge(tile_done, p * 4 + (T_PAIRS + 3))
                dve.tensor_scalar(q32[:, :], banks(0), col("b_in_2", p + Q2 // P), DH ** -0.5, ALU.add, ALU.mult)\
                   .then_inc(q32_ready, 1)
                convolve(range(14, 20))
                dve.wait_ge(q_hi_ready, p + 1)
                for j in range(2):
                    half = slice(DH * j, DH * (j + 1))
                    last = dve.tensor_tensor(q_lo[half, :, half], q32[half, :].rearrange("p (r c) -> p r c", c=GRID_W),
                                             q_hi[half, :, half].bitcast(F32), ALU.subtract)
                last.then_inc(q_split, 1)
                dve.wait_ge(tile_done, p * 4 + (T_PAIRS + 4))
                dve.tensor_scalar(k32[:, :], banks(2), col("b_in_2", p + K2 // P), None, ALU.add).then_inc(k32_ready, 1)
                dve.wait_ge(k_hi_ready, p + 1)
                dve.tensor_tensor(k_lo[:, :], k32[:, :], k_hi[:, :].bitcast(F32), ALU.subtract).then_inc(k_split, 1)
                dve.wait_ge(bias_ready, p + 1)
                for s in range(ROWS + 1):
                    if s < ROWS:
                        dve.wait_ge(scores_done, p * ROWS + (s + 1))
                        dve.sem_inc(dve_passed, 1)
                        _, first = row_window(s)
                        dve.tensor_tensor_reduce(
                            out=prob[:, s % 3, :], in0=psum[:, 4 + s % 2, :],
                            in1=bias[:, first:first + KH, :].rearrange("p r c -> p (r c)"), scale=1.0, scalar=3 * NEG,
                            op0=ALU.add, op1=ALU.max, accum_out=row_max[:, s % 2:s % 2 + 1]).then_inc(scores_max, 1)
                        dve.wait_ge(scores_max, p * ROWS + (s + 3))
                        dve.tensor_scalar(neg_max[:, s % 2:s % 2 + 1], row_max[:, s % 2:s % 2 + 1], -1.0, None,
                                          ALU.mult).then_inc(neg_max_ready, 1)
                    if s >= 1:
                        u = s - 1
                        dve.wait_ge(prob_exp, p * ROWS + (u + 1))
                        dve.reciprocal(row_inv[:, u % 2:u % 2 + 1], row_sum[:, u % 2:u % 2 + 1]).then_inc(inv_ready, 1)
                        dve.wait_ge(inv_ready, p * ROWS + (u + 1))
                        dve.tensor_scalar(prob[:, u % 3, :], prob[:, u % 3, :], row_inv[:, u % 2:u % 2 + 1], None,
                                          ALU.mult).then_inc(prob_ready, 1)
                    if s >= 5 and 15 + s < CONV_K:
                        convolve([15 + s])
                convolve(range(31, CONV_K))

            for c in range(PAIRS):
                dve.wait_ge(branch_hi, c + 1)
                dve.tensor_tensor(att_lo[:, c, :], att_t[:, c, :], att_hi[:, c, :].bitcast(F32), ALU.subtract)\
                   .then_inc(branch_split, 1)
            dve.wait_ge(ln_mean_ready, 1)
            for c in range(CT):
                dve.tensor_tensor(conv_t[:, c, :], conv_t[:, c, :], ln_mean[:, :], ALU.subtract).then_inc(ln_centred, 1)
            dve.wait_ge(ln_inv_ready, 1)
            for c in range(CT):
                dve.tensor_tensor(conv_t[:, c, :], conv_t[:, c, :], ln_inv[:, :], ALU.mult).then_inc(ln_scaled, 1)
            for c in range(CT):
                dve.wait_ge(branch_hi, PAIRS + c + 1)
                dve.tensor_tensor(conv_lo[:, c, :], conv_t[:, c, :], conv_hi[:, c, :].bitcast(F32), ALU.subtract)\
                   .then_inc(branch_split, 1)

            with dve.Fori(0, KT // 2) as i:
                for s in range(2):
                    d1 = i * 2 + (s + 1)
                    dve.wait_ge(tile_done, i * 6 + (T_MERGE + 3 * s + 3))
                    dve.wait_ge(merged, d1)
                    dve.wait_ge(gate_a_ready, d1 + 1)
                    dve.tensor_tensor(br_a[:, :], sig_a[:, :], banks(4), ALU.mult).then_inc(branch_a, 1)
                    dve.wait_ge(gate_b_ready, d1 + 1)
                    dve.tensor_tensor(sig_b[:, :], sig_b[:, :], banks(6), ALU.mult).then_inc(branch_b, 1)
                    dve.wait_ge(branch_b, d1 + 1)
                    dve.tensor_tensor(mix2[:, bass.ds(i * 2 + s, 1), :].rearrange("p a t -> p (a t)"), br_a[:, :],
                                      sig_b[:, :], ALU.add).then_inc(merged, 1)

            project_out(1, mix2, T_OUT2)

            def ffn_taps(c):
                for j in range(2):
                    for part, buf in enumerate((ffn_gate, ffn_val)):
                        tile = c * 4 + (2 * j + part)
                        k = c * 2 + (part * FT2 + j)
                        dve.wait_ge(ffn_mid, tile + 1)
                        dve.scalar_tensor_tensor(buf[:, 1:], banks(2 * part)[:, 0:SEQ - 1], col("ffn_dw_w_2/0", k),
                                                 buf[:, 1:], ALU.mult, ALU.add).then_inc(ffn_left, 1)
                        dve.wait_ge(ffn_left, tile + 1)
                        dve.scalar_tensor_tensor(buf[:, 0:SEQ - 1], banks(2 * part)[:, 1:], col("ffn_dw_w_2/2", k),
                                                 buf[:, 0:SEQ - 1], ALU.mult, ALU.add).then_inc(ffn_right, 1)
                    dve.wait_ge(ffn_gelu, c * 2 + (j + 1))
                    dve.wait_ge(ffn_right, c * 4 + (2 * j + 4))
                    dve.tensor_tensor(ffn_a[:, j, :], ffn_gate[:, :], ffn_val[:, :], ALU.mult).then_inc(act_ready, 1)

            normed(4, 3, "norm2_g_2")
            ffn_taps(0)
            lo_activations(ffn_a, ffn_hi, ffn_lo, 2 * MLP_CHUNKS)
            with dve.Fori(0, FFN_CHUNKS - 1) as i:
                ffn_taps(i + 1)
                add_down(i, i * 6 + (T_FFN + 8), MLP_CHUNKS)
                lo_activations(ffn_a, ffn_hi, ffn_lo, i * 2 + (2 * MLP_CHUNKS + 2))
            add_down(FFN_CHUNKS - 1, T_END - 2, MLP_CHUNKS)

            normed_in_place(5, "norm_f_g_2")


_INS = ["x", "norm_mix_g", "w_in", "pool_w", "pool_scale", "hgrn_norm_g", "w_out", "norm_mlp_g", "w_up", "w_down",
        "final_norm_g", "norm1_g_2", "w_in_2", "b_in_2", "rpb_2", "w_na_out_2", "conv_dw_w_2", "conv_dw_b_2",
        "conv_ln_g_2", "conv_ln_b_2", "w_conv_out_2", "w_out_2", "norm2_g_2", "w_up_2", "ffn_dw_w_2", "ffn_dw_b_2",
        "w_down_2", "norm_f_g_2"]


def _constants():
    import numpy as np

    s, t = np.arange(CHUNK)[:, None], np.arange(CHUNK)[None, :]
    masks = [((s >> (l + 1)) == (t >> (l + 1))) & ((s >> l) & 1 == 0) & ((t >> l) & 1 == 1) for l in range(LEVELS)]
    masks.append(s == t)
    tokens = np.arange(1, SEQ + 1)
    windows = np.repeat(np.array(POOL_WINDOWS), POOL_W // len(POOL_WINDOWS))
    inv = 1.0 / np.minimum(tokens[None, :], windows[:, None])
    c = np.arange(P)[:, None] % GRID_W
    k = np.arange(GRID_W)[None, :]
    first = np.clip(c - KW // 2, 0, GRID_W - KW)
    return {
        "c_ident": np.eye(P, dtype=np.float32),
        "c_pair_mask": np.stack(masks, axis=1).astype(np.float32),
        "c_pool_inv": np.ascontiguousarray(inv.reshape(2, P, SEQ).transpose(1, 0, 2)).astype(np.float32),
        "c_col_mask": np.where((k >= first) & (k < first + KW), 0.0, NEG).astype(np.float32),
    }


def kernel(**inputs):
    import numpy as np
    import concourse.bacc as bacc
    from concourse.bass_utils import run_bass_kernel_spmd as run

    nc = bacc.Bacc("TRN2", target_bir_lowering=False, num_devices=1)
    arrays, dram = {}, {}
    given = {name: np.ascontiguousarray(inputs[name]) for name in _INS} | _constants()
    for name, a in given.items():
        if name not in ("x", "final_norm_g", "norm_f_g_2") and not name.startswith("c_"):
            a = a[0]
        arrays[f"in_{name}"] = a
        dram[name] = nc.dram_tensor(f"in_{name}", a.shape, mybir.dt.from_np(a.dtype), kind="ExternalInput").ap()
    out = nc.dram_tensor("out", (1, SEQ, D), F32, kind="ExternalOutput").ap()
    two_blocks(nc, dram, out)
    return run(nc, [arrays], core_ids=[0]).results[0]["out"]
```

```python
import concourse.bass as bass
from concourse import mybir
from contextlib import ExitStack

F32 = mybir.dt.float32
F32R = mybir.dt.float32r
U32 = mybir.dt.uint32
ACT = mybir.ActivationFunctionType
ALU = mybir.AluOpType
AX = mybir.AxisListType

P = 128
SEQ = 1024
D = 1024
KT = D // P
HALF = 512
BANKS = 8
POOL_W = 256
POOL_WINDOWS = (2, 4, 8, 16)
POOL_PAD = 16
HEADS = 6
HG_W = HEADS * P
CHUNK = 128
NC = SEQ // CHUNK
LEVELS = 7
MASK_W = LEVELS * CHUNK // 2 + CHUNK
D_FF = 4096
GRID_W = 64
ROWS = SEQ // GRID_W
NA_HEADS = 8
DH = 64
D_ATTN = NA_HEADS * DH
KH, KW = 8, 16
WIN = KH * GRID_W
PAIRS = NA_HEADS // 2
RPB_H, RPB_W = 2 * KH - 1, 2 * KW - 1
RPB_PAD = 128
NEG = -1e30
CONV_CH = 512
CT = CONV_CH // P
CONV_K = 31
CONV_PAD = CONV_K // 2
D_FF2 = 2816
FT2 = D_FF2 // P
FFN_K = 3
MLP_CHUNKS = D_FF // (2 * P)
FFN_CHUNKS = FT2 // 2
EPS1, EPS2 = 1e-5, 1e-6

Q1, F1, I1, G1 = POOL_W, POOL_W + HG_W, POOL_W + 2 * HG_W, POOL_W + 3 * HG_W
Q2, K2, V2 = 0, D_ATTN, 2 * D_ATTN
CA2, CB2 = 3 * D_ATTN, 3 * D_ATTN + CONV_CH
GA2, GB2 = 3 * D_ATTN + 2 * CONV_CH, 3 * D_ATTN + 2 * CONV_CH + D
D_IN2 = GB2 + D

VECTORS = [
    [("norm_mix_g", 8), ("pool_scale", 2), ("hgrn_norm_g", 6), ("norm_mlp_g", 8), ("final_norm_g", 8),
     ("norm1_g_2", 8), ("b_in_2", D_IN2 // P), ("norm2_g_2", 8), ("norm_f_g_2", 8), ("conv_dw_b_2", CT),
     ("conv_ln_g_2", CT), ("conv_ln_b_2", CT)],
    [("ffn_dw_b_2", 2 * FT2), ("ffn_dw_w_2/0", 2 * FT2)],
    [("ffn_dw_w_2/1", 2 * FT2), ("ffn_dw_w_2/2", 2 * FT2)],
    [("conv_dw_w_2", CONV_K * CT)],
]
STACK_ROWS = [sum(n for _, n in stack) for stack in VECTORS]
COL = {}
for _s, _stack in enumerate(VECTORS):
    _at = _s * P
    for _name, _n in _stack:
        COL[_name] = _at
        _at += _n

T_POOL = 0
T_HEADS = T_POOL + POOL_W // P
T_OUT1 = T_HEADS + 4 * HEADS
T_MLP = T_OUT1 + KT
T_CB = T_MLP + 4 * MLP_CHUNKS
T_PAIRS = T_CB + CT
T_MERGE = T_PAIRS + 4 * PAIRS
T_OUT2 = T_MERGE + 3 * KT
T_FFN = T_OUT2 + KT
T_END = T_FFN + 6 * FFN_CHUNKS

H_MIX1 = 0
H_MLP = H_MIX1 + 2 * KT
H_MIX2 = H_MLP + KT
H_FFN = H_MIX2 + KT
SUMS_MIX1 = 0
SUMS_MLP = SUMS_MIX1 + 2 * (KT - 1)
SUMS_MIX2 = SUMS_MLP + KT - 1
SUMS_FFN = SUMS_MIX2 + 2 * KT - 1
SUMS_OUT = SUMS_FFN + KT - 1

BASE = 16512
KB = 1024
A_X = BASE
A_HI = A_X + 32 * KB
A_LO = A_HI + 32 * KB
A_RAW = A_LO + 32 * KB
A_WHI = A_RAW + 8 * KB
A_WLO = A_WHI + 8 * KB
A_CONST = A_WLO + 8 * KB
A_ARENA = A_CONST + 9 * KB
A_END = 229344


def two_blocks(nc, dram, out):
    ctx = ExitStack()
    with ctx:
        def sem(name):
            return ctx.enter_context(nc.semaphore(name))

        def at(name, shape, address, dtype=F32):
            return nc.alloc_sbuf_tensor_at(name, shape, dtype, offset=address)

        x_t = at("x_t", [P, KT, SEQ], A_X)
        mix1 = at("mix1", [P, KT, SEQ], A_X)
        h_hi = at("h_hi", [P, KT, SEQ], A_HI, F32R)
        h_lo = at("h_lo", [P, KT, SEQ], A_LO, F32R)
        w_raw = at("w_raw", [P, 2, 1024], A_RAW)
        w_hi = at("w_hi", [P, 2, 1024], A_WHI, F32R)
        w_lo = at("w_lo", [P, 2, 1024], A_WLO, F32R)

        ident = at("ident", [P, P], A_CONST)
        ones = at("ones", [P, P], A_CONST + 512)
        cols = at("cols", [P, 4 * P], A_CONST + 1024)
        eps1, eps2, one, decay, row_max, neg_max, row_sum, row_inv = (
            at(name, [P, n], A_CONST + 4096 + 32 * j) for j, (name, n) in enumerate(
                (("eps1", 1), ("eps2", 1), ("one", 1), ("decay", NC), ("row_max", 2), ("neg_max", 2),
                 ("row_sum", 2), ("row_inv", 2))))
        col_mask = at("col_mask", [P, GRID_W], A_CONST + 4352)
        gain_both, gain_sq, q_bias, out_inv = (
            at(name, [P, 8], A_CONST + 4608 + 32 * j)
            for j, name in enumerate(("gain_both", "gain_sq", "q_bias", "out_inv")))
        rinv = at("rinv", [P, SEQ], A_CONST + 5 * KB)

        def arena(*shapes):
            got, a = [], A_ARENA
            for name, shape, dtype in shapes:
                size = 4
                for n in shape[1:]:
                    size *= n
                got.append(at(name, shape, a, dtype))
                a += -(-size // 32) * 32
            assert a <= A_END, a
            return got

        x_in, stack_rows, rpb_pad = arena(
            ("x_in", [P, KT, D], F32), ("stack_rows", [P, 4, P], F32), ("rpb_pad", [P, RPB_PAD], F32))
        A_NORM = (A_END - 20 * KB) // 32 * 32
        sq = at("sq", [P, 2, SEQ], A_NORM)
        sq_sum = at("sq_sum", [P, SEQ], A_NORM + 8 * KB)
        sq_sum_gain = at("sq_sum_gain", [P, SEQ], A_NORM + 12 * KB)
        rinv1 = at("rinv1", [P, SEQ], A_NORM + 16 * KB)
        (zf, zq, zv, zg, decays, k_t, kd_t, q_t, qd_t, sg_t, v_tok, e_t, s_t, kd_tok, states, pool_w,
         pair_mask) = arena(
            ("zf", [P, SEQ], F32), ("zq", [P, SEQ], F32), ("zv", [P, SEQ], F32), ("zg", [P, SEQ], F32),
            ("decays", [P, 2 * SEQ], F32), ("k_t", [P, SEQ], F32), ("kd_t", [P, SEQ], F32),
            ("q_t", [P, SEQ], F32), ("qd_t", [P, SEQ], F32), ("sg_t", [P, SEQ], F32),
            ("v_tok", [P, NC, P], F32), ("e_t", [P, 2, SEQ], F32), ("s_t", [P, SEQ], F32),
            ("kd_tok", [P, NC, P], F32), ("states", [P, NC, P], F32), ("pool_w", [P, 2, P], F32),
            ("pair_mask", [P, MASK_W], F32))
        PADDED = POOL_PAD + SEQ
        A_POOL = A_ARENA + 16 * KB
        pool_u = at("pool_u", [P, 2, PADDED], A_POOL)
        pool_a = at("pool_a", [P, PADDED], A_POOL + 2 * 4 * PADDED)
        pool_b = at("pool_b", [P, PADDED], A_POOL + 3 * 4 * PADDED)
        pool_inv = at("pool_inv", [P, 2, SEQ], A_POOL + 4 * 4 * PADDED)
        pool_p = at("pool_p", [P, 2, SEQ], A_POOL + 4 * 4 * PADDED + 8 * KB)
        assert A_POOL + 4 * 4 * PADDED + 16 * KB <= A_ARENA + 68 * KB
        mlp_a, mlp_hi, mlp_lo = arena(
            ("mlp_a", [P, 2, SEQ], F32), ("mlp_hi", [P, 2, SEQ], F32R), ("mlp_lo", [P, 2, SEQ], F32R))
        ffn_z, ffn_gate, ffn_val, ffn_a, ffn_hi, ffn_lo = arena(
            ("ffn_z", [P, 2, SEQ], F32),
            ("ffn_gate", [P, SEQ], F32), ("ffn_val", [P, SEQ], F32), ("ffn_a", [P, 2, SEQ], F32),
            ("ffn_hi", [P, 2, SEQ], F32R), ("ffn_lo", [P, 2, SEQ], F32R))
        conv_t = at("conv_t", [P, CT, SEQ], A_X)
        att_t = at("att_t", [P, PAIRS, SEQ], A_X + 16 * KB)
        conv_lo = at("conv_lo", [P, CT, SEQ], A_X, F32R)
        att_lo = at("att_lo", [P, PAIRS, SEQ], A_X + 16 * KB, F32R)
        U_PAD = CONV_PAD + SEQ + CONV_PAD
        (sig_cb, q_hi, q_lo, k_hi, k_lo, v_t, v_even, v_odd, bias, prob, prob_t, u_t, q32, k32) = arena(
            ("sig_cb", [P, CT, SEQ], F32), ("q_hi", [P, ROWS, P], F32R), ("q_lo", [P, ROWS, P], F32R),
            ("k_hi", [P, SEQ], F32R), ("k_lo", [P, SEQ], F32R), ("v_t", [P, SEQ], F32),
            ("v_even", [P, SEQ // P, P], F32), ("v_odd", [P, SEQ // P, P], F32),
            ("bias", [P, RPB_H, GRID_W], F32), ("prob", [P, 3, WIN], F32), ("prob_t", [P, 2, WIN], F32),
            ("u_t", [P, U_PAD], F32), ("q32", [P, SEQ], F32), ("k32", [P, SEQ], F32))
        conv_hi, att_hi, mix2, sig_a, sig_b, br_a = arena(
            ("conv_hi", [P, CT, SEQ], F32R), ("att_hi", [P, PAIRS, SEQ], F32R), ("mix2", [P, KT, SEQ], F32),
            ("sig_a", [P, SEQ], F32), ("sig_b", [P, SEQ], F32), ("br_a", [P, SEQ], F32))
        A_LN = A_ARENA + 32 * KB
        ln_mean = at("ln_mean", [P, SEQ], A_LN)
        ln_sq = at("ln_sq", [P, CT, SEQ], A_LN + 4 * KB)
        ln_inv = at("ln_inv", [P, SEQ], A_LN + 20 * KB)
        y_tok = at("y_tok", [P, KT, D], A_HI)
        out_gain = at("out_gain", [P, D], A_LO)

        psum = ctx.enter_context(nc.psum_tensor("psum", [P, BANKS, HALF], F32))

        def banks(b, n=2):
            return psum[:, b:b + n, :].rearrange("p b t -> p (b t)")

        def col(name, k=0):
            c = COL[name] + k
            return cols[:, bass.ds(c, 1)] if not isinstance(c, int) else cols[:, c:c + 1]

        x_spill = nc.dram_tensor("x_spill", (P, KT * SEQ), F32, kind="Internal").ap()
        rpb_spill = nc.dram_tensor("rpb_spill", (NA_HEADS * RPB_H, RPB_PAD), F32, kind="Internal").ap()
        bias_rows = nc.dram_tensor("bias_rows", (PAIRS, P, RPB_H, GRID_W), F32, kind="Internal").ap()

        weight_loaded = [sem("weight_loaded_0"), sem("weight_loaded_1")]
        weight_split = sem("weight_split")
        weight_hi = sem("weight_hi")
        tile_done = sem("tile_done")
        sp_passed, pool_passed, dve_passed = (sem(f"{e}_passed") for e in ("sp", "pool", "dve"))
        consts_loaded = sem("consts_loaded")
        x_loaded = [sem(f"x_loaded_{t}") for t in range(KT)]
        rows_loaded = sem("rows_loaded")
        rows_zeroed = sem("rows_zeroed")
        rpb_zeroed = sem("rpb_zeroed")
        rpb_loaded = sem("rpb_loaded")
        rpb_stored = sem("rpb_stored")
        bias_stored = sem("bias_stored")
        memsets = sem("memsets")
        cols_turned = sem("cols_turned")
        cols_ready = sem("cols_ready")
        x_turned = sem("x_turned")
        x_copied = sem("x_copied")
        x_copied_rest = sem("x_copied_rest")
        x_spilled = sem("x_spilled")
        x_back = sem("x_back")
        x_ready = sem("x_ready")
        sq_ready = sem("sq_ready")
        sq_summed = sem("sq_summed")
        norm_summed = sem("norm_summed")
        mean_log = sem("mean_log")
        rinv_ready = sem("rinv_ready")
        block_rinv1 = sem("block_rinv1")
        block_mean = sem("block_mean")
        h_hi_ready = sem("h_hi_ready")
        h_ready = sem("h_ready")
        mix_hi_ready = sem("mix_hi_ready")
        mix_split = sem("mix_split")
        x_added = sem("x_added")
        pool_w_zeroed = sem("pool_w_zeroed")
        pool_loaded = sem("pool_loaded")
        pool_u_ready = sem("pool_u_ready")
        pool_step = sem("pool_step")
        pool_p_ready = sem("pool_p_ready")
        pool_mixed = sem("pool_mixed")
        pool_ready = sem("pool_ready")
        zf_ready, zq_ready, zv_ready, zg_ready = (sem(f"z{n}_ready") for n in "fqvg")
        q_gate = sem("q_gate")
        f_ready = sem("f_ready")
        kd_start = sem("kd_start")
        k_ready = sem("k_ready")
        g_gate = sem("g_gate")
        q_ready = sem("q_ready")
        qd_start = sem("qd_start")
        sg_ready = sem("sg_ready")
        level_ready = sem("level_ready")
        level_done = sem("level_done")
        level_moved = sem("level_moved")
        level_merged = sem("level_merged")
        v_turned = sem("v_turned")
        v_ready = sem("v_ready")
        kd_turned = sem("kd_turned")
        kd_tok_ready = sem("kd_tok_ready")
        update_done = sem("update_done")
        state_ready = sem("state_ready")
        o_done = sem("o_done")
        o_sq = sem("o_sq")
        o_mean = sem("o_mean")
        o_log = sem("o_log")
        o_inv = sem("o_inv")
        o_scaled = sem("o_scaled")
        y_ready = sem("y_ready")
        x_back_last = sem("x_back_last")
        up_read = sem("up_read")
        act_ready = sem("act_ready")
        act_hi_ready = sem("act_hi_ready")
        act_split = sem("act_split")
        down_done = sem("down_done")
        down_added = sem("down_added")
        ffn_read = sem("ffn_read")
        ffn_mid = sem("ffn_mid")
        ffn_left = sem("ffn_left")
        ffn_right = sem("ffn_right")
        ffn_gelu = sem("ffn_gelu")
        cb_read = sem("cb_read")
        cb_ready = sem("cb_ready")
        q_zeroed = sem("q_zeroed")
        u_zeroed = sem("u_zeroed")
        bias_loaded = sem("bias_loaded")
        bias_ready = sem("bias_ready")
        v_read = sem("v_read")
        vt_ready = sem("vt_ready")
        v_tiles_turned = sem("v_tiles_turned")
        v_tiles_ready = sem("v_tiles_ready")
        q_read = sem("q_read")
        q32_ready = sem("q32_ready")
        q_hi_ready = sem("q_hi_ready")
        q_split = sem("q_split")
        k_read = sem("k_read")
        k32_ready = sem("k32_ready")
        k_hi_ready = sem("k_hi_ready")
        k_split = sem("k_split")
        u_read = sem("u_read")
        u_ready = sem("u_ready")
        conv_step = sem("conv_step")
        scores_done = sem("scores_done")
        scores_max = sem("scores_max")
        neg_max_ready = sem("neg_max_ready")
        prob_exp = sem("prob_exp")
        inv_ready = sem("inv_ready")
        prob_ready = sem("prob_ready")
        prob_turned = sem("prob_turned")
        prob_t_ready = sem("prob_t_ready")
        pv_done = sem("pv_done")
        att_ready = sem("att_ready")
        ln_summed = sem("ln_summed")
        ln_mean_ready = sem("ln_mean_ready")
        ln_centred = sem("ln_centred")
        ln_sq_ready = sem("ln_sq_ready")
        ln_var = sem("ln_var")
        ln_log = sem("ln_log")
        ln_inv_ready = sem("ln_inv_ready")
        ln_scaled = sem("ln_scaled")
        ln_silu = sem("ln_silu")
        branch_hi = sem("branch_hi")
        branch_split = sem("branch_split")
        gate_a_read = sem("gate_a_read")
        gate_b_read = sem("gate_b_read")
        gate_a_ready = sem("gate_a_ready")
        gate_b_ready = sem("gate_b_ready")
        branch_a = sem("branch_a")
        branch_b = sem("branch_b")
        merged = sem("merged")
        y_turned = sem("y_turned")
        y_copied = sem("y_copied")
        out_gain_loaded = sem("out_gain_loaded")
        out_inv_ready = sem("out_inv_ready")
        out_ready = sem("out_ready")
        stored = sem("stored")

        block = ctx.enter_context(nc.Block())

        def columns(w, first):
            v = w.rearrange("(k p) n -> p k n", p=P)
            c = slice(first, first + P) if isinstance(first, int) else bass.ds(first, P)
            return [v[:, 0:4, c], v[:, 4:8, c]]

        def rows(w, first, left):
            r = [slice(first + P * k, first + P * k + P) if isinstance(first, int)
                 else bass.ds(first + P * k, P) for k in range(2)]
            return [w[r[k], left:left + HALF] for k in range(2)]

        def branches(first):
            c = slice(first, first + P) if isinstance(first, int) else bass.ds(first, P)
            return [dram[n].rearrange("(k p) n -> p k n", p=P)[:, :, c] for n in ("w_na_out_2", "w_conv_out_2")]

        w_in, w_in2 = dram["w_in"], dram["w_in_2"]

        def head_tiles(h):
            return [columns(w_in, c + h * P) for c in (F1, Q1, I1, G1)]

        def mlp_up(c):
            return [columns(dram["w_up"], c * 2 * P + j * P) for j in range(2)]

        def mlp_down(c):
            return [rows(dram["w_down"], c * 2 * P, j * HALF) for j in range(2)]

        def pair_tiles(p):
            return [columns(w_in2, c + p * P) for c in (CA2, V2, Q2, K2)]

        def merge_tiles(d):
            return [columns(w_in2, GA2 + d * P), columns(w_in2, GB2 + d * P), branches(d * P)]

        def ffn_up(c):
            return [columns(dram["w_up_2"], part + c * 2 * P + j * P) for j in range(2) for part in (0, D_FF2)]

        def ffn_down(c):
            return [rows(dram["w_down_2"], c * 2 * P, j * HALF) for j in range(2)]

        pool_tiles = [columns(w_in, j * P) for j in range(POOL_W // P)]

        def weight_stream(eng, step, begun=False):
            parts = [
                ([] if begun else pool_tiles, 0, None, []),
                (head_tiles(0), HEADS - 1, lambda i: head_tiles(i + 1), []),
                ([], KT // 2, lambda i: [columns(dram["w_out"], i * 2 * P + j * P) for j in range(2)], []),
                (mlp_up(0), MLP_CHUNKS - 1, lambda i: mlp_up(i + 1) + mlp_down(i), mlp_down(MLP_CHUNKS - 1)),
                ([], CT // 2, lambda i: [columns(w_in2, CB2 + i * 2 * P + j * P) for j in range(2)], []),
                ([], PAIRS, pair_tiles, []),
                ([], KT // 2, lambda i: merge_tiles(i * 2) + merge_tiles(i * 2 + 1), []),
                ([], KT // 2, lambda i: [columns(dram["w_out_2"], i * 2 * P + j * P) for j in range(2)], []),
                (ffn_up(0), FFN_CHUNKS - 1, lambda i: ffn_up(i + 1) + ffn_down(i), ffn_down(FFN_CHUNKS - 1)),
            ]
            n = len(pool_tiles) if begun else 0
            for ahead, count, body, behind in parts:
                for halves in ahead:
                    step(n, n % 2, halves)
                    n += 1
                if count:
                    size = len(body(0))
                    assert size % 2 == 0 and n % 2 == 0
                    with eng.Fori(0, count) as i:
                        for j, halves in enumerate(body(i)):
                            step(i * size + (n + j), j % 2, halves)
                    n += count * size
                for halves in behind:
                    step(n, n % 2, halves)
                    n += 1
            assert n == T_END

        @block.sync
        def _(sp):
            def load(n, slot, halves):
                if not isinstance(n, int) or n >= 2:
                    sp.wait_ge(weight_split, n - 1)
                    sp.sem_inc(sp_passed, 1)
                for j, half in enumerate(halves):
                    dst = w_raw[:, slot, j * HALF:(j + 1) * HALF]
                    if len(half.shape) == 3:
                        dst = dst.rearrange("p (k n) -> p k n", n=P)
                    sp.dma_start(dst, half).then_inc(weight_loaded[slot], 16)

            for t in range(KT):
                sp.dma_start(x_in[:, t, :], dram["x"][0, t * P:(t + 1) * P, :]).then_inc(x_loaded[t], 16)
                if t in (2, 4):
                    load(t // 2 - 1, t // 2 - 1, pool_tiles[t // 2 - 1])
            sp.wait_ge(rpb_zeroed, 1)
            left = GRID_W - KW
            sp.dma_start(rpb_pad[0:NA_HEADS * RPB_H, left:left + RPB_W],
                         dram["rpb_2"].rearrange("h r c -> (h r) c")).then_inc(rpb_loaded, 16)

            weight_stream(sp, load, begun=True)

            for t in range(KT):
                sp.wait_ge(out_ready, t + 1)
                sp.dma_start(out[0, t * P:(t + 1) * P, :], y_tok[:, t, :]).then_inc(stored, 16)
            sp.wait_ge(stored, 16 * KT)

        @block.gpsimd
        def _(pool):
            pool.memset(stack_rows[:, :, :], 0.0).then_inc(rows_zeroed, 1)
            pool.memset(rpb_pad[:, :], 0.0).then_inc(rpb_zeroed, 1)
            pool.memset(ones[:, :], 1.0).then_inc(memsets, 1)
            pool.memset(eps1[:, :], EPS1).then_inc(memsets, 1)
            pool.memset(eps2[:, :], EPS2).then_inc(memsets, 1)
            pool.memset(one[:, :], 1.0).then_inc(memsets, 1)

            def split(n, slot, _):
                pool.wait_ge(weight_loaded[slot], arrived(n, slot))
                if not isinstance(n, int) or n >= 2:
                    pool.wait_ge(tile_done, n - 1)
                pool.sem_inc(pool_passed, 1)
                pool.tensor_copy(w_hi[:, slot, :], w_raw[:, slot, :]).then_inc(weight_hi, 1)
                pool.wait_ge(weight_hi, n + 1)
                pool.tensor_tensor(w_lo[:, slot, :], w_raw[:, slot, :], w_hi[:, slot, :].bitcast(F32),
                                   ALU.subtract).then_inc(weight_split, 1)

            def arrived(n, slot):
                return (n - slot) * 16 + 32

            weight_stream(pool, split)

        def row_window(r):
            first = min(max(r - KH // 2, 0), ROWS - KH)
            return first, first - r + KH - 1

        def level_parts(tile, level):
            return tile.rearrange("p (n two s) -> p n two s", two=2, s=1 << level)

        @block.tensor
        def _(pe):
            def product(n, slot, first_bank, hi, lo, part=range(KT), split=None, halves=range(2)):
                pe.wait_ge(weight_split, n + 1)
                for k in part:
                    if split is not None:
                        pe.wait_ge(*split(k))
                    wh = w_hi[:, slot, k * P:(k + 1) * P]
                    wl = w_lo[:, slot, k * P:(k + 1) * P]
                    for j, (w, a) in enumerate(((wh, hi), (wh, lo), (wl, hi))):
                        for t in halves:
                            last = pe.matmul(psum[:, first_bank + t, :], w, a[:, k, t * HALF:(t + 1) * HALF],
                                             start=(k == 0 and j == 0), stop=(k == KT - 1 and j == 2))
                if part[-1] == KT - 1 and halves[-1] == 1:
                    last.then_inc(tile_done, 1)

            def down(n, slot, first_group, hi, lo, after_group=lambda g: None):
                pe.wait_ge(weight_split, n + 1)
                for g in range(8):
                    pe.wait_ge(down_added, first_group + (g + 1))
                    d, t = g // 2, g % 2
                    for k in range(2):
                        at_d = slice(k * HALF + d * P, k * HALF + (d + 1) * P)
                        wh, wl = w_hi[:, slot, at_d], w_lo[:, slot, at_d]
                        for j, (w, a) in enumerate(((wh, hi), (wh, lo), (wl, hi))):
                            last = pe.matmul(psum[:, 4 + g % 4, :], w, a[:, k, t * HALF:(t + 1) * HALF],
                                             start=(k == 0 and j == 0), stop=(k == 1 and j == 2))
                    last.then_inc(down_done if g < 7 else tile_done, 1)
                    after_group(g)

            def sum_features(src, summed, first_bank):
                pe.wait_ge(sq_summed, summed)
                for t in range(2):
                    last = pe.matmul(psum[:, first_bank + t, :], ones[:, :], src[:, t * HALF:(t + 1) * HALF],
                                     start=True, stop=True)
                last.then_inc(norm_summed, 1)

            def normed(first):
                return lambda k: (h_ready, first + k + 1)

            def turn(src, dst_bank, tiles, done):
                for c, block_in in enumerate(tiles):
                    last = pe.transpose(psum[:, dst_bank + c // 4, (c % 4) * P:(c % 4 + 1) * P],
                                        block_in, ident[:, :])
                last.then_inc(done, 1)

            pe.wait_ge(consts_loaded, 16)
            for t in range(KT):
                pe.wait_ge(x_loaded[t], 16)
                if t == 3:
                    pe.wait_ge(rows_loaded, 16 * sum(len(stack) for stack in VECTORS))
                    turn(stack_rows, 7, [stack_rows[:, s, :] for s in range(4)], cols_turned)
                    pe.wait_ge(cols_ready, 1)
                if t >= 4:
                    pe.wait_ge(x_copied, t - 3)
                    pe.wait_ge(x_copied_rest, t - 3)
                for d in range(0, KT, 4):
                    turn(x_in, 2 * (t % 4) + d // 4,
                         [x_in[:, t, (d + c) * P:(d + c + 1) * P] for c in range(4)], x_turned)

            for t in range(2):
                for j in range(2):
                    if t == 0:
                        pe.wait_ge(x_copied, 5 + j)
                        pe.wait_ge(x_copied_rest, 5 + j)
                    product(T_POOL + j, j, 2 * j, h_hi, h_lo, split=normed(H_MIX1 + KT * t), halves=[t])
                    if t == 1 and j == 0:
                        pe.wait_ge(memsets, 4)
                        sum_features(sq_sum, SUMS_MIX1 + 2 * (KT - 1), 4)

            def project_f(h):
                pe.wait_ge(*((pool_u_ready, 1) if isinstance(h, int) and h == 0 else (zv_ready, h)))
                product(h * 4 + T_HEADS, 0, 0, h_hi, h_lo)

            def project_q(h):
                pe.wait_ge(*((pool_u_ready, 2) if isinstance(h, int) and h == 0 else (zg_ready, h)))
                product(h * 4 + (T_HEADS + 1), 1, 2, h_hi, h_lo)

            def project_i(h, part=range(KT)):
                pe.wait_ge(zf_ready, h + 1)
                product(h * 4 + (T_HEADS + 2), 0, 0, h_hi, h_lo, part)

            def project_g(h, part=range(KT)):
                pe.wait_ge(zq_ready, h + 1)
                product(h * 4 + (T_HEADS + 3), 1, 2, h_hi, h_lo, part)

            first_half, second_half = range(KT // 2), range(KT // 2, KT)

            def head(h, meanwhile):
                def level(l, bank):
                    pe.wait_ge(level_ready, h * LEVELS + (l + 1))
                    for c in range(NC):
                        e = e_t[:, l % 2, c * CHUNK:(c + 1) * CHUNK]
                        last = pe.matmul(psum[:, bank, c * (CHUNK // 2):(c + 1) * (CHUNK // 2)], e,
                                         level_parts(e, l)[:, :, 1, :], start=True, stop=True)
                    last.then_inc(level_done, 1)

                def merged_up_to(l):
                    pe.wait_ge(level_merged, h * (LEVELS + 1) + (l + 2))

                meanwhile[0]()
                pe.wait_ge(o_scaled, h + 1)
                pe.wait_ge(k_ready, h + 1)
                pe.wait_ge(q_ready, h + 1)
                for c in range(NC):
                    last = pe.matmul(psum[:, 6 + c // 4, (c % 4) * P:(c % 4 + 1) * P],
                                     k_t[:, c * CHUNK:(c + 1) * CHUNK], q_t[:, c * CHUNK:(c + 1) * CHUNK],
                                     start=True, stop=True)
                last.then_inc(level_done, 1)
                pe.wait_ge(o_log, h + 1)
                level(0, 4)
                level(1, 5)
                meanwhile[1]()
                pe.wait_ge(zv_ready, h + 1)
                merged_up_to(-1)
                turn(zv, 6, [zv[:, c * P:(c + 1) * P] for c in range(NC)], v_turned)
                merged_up_to(0)
                level(2, 4)
                merged_up_to(1)
                level(3, 5)
                meanwhile[2]()
                pe.wait_ge(v_ready, h + 1)
                level(4, 6)
                merged_up_to(2)
                level(5, 4)
                meanwhile[3]()
                merged_up_to(3)
                level(6, 5)
                pe.wait_ge(level_moved, h * LEVELS + LEVELS)
                merged_up_to(4)
                turn(kd_t, 6, [kd_t[:, c * P:(c + 1) * P] for c in range(NC)], kd_turned)
                meanwhile[4]()
                pe.wait_ge(kd_tok_ready, h + 1)
                merged_up_to(6)
                for c in range(NC - 1):
                    last = pe.matmul(psum[:, 4 + c // 4, (c % 4) * P:(c % 4 + 1) * P], kd_tok[:, c, :],
                                     v_tok[:, c, :], start=True, stop=True)
                last.then_inc(update_done, 1)
                meanwhile[5]()
                pe.wait_ge(state_ready, h * (NC - 1) + (NC - 1))
                for c in range(NC):
                    o = psum[:, 6 + c // 4, (c % 4) * P:(c % 4 + 1) * P]
                    tokens = slice(c * CHUNK, (c + 1) * CHUNK)
                    last = pe.matmul(o, v_tok[:, c, :], s_t[:, tokens], start=True, stop=(c == 0))
                    if c >= 1:
                        last = pe.matmul(o, states[:, c, :], qd_t[:, tokens], start=False, stop=True)
                last.then_inc(o_done, 1)
                pe.wait_ge(o_sq, h + 1)
                for t in range(2):
                    last = pe.matmul(psum[:, 4 + t, :], ones[:, :], e_t[:, 1, t * HALF:(t + 1) * HALF],
                                     start=True, stop=True)
                last.then_inc(o_mean, 1)

            def next_head(h):
                return [lambda: project_f(h), lambda: project_q(h),
                        lambda: project_i(h, first_half), lambda: project_i(h, second_half),
                        lambda: project_g(h, first_half), lambda: project_g(h, second_half)]

            project_f(0)
            project_q(0)
            project_i(0)
            project_g(0)
            pe.wait_ge(pool_loaded, 16 * 7)
            for j in range(2):
                pe.wait_ge(pool_p_ready, j + 1)
                for t in range(2):
                    last = pe.matmul(psum[:, 4 + 2 * j + t, :], pool_w[:, j, :],
                                     pool_p[:, j, t * HALF:(t + 1) * HALF], start=True, stop=True)
                last.then_inc(pool_mixed, 1)
            pe.wait_ge(pool_ready, 2)
            with pe.Fori(0, HEADS - 1) as i:
                head(i, next_head(i + 1))

            def out_tile(n, slot, part):
                product(n, slot, 2 * slot, h_hi, h_lo, part, split=lambda k: (mix_split, k + 1))

            def begin_out(slot, part):
                pe.wait_ge(zg_ready if slot else zv_ready, HEADS)
                out_tile(T_OUT1 + slot, slot, part)

            head(HEADS - 1, [lambda: None, lambda: begin_out(0, range(KT - 1)),
                             lambda: begin_out(1, range(KT // 2)), lambda: begin_out(1, range(KT // 2, KT - 1)),
                             lambda: None, lambda: None])
            for s in range(2):
                out_tile(T_OUT1 + s, s, [KT - 1])

            def project_out(count, first_tile, first_added):
                with pe.Fori(0, count) as i:
                    for s in range(2):
                        pe.wait_ge(x_added, i * 2 + (first_added + s + 1))
                        product(i * 2 + (first_tile + s), s, 2 * s, h_hi, h_lo)

            project_out(KT // 2 - 1, T_OUT1 + 2, 2)

            def up_product(n, slot, tile, read, first_bank):
                pe.wait_ge(read, tile + 1)
                product(n, slot, first_bank, h_hi, h_lo)

            def mlp_up_part(c, n):
                for j in range(2):
                    up_product(n + j, j, c * 2 + j, up_read, 2 * j)

            def mlp_down_part(c, n):
                pe.wait_ge(act_split, c * 2 + 4)
                for j in range(2):
                    down(n + j, j, c * 16 + 8 * j, mlp_hi, mlp_lo)

            product(T_MLP, 0, 0, h_hi, h_lo, split=normed(H_MLP))
            sum_features(sq_sum, SUMS_MLP + KT - 1, 4)
            product(T_MLP + 1, 1, 2, h_hi, h_lo)
            with pe.Fori(0, MLP_CHUNKS - 1) as i:
                mlp_up_part(i + 1, i * 4 + (T_MLP + 2))
                mlp_down_part(i, i * 4 + (T_MLP + 4))
            mlp_down_part(MLP_CHUNKS - 1, T_CB - 2)

            product(T_CB, 0, 0, h_hi, h_lo, split=normed(H_MIX2))
            product(T_CB + 1, 1, 2, h_hi, h_lo, range(KT // 2))
            sum_features(sq_sum, SUMS_MIX2 + 2 * KT - 1, 4)
            sum_features(sq_sum_gain, SUMS_MIX2 + 2 * KT - 1, 6)
            product(T_CB + 1, 1, 2, h_hi, h_lo, range(KT // 2, KT))
            for c in range(2, CT):
                pe.wait_ge(cb_read, c - 1)
                product(T_CB + c, c % 2, 2 * (c % 2), h_hi, h_lo)

            def scores(p, s):
                first, _ = row_window(s)
                pe.wait_ge(scores_max, p * ROWS + (s + 1))
                k = slice(first * GRID_W, first * GRID_W + WIN)
                for j, (q, kk) in enumerate(((q_hi, k_hi), (q_hi, k_lo), (q_lo, k_hi))):
                    last = pe.matmul(psum[:, 4 + s % 2, :], q[:, s, :], kk[:, k], start=(j == 0), stop=(j == 2))
                last.then_inc(scores_done, 1)

            def turn_probabilities(p, s):
                pe.wait_ge(prob_ready, p * ROWS + (s + 1))
                pe.wait_ge(prob_t_ready, p * ROWS + (s + 1))
                turn(prob, 6 + s % 2, [prob[:, s % 3, c * P:(c + 1) * P] for c in range(4)], prob_turned)

            def weigh_values(p, s):
                first, _ = row_window(s)
                pe.wait_ge(prob_t_ready, p * ROWS + (s + 3))
                pe.wait_ge(att_ready, p * 4 + (s // 4 + 3))
                v = v_odd if first % 2 else v_even
                for c in range(4):
                    last = pe.matmul(psum[:, (s // 4) % 2, (s % 4) * P:(s % 4 + 1) * P], v[:, first // 2 + c, :],
                                     prob_t[:, s % 2, c * P:(c + 1) * P], start=(c == 0), stop=(c == 3))
                if s % 4 == 3:
                    last.then_inc(pv_done, 1)

            pe.wait_ge(cb_read, CT)
            with pe.Fori(0, PAIRS) as p:
                pe.wait_ge(att_ready, p * 4 + 4)
                product(p * 4 + T_PAIRS, 0, 0, h_hi, h_lo)
                pe.wait_ge(k_read, p + 1)
                product(p * 4 + (T_PAIRS + 1), 1, 2, h_hi, h_lo)
                pe.wait_ge(u_read, p + 1)
                product(p * 4 + (T_PAIRS + 2), 0, 0, h_hi, h_lo)
                pe.wait_ge(vt_ready, p + 1)
                pe.wait_ge(scores_max, p * ROWS + 2)
                turn(v_t, 4, [v_t[:, c * P:(c + 1) * P] for c in range(8)], v_tiles_turned)
                pe.wait_ge(prob_t_ready, p * ROWS + 2)
                turn(v_t, 6, [v_t[:, c * P + GRID_W:(c + 1) * P + GRID_W] for c in range(7)], v_tiles_turned)
                product(p * 4 + (T_PAIRS + 3), 1, 2, h_hi, h_lo)
                pe.wait_ge(q_split, p + 1)
                pe.wait_ge(k_split, p + 1)
                pe.wait_ge(v_tiles_ready, p * 2 + 2)
                for s in range(ROWS + 3):
                    if s < ROWS:
                        scores(p, s)
                    if 2 <= s < ROWS + 2:
                        turn_probabilities(p, s - 2)
                    if s >= 3:
                        weigh_values(p, s - 3)

            pe.wait_ge(conv_step, CONV_K * CT)
            for t in range(2):
                for c in range(CT):
                    last = pe.matmul(psum[:, 4 + t, :], ones[:, :], conv_t[:, c, t * HALF:(t + 1) * HALF],
                                     start=(c == 0), stop=(c == CT - 1))
            last.then_inc(ln_summed, 1)
            pe.wait_ge(ln_sq_ready, CT)
            for t in range(2):
                for c in range(CT):
                    last = pe.matmul(psum[:, 6 + t, :], ones[:, :], ln_sq[:, c, t * HALF:(t + 1) * HALF],
                                     start=(c == 0), stop=(c == CT - 1))
            last.then_inc(ln_var, 1)

            pe.wait_ge(att_ready, 4 + 4 * PAIRS)
            with pe.Fori(0, KT // 2) as i:
                for s in range(2):
                    n = i * 6 + (T_MERGE + 3 * s)
                    d1 = i * 2 + (s + 1)
                    pe.wait_ge(gate_a_read, d1)
                    product(n, s % 2, 0, h_hi, h_lo)
                    pe.wait_ge(gate_b_read, d1)
                    product(n + 1, (s + 1) % 2, 2, h_hi, h_lo)
                    pe.wait_ge(branch_split, PAIRS + CT)
                    pe.wait_ge(weight_split, n + 3)
                    for branch, read, bank, hi, lo in ((0, branch_a, 4, att_hi, att_lo),
                                                       (1, branch_b, 6, conv_hi, conv_lo)):
                        pe.wait_ge(read, d1)
                        for k in range(4):
                            at_k = slice((4 * branch + k) * P, (4 * branch + k + 1) * P)
                            wh, wl = w_hi[:, s % 2, at_k], w_lo[:, s % 2, at_k]
                            for j, (w, a) in enumerate(((wh, hi), (wh, lo), (wl, hi))):
                                for t in range(2):
                                    last = pe.matmul(psum[:, bank + t, :], w, a[:, k, t * HALF:(t + 1) * HALF],
                                                     start=(k == 0 and j == 0), stop=(k == 3 and j == 2))
                    last.then_inc(tile_done, 1)

            pe.wait_ge(mix_split, 2 * KT)
            project_out(KT // 2, T_OUT2, KT)

            def ffn_up_part(c, n):
                for j in range(4):
                    up_product(n + j, j % 2, c * 4 + j, ffn_read, 2 * (j % 2))

            def ffn_down_part(c, n, after_group=lambda j, g: None):
                pe.wait_ge(act_split, c * 2 + (2 * MLP_CHUNKS + 4))
                for j in range(2):
                    down(n + j, j, c * 16 + (16 * MLP_CHUNKS + 8 * j), ffn_hi, ffn_lo,
                         lambda g: after_group(j, g))

            product(T_FFN, 0, 0, h_hi, h_lo, split=normed(H_FFN))
            sum_features(sq_sum, SUMS_FFN + KT - 1, 4)
            product(T_FFN + 1, 1, 2, h_hi, h_lo)
            for j in range(2, 4):
                up_product(T_FFN + j, j % 2, j, ffn_read, 2 * (j % 2))
            with pe.Fori(0, FFN_CHUNKS - 1) as i:
                ffn_up_part(i + 1, i * 6 + (T_FFN + 4))
                ffn_down_part(i, i * 6 + (T_FFN + 8))

            def turn_back(d):
                pe.wait_ge(down_added, 4 + 16 * (MLP_CHUNKS + FFN_CHUNKS - 1) + 2 * (d + 1))
                if d >= 2:
                    pe.wait_ge(y_copied, d - 1)
                turn(x_t, 2 * (d % 2), [x_t[:, d, t * P:(t + 1) * P] for t in range(KT)], y_turned)

            def after_group(j, g):
                group = 8 * j + g
                if group >= 4 and group % 2 == 0:
                    turn_back(group // 2 - 2)

            ffn_down_part(FFN_CHUNKS - 1, T_END - 2, after_group)
            turn_back(KT - 2)
            turn_back(KT - 1)
            pe.wait_ge(sq_summed, SUMS_OUT + KT - 1)
            for t in range(KT):
                last = pe.matmul(psum[:, 4, t:t + 1], sq_sum[:, t * P:(t + 1) * P], ones[:, 0:1], start=True, stop=True)
            last.then_inc(norm_summed, 1)

        @block.scalar
        def _(act):
            def square(d, first_sum, part=slice(0, SEQ)):
                if d >= 3:
                    act.wait_ge(sq_summed, first_sum)
                dst = sq[:, d % 2, part] if d else sq_sum[:, part]
                act.activation(dst, x_t[:, d, part], ACT.Square).then_inc(sq_ready, 1)

            def inverse(m, norm, eps):
                act.wait_ge(norm_summed, norm)
                act.activation(rinv[:, :], banks(4), ACT.Ln, scale=1.0 / D, bias=eps[:, :]).then_inc(mean_log, 1)
                act.wait_ge(mean_log, m + 1)
                act.activation(rinv[:, :], rinv[:, :], ACT.Exp, scale=-0.5).then_inc(rinv_ready, 1)

            def hi_part(d, gain, part=slice(0, SEQ)):
                act.activation(h_hi[:, d, part], x_t[:, d, part], ACT.Copy, scale=gain).then_inc(h_hi_ready, 1)

            act.dma_start(ident[:, :], dram["c_ident"]).then_inc(consts_loaded, 16)
            act.wait_ge(rows_zeroed, 1)
            for s, stack in enumerate(VECTORS):
                r = 0
                for name, n in stack:
                    if "/" in name:
                        name, tap = name.split("/")
                        src = dram[name][int(tap), :].rearrange("(n c) -> n c", c=P)
                    elif name == "conv_dw_w_2":
                        src = dram[name].rearrange("k (n c) -> (k n) c", c=P)
                    else:
                        src = dram[name].rearrange("(n c) -> n c", c=P)
                    act.dma_start(stack_rows[r:r + n, s, :], src).then_inc(rows_loaded, 16)
                    r += n

            for half in range(2):
                part = slice(half * HALF, (half + 1) * HALF)
                for t in range(4 * half, 4 * half + 4):
                    act.wait_ge(x_turned, 2 * t + 1)
                    act.activation(x_t[:, 0:4, t * P:(t + 1) * P],
                                   psum[:, 2 * (t % 4), :].rearrange("p (d t) -> p d t", t=P),
                                   ACT.Copy).then_inc(x_copied, 1)
                    if t == 2:
                        act.wait_ge(cols_turned, 1)
                        act.activation(cols[:, :], psum[:, 7, :], ACT.Copy).then_inc(cols_ready, 1)
                        act.wait_ge(cols_ready, 1)
                if half == 1:
                    for d in range(KT):
                        square(d, SUMS_MIX1 + d - 2, slice(0, HALF))
                act.wait_ge(x_copied, 4 * half + 4)
                act.wait_ge(x_copied_rest, 4 * half + 4)
                for d in range(KT):
                    hi_part(d, col("norm_mix_g", d), part)
            for d in range(KT):
                square(d, SUMS_MIX1 + KT - 1 + d - 2, slice(HALF, SEQ))
            act.wait_ge(rpb_loaded, 16)
            act.dma_start(rpb_spill, rpb_pad[0:NA_HEADS * RPB_H, :]).then_inc(rpb_stored, 16)
            inverse(0, 1, eps1)
            act.wait_ge(rpb_stored, 16)
            act.wait_ge(pool_w_zeroed, 1)
            for g in range(4):
                half = slice(64 * (g % 2), 64 * (g % 2) + 64)
                act.dma_start(pool_w[half, g // 2, half], dram["pool_w"][g, :, :]).then_inc(pool_loaded, 16)
            act.dma_start(col_mask[:, :], dram["c_col_mask"]).then_inc(pool_loaded, 16)
            act.dma_start(pool_inv[:, :, :], dram["c_pool_inv"]).then_inc(pool_loaded, 16)
            act.dma_start(pair_mask[:, :], dram["c_pair_mask"]).then_inc(pool_loaded, 16)

            act.dma_start(x_spill, x_t[:, :, :].rearrange("p d t -> p (d t)")).then_inc(x_spilled, 16)
            for h in range(NA_HEADS):
                diagonals = bass.AP(rpb_spill.tensor, h * RPB_H * RPB_PAD + GRID_W - 1,
                                    [[RPB_PAD, RPB_H], [-1, GRID_W], [1, GRID_W]])
                to = bias_rows[h // 2, DH * (h % 2):DH * (h % 2) + GRID_W, :, :].rearrange("q r c -> r q c")
                act.dma_start(to, diagonals).then_inc(bias_stored, 16)

            act.wait_ge(x_spilled, 16)
            for j in range(2):
                act.wait_ge(pool_mixed, j + 1)
                act.activation(mix1[:, j, :], banks(4 + 2 * j), ACT.Copy,
                               scale=col("pool_scale", j)).then_inc(pool_ready, 1)

            def mix_hi(d, mix, ready):
                act.wait_ge(*ready)
                act.activation(h_hi[:, d, :], mix[:, d, :], ACT.Copy).then_inc(mix_hi_ready, 1)

            def mix1_hi(d):
                mix_hi(d, mix1, (pool_ready, d + 1) if d < 2 else (y_ready, d))

            def head(h, last):
                def level(l):
                    if l == 0:
                        act.wait_ge(qd_start, h + 1)
                    else:
                        act.wait_ge(level_moved, h * LEVELS + l)
                    if l >= 2:
                        act.wait_ge(level_done, h * (LEVELS + 1) + l)
                    e = level_parts(e_t[:, l % 2, :], l)
                    act.activation(e[:, :, 0, :], level_parts(kd_t[:, :], l)[:, :, 0, :], ACT.Copy)
                    act.activation(e[:, :, 1, :], level_parts(qd_t[:, :], l)[:, :, 1, :], ACT.Copy)\
                       .then_inc(level_ready, 1)

                act.wait_ge(zq_ready, h + 1)
                act.activation(q_t[:, :], zq[:, :], ACT.Sigmoid).then_inc(q_gate, 1)
                act.wait_ge(zf_ready, h + 1)
                act.activation(decays[:, 0:SEQ], zf[:, :], ACT.Sigmoid).then_inc(f_ready, 1)
                act.activation(kd_t[:, :], zf[:, :], ACT.Sigmoid, scale=-1.0).then_inc(kd_start, 1)
                act.activation(k_t[:, :], zf[:, :], ACT.Sigmoid, scale=-1.0).then_inc(k_ready, 1)
                act.wait_ge(y_ready, h + 1)
                act.wait_ge(zg_ready, h + 1)
                act.activation(sg_t[:, :], zg[:, :], ACT.Sigmoid).then_inc(g_gate, 1)
                act.wait_ge(kd_start, h + 1)
                level(0)
                level(1)
                level(2)
                if last:
                    act.wait_ge(tile_done, T_OUT1)
                    for d in range(KT - 1):
                        mix1_hi(d)
                level(3)
                act.wait_ge(v_turned, h + 1)
                act.activation(v_tok[:, :, :].rearrange("p c v -> p (c v)"), banks(6), ACT.Copy).then_inc(v_ready, 1)
                if last:
                    act.wait_ge(mix_split, KT - 1)
                    act.dma_start(x_t[:, 0:KT - 1, :].rearrange("p d t -> p (d t)"),
                                  x_spill[:, 0:(KT - 1) * SEQ]).then_inc(x_back, 16)
                level(4)
                level(5)
                level(6)
                act.wait_ge(kd_turned, h + 1)
                act.activation(kd_tok[:, :, :].rearrange("p c k -> p (c k)"), banks(6), ACT.Copy)\
                   .then_inc(kd_tok_ready, 1)
                act.wait_ge(o_done, h + 1)
                act.activation(e_t[:, 1, :], banks(6), ACT.Square).then_inc(o_sq, 1)
                act.wait_ge(o_mean, h + 1)
                act.activation(e_t[:, 0, :], banks(4), ACT.Ln, scale=1.0 / P, bias=eps1[:, :]).then_inc(o_log, 1)
                act.wait_ge(o_log, h + 2)
                act.activation(e_t[:, 0, :], e_t[:, 0, :], ACT.Exp, scale=-0.5).then_inc(o_inv, 1)

            with act.Fori(0, HEADS - 1) as i:
                head(i, False)
            head(HEADS - 1, True)
            mix1_hi(KT - 1)
            act.wait_ge(mix_split, KT)
            act.dma_start(x_t[:, KT - 1, :], x_spill[:, (KT - 1) * SEQ:]).then_inc(x_back_last, 16)

            def split_activations(a, hi, first, after):
                if after is not None:
                    act.wait_ge(tile_done, after)
                for j in range(2):
                    act.wait_ge(act_ready, first + (j + 1))
                    act.activation(hi[:, j, :], a[:, j, :], ACT.Copy).then_inc(act_hi_ready, 1)

            def mlp_square(c):
                for j in range(2):
                    act.wait_ge(up_read, c * 2 + (2 + j + 1))
                    act.activation(mlp_a[:, j, :], mlp_a[:, j, :], ACT.Square).then_inc(act_ready, 1)

            def next_norm(m, norm, first_added, first_sum, last_use, gain, eps):
                for d in range(KT):
                    if d == KT - 1:
                        act.wait_ge(tile_done, last_use)
                        hi_part(0, col(gain, 0))
                    act.wait_ge(x_added, first_added + d + 1)
                    square(d, first_sum + d - 2)
                for d in range(1, KT):
                    hi_part(d, col(gain, d))
                inverse(m, norm, eps)

            next_norm(1, 2, 2, SUMS_MLP, T_MLP, "norm_mlp_g", eps1)
            mlp_square(0)
            split_activations(mlp_a, mlp_hi, 0, None)
            with act.Fori(0, MLP_CHUNKS - 1) as i:
                mlp_square(i + 1)
                split_activations(mlp_a, mlp_hi, i * 2 + 2, i * 4 + (T_MLP + 6))

            def down_x(d):
                act.wait_ge(down_added, 4 + 16 * (MLP_CHUNKS - 1) + 2 * (d + 1))

            act.wait_ge(tile_done, T_CB - 2)
            for d in range(4):
                down_x(d)
                hi_part(d, gain_both[:, d:d + 1])
                square(d, SUMS_MIX2 + 2 * d - 3)
            for d in range(4, KT):
                down_x(d)
                hi_part(d, gain_both[:, d:d + 1])
            for d in range(4, KT):
                square(d, SUMS_MIX2 + 2 * d - 3)
            act.wait_ge(norm_summed, 3)
            act.activation(rinv1[:, :], banks(4), ACT.Ln, scale=1.0 / D, bias=eps1[:, :]).then_inc(mean_log, 1)
            act.wait_ge(mean_log, 3)
            act.activation(sq[:, 0, :], rinv1[:, :], ACT.Exp, scale=-1.0)
            act.activation(rinv1[:, :], rinv1[:, :], ACT.Exp, scale=-0.5).then_inc(block_rinv1, 1)
            act.wait_ge(block_mean, 1)
            act.activation(sq[:, 0, :], sq[:, 0, :], ACT.Ln, scale=1.0 / D, bias=eps2[:, :]).then_inc(mean_log, 1)
            act.wait_ge(mean_log, 4)
            act.activation(sq[:, 1, :], sq[:, 0, :], ACT.Exp, scale=-0.5).then_inc(rinv_ready, 1)

            for c in range(CT):
                act.wait_ge(cb_read, c + 1)
                act.activation(sig_cb[:, c, :], sig_cb[:, c, :], ACT.Sigmoid, bias=col("b_in_2", CB2 // P + c))\
                   .then_inc(cb_ready, 1)
            act.wait_ge(x_ready, KT)
            act.dma_start(x_spill, x_t[:, :, :].rearrange("p d t -> p (d t)")).then_inc(x_spilled, 16)

            act.wait_ge(x_spilled, 32)
            act.wait_ge(bias_stored, 16 * NA_HEADS)
            with act.Fori(0, PAIRS) as p:
                act.wait_ge(scores_max, p * ROWS + 2)
                act.dma_start(bias[:, :, :], bias_rows[bass.ds(p, 1), :, :, :].rearrange("a q r c -> (a q) r c"))\
                   .then_inc(bias_loaded, 16)
                act.wait_ge(v_read, p + 1)
                act.activation(v_t[:, :], v_t[:, :], ACT.Identity, bias=col("b_in_2", p + V2 // P)).then_inc(vt_ready, 1)
                act.wait_ge(q_read, p + 1)
                act.activation(q32[:, :], q32[:, :], ACT.Identity, scale=DH ** -0.5, bias=q_bias[:, bass.ds(p, 1)])\
                   .then_inc(q32_ready, 1)
                act.wait_ge(q32_ready, p + 1)
                for j in range(2):
                    half = slice(DH * j, DH * (j + 1))
                    last = act.activation(q_hi[half, :, half], q32[half, :].rearrange("p (r c) -> p r c", c=GRID_W),
                                          ACT.Copy)
                last.then_inc(q_hi_ready, 1)
                act.wait_ge(v_tiles_turned, p * 2 + 1)
                act.activation(v_even[:, :, :].rearrange("p c v -> p (c v)"), banks(4), ACT.Copy)\
                   .then_inc(v_tiles_ready, 1)
                act.wait_ge(v_tiles_turned, p * 2 + 2)
                act.activation(v_odd[:, 0:7, :].rearrange("p c v -> p (c v)"), banks(6)[:, 0:7 * P], ACT.Copy)\
                   .then_inc(v_tiles_ready, 1)
                act.wait_ge(k_read, p + 2)
                act.activation(k32[:, :], k32[:, :], ACT.Identity, bias=col("b_in_2", p + K2 // P)).then_inc(k32_ready, 1)
                act.wait_ge(k32_ready, p + 1)
                act.activation(k_hi[:, :], k32[:, :], ACT.Copy).then_inc(k_hi_ready, 1)
                for s in range(ROWS + 4):
                    if s < ROWS:
                        act.wait_ge(neg_max_ready, p * ROWS + (s + 1))
                        act.activation(prob[:, s % 3, :], prob[:, s % 3, :], ACT.Exp, bias=neg_max[:, s % 2:s % 2 + 1],
                                       accum_out=row_sum[:, s % 2:s % 2 + 1]).then_inc(prob_exp, 1)
                    if 2 <= s < ROWS + 2:
                        u = s - 2
                        act.wait_ge(prob_turned, p * ROWS + (u + 1))
                        act.activation(prob_t[:, u % 2, :], psum[:, 6 + u % 2, :], ACT.Copy).then_inc(prob_t_ready, 1)
                    if s >= 4 and s % 4 == 3:
                        pass
                    if s >= 4 and (s - 4) % 4 == 3:
                        g = (s - 4) // 4
                        act.wait_ge(pv_done, p * 4 + (g + 1))
                        for j in range(2):
                            half = slice(DH * j, DH * (j + 1))
                            dst = att_t[half, bass.ds(p, 1), 4 * g * GRID_W:4 * (g + 1) * GRID_W]
                            last = act.activation(
                                dst.rearrange("p a (r c) -> p (a r) c", c=GRID_W),
                                psum[half, g % 2, :].rearrange("p (r c) -> p r c", c=P)[:, :, half], ACT.Copy)
                        last.then_inc(att_ready, 1)

            act.wait_ge(att_ready, 4 + 4 * PAIRS)
            act.wait_ge(scores_done, ROWS * PAIRS)
            for c in range(PAIRS):
                act.activation(att_hi[:, c, :], att_t[:, c, :], ACT.Copy).then_inc(branch_hi, 1)
            act.wait_ge(ln_summed, 1)
            act.activation(ln_mean[:, :], banks(4), ACT.Copy, scale=1.0 / CONV_CH).then_inc(ln_mean_ready, 1)
            for c in range(CT):
                act.wait_ge(ln_centred, c + 1)
                act.activation(ln_sq[:, c, :], conv_t[:, c, :], ACT.Square).then_inc(ln_sq_ready, 1)
            act.wait_ge(ln_var, 1)
            act.activation(ln_inv[:, :], banks(6), ACT.Ln, scale=1.0 / CONV_CH, bias=eps2[:, :]).then_inc(ln_log, 1)
            act.wait_ge(ln_log, 1)
            act.activation(ln_inv[:, :], ln_inv[:, :], ACT.Exp, scale=-0.5).then_inc(ln_inv_ready, 1)
            for c in range(CT):
                act.wait_ge(ln_scaled, c + 1)
                act.activation(conv_t[:, c, :], conv_t[:, c, :], ACT.Silu, scale=col("conv_ln_g_2", c),
                               bias=col("conv_ln_b_2", c)).then_inc(ln_silu, 1)
                act.wait_ge(ln_silu, c + 1)
                act.activation(conv_hi[:, c, :], conv_t[:, c, :], ACT.Copy).then_inc(branch_hi, 1)

            with act.Fori(0, KT // 2) as i:
                for s in range(2):
                    d1 = i * 2 + (s + 1)
                    act.wait_ge(gate_a_read, d1 + 1)
                    act.activation(sig_a[:, :], sig_a[:, :], ACT.Sigmoid, bias=col("b_in_2", i * 2 + (GA2 // P + s)))\
                       .then_inc(gate_a_ready, 1)
                    act.wait_ge(gate_b_read, d1 + 1)
                    act.activation(sig_b[:, :], sig_b[:, :], ACT.Sigmoid, bias=col("b_in_2", i * 2 + (GB2 // P + s)))\
                       .then_inc(gate_b_ready, 1)

            act.wait_ge(tile_done, T_OUT2)
            act.dma_start(x_t[:, :, :].rearrange("p d t -> p (d t)"), x_spill).then_inc(x_back, 16)
            for d in range(KT):
                mix_hi(d, mix2, (merged, d + 2))

            def ffn_middle(c):
                for j in range(2):
                    for part, buf in enumerate((ffn_gate, ffn_val)):
                        act.wait_ge(ffn_read, c * 4 + (2 + 2 * j + part + 1))
                        act.wait_ge(act_ready, c * 2 + (2 * MLP_CHUNKS + j))
                        k = c * 2 + (part * FT2 + j)
                        act.activation(buf[:, :], ffn_z[:, part, :], ACT.Identity, scale=col("ffn_dw_w_2/1", k),
                                       bias=col("ffn_dw_b_2", k)).then_inc(ffn_mid, 1)
                        if part == 0:
                            act.wait_ge(ffn_right, c * 4 + (2 * j + 1))
                            act.activation(ffn_gate[:, :], ffn_gate[:, :], ACT.Gelu).then_inc(ffn_gelu, 1)

            next_norm(4, 5, 2 + KT, SUMS_FFN, T_FFN, "norm2_g_2", eps2)
            ffn_middle(0)
            split_activations(ffn_a, ffn_hi, 2 * MLP_CHUNKS, None)
            with act.Fori(0, FFN_CHUNKS - 1) as i:
                ffn_middle(i + 1)
                split_activations(ffn_a, ffn_hi, i * 2 + (2 * MLP_CHUNKS + 2), i * 6 + (T_FFN + 10))

            act.wait_ge(tile_done, T_END - 2)
            act.dma_start(out_gain[:, :], bass.AP(dram["norm_f_g_2"].tensor, 0, [[0, P], [1, D]]))\
               .then_inc(out_gain_loaded, 16)

            def take_back(d):
                act.wait_ge(y_turned, d + 1)
                act.activation(y_tok[:, :, d * P:(d + 1) * P], banks(2 * (d % 2)).rearrange("p (t f) -> p t f", f=P),
                               ACT.Copy).then_inc(y_copied, 1)

            for d in range(KT):
                act.wait_ge(down_added, 4 + 16 * (MLP_CHUNKS + FFN_CHUNKS - 1) + 2 * (d + 1))
                square(d, SUMS_OUT + d - 2)
                if d >= 2:
                    take_back(d - 2)
            take_back(KT - 2)
            take_back(KT - 1)
            act.wait_ge(norm_summed, 6)
            act.activation(out_inv[:, :], psum[:, 4, 0:KT], ACT.Ln, scale=1.0 / D, bias=eps2[:, :]).then_inc(mean_log, 1)
            act.wait_ge(mean_log, 6)
            act.activation(out_inv[:, :], out_inv[:, :], ACT.Exp, scale=-0.5).then_inc(out_inv_ready, 1)

        @block.vector
        def _(dve):
            dve.sem_inc(down_added, 4)
            dve.sem_inc(x_added, 2)
            dve.sem_inc(o_log, 1)
            dve.sem_inc(o_scaled, 1)
            dve.sem_inc(y_ready, 1)
            dve.sem_inc(up_read, 2)
            dve.sem_inc(act_split, 2)
            dve.sem_inc(att_ready, 4)
            dve.sem_inc(k_read, 1)
            dve.sem_inc(scores_max, 2)
            dve.sem_inc(prob_t_ready, 2)
            for free in (gate_a_read, gate_b_read, branch_a, branch_b, merged):
                dve.sem_inc(free, 1)
            dve.sem_inc(ffn_read, 2)

            def add_square(d, first_sum, first_ready, part=slice(0, SEQ)):
                dve.wait_ge(sq_ready, first_ready + d + 1)
                if d >= 2:
                    dve.wait_ge(sq_summed, first_sum + d - 1)
                dve.tensor_tensor(sq_sum[:, part], sq_sum[:, part], sq[:, d % 2, part], ALU.add).then_inc(sq_summed, 1)

            def lo_part(d, gain, first, part=slice(0, SEQ)):
                dve.wait_ge(h_hi_ready, first + d + 1)
                dve.scalar_tensor_tensor(h_lo[:, d, part], x_t[:, d, part], gain, h_hi[:, d, part].bitcast(F32),
                                         ALU.mult, ALU.subtract).then_inc(h_ready, 1)

            for half in range(2):
                part = slice(half * HALF, (half + 1) * HALF)
                for t in range(4 * half, 4 * half + 4):
                    dve.wait_ge(x_turned, 2 * t + 2)
                    dve.tensor_copy(x_t[:, 4:8, t * P:(t + 1) * P],
                                    psum[:, 2 * (t % 4) + 1, :].rearrange("p (d t) -> p d t", t=P))\
                       .then_inc(x_copied_rest, 1)
                if half == 0:
                    dve.wait_ge(cols_ready, 1)
                else:
                    for d in range(1, KT):
                        add_square(d, SUMS_MIX1, 0, slice(0, HALF))
                dve.wait_ge(x_copied_rest, 4 * half + 4)
                for d in range(KT):
                    lo_part(d, col("norm_mix_g", d), H_MIX1 + KT * half, part)
            for d in range(1, KT):
                add_square(d, SUMS_MIX1 + KT - 1, KT, slice(HALF, SEQ))
            both, g1, b = COL["final_norm_g"], COL["norm1_g_2"], COL["b_in_2"] + Q2 // P
            dve.tensor_tensor(gain_both[:, :], cols[:, both:both + KT], cols[:, g1:g1 + KT], ALU.mult)
            dve.tensor_tensor(gain_sq[:, :], cols[:, both:both + KT], cols[:, both:both + KT], ALU.mult)
            dve.tensor_scalar(q_bias[:, 0:PAIRS], cols[:, b:b + PAIRS], DH ** -0.5, None, ALU.mult)

            dve.wait_ge(rinv_ready, 1)
            dve.memset(pool_w[:, :, :], 0.0).then_inc(pool_w_zeroed, 1)
            dve.memset(pool_u[:, :, 0:POOL_PAD], 0.0)
            dve.memset(pool_a[:, 0:POOL_PAD], 0.0)
            dve.memset(pool_b[:, 0:POOL_PAD], 0.0).then_inc(pool_step, 1)
            steps = 1
            for j in range(2):
                dve.wait_ge(tile_done, T_POOL + j + 1)
                dve.tensor_tensor(pool_u[:, j, POOL_PAD:], banks(2 * j), rinv[:, :], ALU.mult).then_inc(pool_u_ready, 1)
            dve.wait_ge(pool_loaded, 16 * 7)
            for j in range(2):
                dve.wait_ge(pool_u_ready, j + 1)
                src, sums, shift = pool_u[:, j, :], [], 1
                spare = [pool_a, pool_b]
                for n in range(2 * j + 2):
                    dst = spare[n % 2][:, :]
                    dve.wait_ge(pool_step, steps)
                    dve.tensor_tensor(dst[:, POOL_PAD:], src[:, POOL_PAD:], src[:, POOL_PAD - shift:PADDED - shift],
                                      ALU.add).then_inc(pool_step, 1)
                    steps += 1
                    sums.append(dst)
                    src, shift = dst, 2 * shift
                dve.wait_ge(pool_step, steps)
                for half, window_sum in ((slice(0, 64), sums[-2]), (slice(64, P), sums[-1])):
                    dve.tensor_tensor(pool_p[half, j, :], window_sum[half, POOL_PAD:], pool_inv[half, j, :],
                                      ALU.mult).then_inc(pool_step, 1)
                    steps += 1
                dve.wait_ge(pool_step, steps)
                dve.tensor_tensor(pool_p[:, j, :], pool_p[:, j, :], pool_u[:, j, POOL_PAD:], ALU.subtract)\
                   .then_inc(pool_p_ready, 1)

            def take(z, n, bank, ready):
                dve.wait_ge(tile_done, n + 1)
                dve.tensor_tensor(z[:, :], banks(bank), rinv[:, :], ALU.mult).then_inc(ready, 1)

            def take_f(h):
                take(zf, h * 4 + T_HEADS, 0, zf_ready)

            def take_q(h):
                take(zq, h * 4 + (T_HEADS + 1), 2, zq_ready)

            def take_i(h):
                take(zv, h * 4 + (T_HEADS + 2), 0, zv_ready)

            def take_g(h):
                take(zg, h * 4 + (T_HEADS + 3), 2, zg_ready)

            for take_z in (take_f, take_q, take_i, take_g):
                take_z(0)
            dve.wait_ge(x_spilled, 16)
            dve.wait_ge(pool_ready, 2)
            dve.memset(s_t[:, :], 0.0).then_inc(pool_step, 1)
            steps += 1
            dve.wait_ge(pool_step, steps)

            def mix_lo(m, d, mix):
                dve.wait_ge(mix_hi_ready, KT * m + d + 1)
                dve.tensor_tensor(h_lo[:, d, :], mix[:, d, :], h_hi[:, d, :].bitcast(F32),
                                  ALU.subtract).then_inc(mix_split, 1)

            def head(h, last):
                def decay_of(l):
                    first = 2 * SEQ - (2 * SEQ >> l)
                    return decays[:, first:first + (SEQ >> l)].rearrange("p (n two) -> p n two", two=2)

                def move(l):
                    n, s = SEQ >> (l + 1), 1 << l
                    decay, twice = decay_of(l), 2 * SEQ - (2 * SEQ >> (l + 1))
                    q, k = level_parts(qd_t[:, :], l)[:, :, 1, :], level_parts(kd_t[:, :], l)[:, :, 0, :]
                    dve.wait_ge(level_ready, h * LEVELS + (l + 1))
                    dve.tensor_tensor(q, q, decay[:, :, 0:1].to_broadcast([P, n, s]), ALU.mult)
                    dve.tensor_tensor(k, k, decay[:, :, 1:2].to_broadcast([P, n, s]), ALU.mult)
                    dve.tensor_tensor(decays[:, twice:twice + n], decay[:, :, 0], decay[:, :, 1], ALU.mult)\
                       .then_inc(level_moved, 1)

                def merge_diagonal():
                    dve.wait_ge(level_done, h * (LEVELS + 1) + 1)
                    dve.sem_inc(dve_passed, 1)
                    mask = pair_mask[:, LEVELS * CHUNK // 2:].bitcast(U32).unsqueeze(1).to_broadcast([P, NC, CHUNK])
                    dve.copy_predicated(s_t[:, :].rearrange("p (c t) -> p c t", t=CHUNK), mask,
                                        banks(6).rearrange("p (c t) -> p c t", t=CHUNK)).then_inc(level_merged, 1)

                def merge(l, bank):
                    n, s = CHUNK >> (l + 1), 1 << l
                    dve.wait_ge(level_merged, h * (LEVELS + 1) + (l + 1))
                    dve.wait_ge(level_done, h * (LEVELS + 1) + (l + 2))
                    dve.sem_inc(dve_passed, 1)
                    mask = pair_mask[:, l * CHUNK // 2:(l + 1) * CHUNK // 2].bitcast(U32)\
                        .rearrange("p (n s) -> p n s", s=s).unsqueeze(1).to_broadcast([P, NC, n, s])
                    right = s_t[:, :].rearrange("p (c n two s) -> p c n two s", c=NC, two=2, s=s)[:, :, :, 1, :]
                    dve.copy_predicated(right, mask, psum[:, bank, :].rearrange("p (c n s) -> p c n s", c=NC, s=s))\
                       .then_inc(level_merged, 1)

                dve.wait_ge(q_gate, h + 1)
                dve.tensor_tensor(q_t[:, :], zq[:, :], q_t[:, :], ALU.mult).then_inc(q_ready, 1)
                dve.wait_ge(q_ready, h + 1)
                dve.wait_ge(f_ready, h + 1)
                dve.tensor_tensor(qd_t[:, :], q_t[:, :], decays[:, 0:SEQ], ALU.mult).then_inc(qd_start, 1)
                dve.wait_ge(g_gate, h + 1)
                dve.tensor_tensor(sg_t[:, :], zg[:, :], sg_t[:, :], ALU.mult).then_inc(sg_ready, 1)
                move(0)
                move(1)
                if not last:
                    dve.wait_ge(k_ready, h + 1)
                    take_f(h + 1)
                merge_diagonal()
                merge(0, 4)
                move(2)
                if last:
                    for d in range(KT - 1):
                        mix_lo(0, d, mix1)
                merge(1, 5)
                move(3)
                if not last:
                    take_q(h + 1)
                merge(2, 4)
                move(4)
                merge(3, 5)
                move(5)
                merge(4, 6)
                move(6)
                merge(5, 4)
                if not last:
                    dve.wait_ge(v_turned, h + 1)
                    take_i(h + 1)
                merge(6, 5)
                chunk_decay = 2 * SEQ - (2 * SEQ >> LEVELS)
                dve.wait_ge(level_moved, h * LEVELS + LEVELS)
                dve.wait_ge(update_done, h + 1)
                for c in range(NC - 1):
                    update = psum[:, 4 + c // 4, (c % 4) * P:(c % 4 + 1) * P]
                    if c == 0:
                        dve.tensor_copy(states[:, 1, :], update).then_inc(state_ready, 1)
                    else:
                        dve.wait_ge(state_ready, h * (NC - 1) + c)
                        dve.scalar_tensor_tensor(states[:, c + 1, :], states[:, c, :],
                                                 decays[:, chunk_decay + c:chunk_decay + c + 1], update,
                                                 ALU.mult, ALU.add).then_inc(state_ready, 1)
                if not last:
                    dve.wait_ge(sg_ready, h + 1)
                    take_g(h + 1)
                dve.wait_ge(o_inv, h + 1)
                dve.tensor_tensor(e_t[:, 1, :], banks(6), e_t[:, 0, :], ALU.mult).then_inc(o_scaled, 1)
                dve.wait_ge(o_scaled, h + 2)
                dve.wait_ge(sg_ready, h + 1)
                y = mix1[:, h + 2, :] if isinstance(h, int) else \
                    mix1[:, bass.ds(h + 2, 1), :].rearrange("p a t -> p (a t)")
                dve.scalar_tensor_tensor(y, e_t[:, 1, :], col("hgrn_norm_g", h), sg_t[:, :], ALU.mult, ALU.mult)\
                   .then_inc(y_ready, 1)

            with dve.Fori(0, HEADS - 1) as i:
                head(i, False)
            head(HEADS - 1, True)
            mix_lo(0, KT - 1, mix1)

            def add_out(first_tile, first_sum, first_ready, gain, first_h):
                for d in range(KT):
                    dve.wait_ge(tile_done, first_tile + d + 1)
                    dve.tensor_tensor(x_t[:, d, :], x_t[:, d, :], banks(2 * (d % 2)), ALU.add).then_inc(x_added, 1)
                    if d >= 2:
                        add_square(d - 1, first_sum, first_ready)
                lo_part(0, col(gain, 0), first_h)
                add_square(KT - 1, first_sum, first_ready)
                for d in range(1, KT):
                    lo_part(d, col(gain, d), first_h)

            dve.wait_ge(x_back, 16)
            dve.wait_ge(x_back_last, 16)
            add_out(T_OUT1, SUMS_MLP, 2 * KT, "norm_mlp_g", H_MLP)

            def add_down(c, n, first_chunk, after_group=lambda g: None):
                for part in range(2):
                    for g in range(8):
                        if g < 7:
                            dve.wait_ge(down_done, c * 14 + (14 * first_chunk + 7 * part + g + 1))
                        else:
                            dve.wait_ge(tile_done, n + (part + 1))
                        x_d = x_t[:, 4 * part + g // 2, (g % 2) * HALF:(g % 2 + 1) * HALF]
                        dve.tensor_tensor(x_d, x_d, psum[:, 4 + g % 4, :], ALU.add).then_inc(down_added, 1)
                        after_group(8 * part + g)

            def lo_activations(a, hi, lo, first):
                for j in range(2):
                    dve.wait_ge(act_hi_ready, first + (j + 1))
                    dve.tensor_tensor(lo[:, j, :], a[:, j, :], hi[:, j, :].bitcast(F32),
                                      ALU.subtract).then_inc(act_split, 1)

            def mlp_relu(c, n):
                for j in range(2):
                    dve.wait_ge(tile_done, n + (j + 1))
                    dve.wait_ge(act_split, c * 2 + (j + 1))
                    dve.scalar_tensor_tensor(mlp_a[:, j, :], banks(2 * j), 0.0, rinv[:, :], ALU.max, ALU.mult)\
                       .then_inc(up_read, 1)

            dve.wait_ge(rinv_ready, 2)
            mlp_relu(0, T_MLP)
            lo_activations(mlp_a, mlp_hi, mlp_lo, 0)
            with dve.Fori(0, MLP_CHUNKS - 1) as i:
                mlp_relu(i + 1, i * 4 + (T_MLP + 2))
                add_down(i, i * 4 + (T_MLP + 4), 0)
                lo_activations(mlp_a, mlp_hi, mlp_lo, i * 2 + 2)

            def block_lo(d):
                lo_part(d, gain_both[:, d:d + 1], H_MIX2)

            def sum_gained(d):
                dve.wait_ge(sq_ready, 3 * KT + d + 1)
                if d == 0:
                    dve.tensor_scalar(sq_sum_gain[:, :], sq_sum[:, :], gain_sq[:, 0:1], None, ALU.mult)\
                       .then_inc(sq_summed, 1)
                else:
                    dve.wait_ge(sq_summed, SUMS_MIX2 + 2 * d - 1)
                    dve.scalar_tensor_tensor(sq_sum_gain[:, :], sq[:, d % 2, :], gain_sq[:, d:d + 1], sq_sum_gain[:, :],
                                             ALU.mult, ALU.add).then_inc(sq_summed, 1)

            def sum_plain(d):
                dve.wait_ge(sq_ready, 3 * KT + d + 1)
                dve.wait_ge(sq_summed, SUMS_MIX2 + 2 * d - 1)
                dve.tensor_tensor(sq_sum[:, :], sq_sum[:, :], sq[:, d % 2, :], ALU.add).then_inc(sq_summed, 1)

            between_adds = [(block_lo, 0), (sum_gained, 0)]
            for d in range(1, 4):
                between_adds += [(block_lo, d), (sum_plain, d), (sum_gained, d)]

            def after_group(g):
                if 3 <= g < 3 + len(between_adds):
                    step, d = between_adds[g - 3]
                    step(d)

            add_down(MLP_CHUNKS - 1, T_CB - 2, 0, after_group)
            for d in range(4, KT):
                block_lo(d)
            for d in range(4, KT):
                sum_plain(d)
                sum_gained(d)
            dve.wait_ge(block_rinv1, 1)
            dve.wait_ge(norm_summed, 4)
            dve.tensor_tensor(sq[:, 0, :], sq[:, 0, :], banks(6), ALU.mult).then_inc(block_mean, 1)
            dve.wait_ge(rinv_ready, 3)
            dve.tensor_tensor(rinv[:, :], rinv1[:, :], sq[:, 1, :], ALU.mult).then_inc(rinv_ready, 1)
            dve.wait_ge(rinv_ready, 4)

            for c in range(CT):
                dve.wait_ge(tile_done, T_CB + c + 1)
                dve.tensor_tensor(sig_cb[:, c, :], banks(2 * (c % 2)), rinv[:, :], ALU.mult).then_inc(cb_read, 1)
                if c == 1:
                    for d in range(KT):
                        dve.scalar_tensor_tensor(x_t[:, d, :], x_t[:, d, :], col("final_norm_g", d), rinv1[:, :],
                                                 ALU.mult, ALU.mult).then_inc(x_ready, 1)
            dve.wait_ge(x_ready, KT)

            dve.memset(q_hi[:, :, :].bitcast(F32), 0.0)
            dve.memset(q_lo[:, :, :].bitcast(F32), 0.0).then_inc(q_zeroed, 1)
            dve.memset(u_t[:, 0:CONV_PAD], 0.0)
            dve.memset(u_t[:, CONV_PAD + SEQ:], 0.0).then_inc(u_zeroed, 1)
            dve.wait_ge(q_zeroed, 1)
            dve.wait_ge(u_zeroed, 1)
            dve.wait_ge(x_spilled, 32)

            with dve.Fori(0, PAIRS) as p:
                def convolve(taps):
                    acc = conv_t[:, bass.ds(p, 1), :].rearrange("p a t -> p (a t)")
                    for tap in taps:
                        w = col("conv_dw_w_2", p + tap * CT)
                        if tap == 0:
                            dve.tensor_scalar(acc, u_t[:, 0:SEQ], w, col("conv_dw_b_2", p), ALU.mult, ALU.add)\
                               .then_inc(conv_step, 1)
                        else:
                            dve.wait_ge(conv_step, p * CONV_K + tap)
                            dve.scalar_tensor_tensor(acc, u_t[:, tap:tap + SEQ], w, acc, ALU.mult, ALU.add)\
                               .then_inc(conv_step, 1)

                dve.wait_ge(bias_loaded, p * 16 + 16)
                dve.tensor_tensor(bias[:, :, :], bias[:, :, :],
                                  col_mask[:, :].unsqueeze(1).to_broadcast([P, RPB_H, GRID_W]),
                                  ALU.add).then_inc(bias_ready, 1)
                u = u_t[:, CONV_PAD:CONV_PAD + SEQ]
                dve.wait_ge(tile_done, p * 4 + (T_PAIRS + 1))
                dve.tensor_tensor(u, banks(0), rinv[:, :], ALU.mult).then_inc(u_read, 1)
                dve.wait_ge(u_read, p + 1)
                dve.wait_ge(cb_ready, CT)
                dve.scalar_tensor_tensor(u, u, col("b_in_2", p + CA2 // P),
                                         sig_cb[:, bass.ds(p, 1), :].rearrange("p a t -> p (a t)"),
                                         ALU.add, ALU.mult).then_inc(u_ready, 1)
                dve.wait_ge(u_ready, p + 1)
                convolve(range(0, 7))
                dve.wait_ge(tile_done, p * 4 + (T_PAIRS + 2))
                dve.tensor_tensor(v_t[:, :], banks(2), rinv[:, :], ALU.mult).then_inc(v_read, 1)
                convolve(range(7, 14))
                dve.wait_ge(tile_done, p * 4 + (T_PAIRS + 3))
                dve.tensor_tensor(q32[:, :], banks(0), rinv[:, :], ALU.mult).then_inc(q_read, 1)
                convolve(range(14, 20))
                dve.wait_ge(q_hi_ready, p + 1)
                for j in range(2):
                    half = slice(DH * j, DH * (j + 1))
                    last = dve.tensor_tensor(q_lo[half, :, half], q32[half, :].rearrange("p (r c) -> p r c", c=GRID_W),
                                             q_hi[half, :, half].bitcast(F32), ALU.subtract)
                last.then_inc(q_split, 1)
                dve.wait_ge(tile_done, p * 4 + (T_PAIRS + 4))
                dve.tensor_tensor(k32[:, :], banks(2), rinv[:, :], ALU.mult).then_inc(k_read, 1)
                dve.wait_ge(k_hi_ready, p + 1)
                dve.tensor_tensor(k_lo[:, :], k32[:, :], k_hi[:, :].bitcast(F32), ALU.subtract).then_inc(k_split, 1)
                dve.wait_ge(bias_ready, p + 1)
                for s in range(ROWS + 1):
                    if s < ROWS:
                        dve.wait_ge(scores_done, p * ROWS + (s + 1))
                        dve.sem_inc(dve_passed, 1)
                        _, first = row_window(s)
                        dve.tensor_tensor_reduce(
                            out=prob[:, s % 3, :], in0=psum[:, 4 + s % 2, :],
                            in1=bias[:, first:first + KH, :].rearrange("p r c -> p (r c)"), scale=1.0, scalar=3 * NEG,
                            op0=ALU.add, op1=ALU.max, accum_out=row_max[:, s % 2:s % 2 + 1]).then_inc(scores_max, 1)
                        dve.wait_ge(scores_max, p * ROWS + (s + 3))
                        dve.tensor_scalar(neg_max[:, s % 2:s % 2 + 1], row_max[:, s % 2:s % 2 + 1], -1.0, None,
                                          ALU.mult).then_inc(neg_max_ready, 1)
                    if s >= 1:
                        u = s - 1
                        dve.wait_ge(prob_exp, p * ROWS + (u + 1))
                        dve.reciprocal(row_inv[:, u % 2:u % 2 + 1], row_sum[:, u % 2:u % 2 + 1]).then_inc(inv_ready, 1)
                        dve.wait_ge(inv_ready, p * ROWS + (u + 1))
                        dve.tensor_scalar(prob[:, u % 3, :], prob[:, u % 3, :], row_inv[:, u % 2:u % 2 + 1], None,
                                          ALU.mult).then_inc(prob_ready, 1)
                    if s >= 5 and 15 + s < CONV_K:
                        convolve([15 + s])
                convolve(range(31, CONV_K))

            for c in range(PAIRS):
                dve.wait_ge(branch_hi, c + 1)
                dve.tensor_tensor(att_lo[:, c, :], att_t[:, c, :], att_hi[:, c, :].bitcast(F32), ALU.subtract)\
                   .then_inc(branch_split, 1)
            dve.wait_ge(ln_mean_ready, 1)
            for c in range(CT):
                dve.tensor_tensor(conv_t[:, c, :], conv_t[:, c, :], ln_mean[:, :], ALU.subtract).then_inc(ln_centred, 1)
            dve.wait_ge(ln_inv_ready, 1)
            for c in range(CT):
                dve.tensor_tensor(conv_t[:, c, :], conv_t[:, c, :], ln_inv[:, :], ALU.mult).then_inc(ln_scaled, 1)
            for c in range(CT):
                dve.wait_ge(branch_hi, PAIRS + c + 1)
                dve.tensor_tensor(conv_lo[:, c, :], conv_t[:, c, :], conv_hi[:, c, :].bitcast(F32), ALU.subtract)\
                   .then_inc(branch_split, 1)

            with dve.Fori(0, KT // 2) as i:
                for s in range(2):
                    d1 = i * 2 + (s + 1)
                    dve.wait_ge(tile_done, i * 6 + (T_MERGE + 3 * s + 1))
                    dve.wait_ge(branch_a, d1)
                    dve.tensor_tensor(sig_a[:, :], banks(0), rinv[:, :], ALU.mult).then_inc(gate_a_read, 1)
                    dve.wait_ge(tile_done, i * 6 + (T_MERGE + 3 * s + 2))
                    dve.wait_ge(merged, d1)
                    dve.tensor_tensor(sig_b[:, :], banks(2), rinv[:, :], ALU.mult).then_inc(gate_b_read, 1)
                    dve.wait_ge(tile_done, i * 6 + (T_MERGE + 3 * s + 3))
                    dve.wait_ge(gate_a_ready, d1)
                    dve.tensor_tensor(br_a[:, :], sig_a[:, :], banks(4), ALU.mult).then_inc(branch_a, 1)
                    dve.wait_ge(gate_b_ready, d1)
                    dve.tensor_tensor(sig_b[:, :], sig_b[:, :], banks(6), ALU.mult).then_inc(branch_b, 1)
                    dve.wait_ge(branch_b, d1 + 1)
                    dve.tensor_tensor(mix2[:, bass.ds(i * 2 + s, 1), :].rearrange("p a t -> p (a t)"), br_a[:, :],
                                      sig_b[:, :], ALU.add).then_inc(merged, 1)

            for d in range(KT):
                mix_lo(1, d, mix2)
            dve.wait_ge(x_back, 32)
            add_out(T_OUT2, SUMS_FFN, 4 * KT, "norm2_g_2", H_FFN)

            def ffn_read_out(c, n, j):
                for part in range(2):
                    tile = c * 4 + (2 * j + part)
                    dve.wait_ge(tile_done, n + (2 * j + part + 1))
                    if not isinstance(c, int) or j == 1:
                        dve.wait_ge(ffn_right, tile - 1)
                    dve.tensor_tensor(ffn_z[:, part, :], banks(2 * part), rinv[:, :], ALU.mult).then_inc(ffn_read, 1)

            def ffn_steps(c, j):
                def tap(part, buf, left):
                    tile, k = c * 4 + (2 * j + part), c * 2 + (part * FT2 + j)
                    if left:
                        dve.wait_ge(ffn_mid, tile + 1)
                        dve.scalar_tensor_tensor(buf[:, 1:], ffn_z[:, part, 0:SEQ - 1], col("ffn_dw_w_2/0", k),
                                                 buf[:, 1:], ALU.mult, ALU.add).then_inc(ffn_left, 1)
                    else:
                        dve.wait_ge(ffn_left, tile + 1)
                        dve.scalar_tensor_tensor(buf[:, 0:SEQ - 1], ffn_z[:, part, 1:], col("ffn_dw_w_2/2", k),
                                                 buf[:, 0:SEQ - 1], ALU.mult, ALU.add).then_inc(ffn_right, 1)

                def gate():
                    dve.wait_ge(ffn_gelu, c * 2 + (j + 1))
                    dve.wait_ge(ffn_right, c * 4 + (2 * j + 2))
                    dve.tensor_tensor(ffn_a[:, j, :], ffn_gate[:, :], ffn_val[:, :], ALU.mult).then_inc(act_ready, 1)

                return [lambda: tap(0, ffn_gate, True), lambda: tap(0, ffn_gate, False),
                        lambda: tap(1, ffn_val, True), lambda: tap(1, ffn_val, False), gate]

            def ffn_first(c, n):
                ffn_read_out(c, n, 0)
                for step in ffn_steps(c, 0):
                    step()
                ffn_read_out(c, n, 1)

            dve.wait_ge(rinv_ready, 5)
            ffn_first(0, T_FFN)
            for step in ffn_steps(0, 1):
                step()
            lo_activations(ffn_a, ffn_hi, ffn_lo, 2 * MLP_CHUNKS)
            with dve.Fori(0, FFN_CHUNKS - 1) as i:
                ffn_first(i + 1, i * 6 + (T_FFN + 4))
                steps = ffn_steps(i + 1, 1)
                add_down(i, i * 6 + (T_FFN + 8), MLP_CHUNKS, lambda g: steps[g]() if g < len(steps) else None)
                lo_activations(ffn_a, ffn_hi, ffn_lo, i * 2 + (2 * MLP_CHUNKS + 2))

            def sum_after_group(g):
                if g % 2 == 1 and g >= 5:
                    add_square(g // 2 - 1, SUMS_OUT, 5 * KT)

            add_down(FFN_CHUNKS - 1, T_END - 2, MLP_CHUNKS, sum_after_group)
            add_square(KT - 1, SUMS_OUT, 5 * KT)
            dve.wait_ge(out_gain_loaded, 16)
            dve.wait_ge(y_copied, KT)
            dve.wait_ge(out_inv_ready, 1)
            for t in range(KT):
                dve.scalar_tensor_tensor(y_tok[:, t, :], y_tok[:, t, :], out_inv[:, t:t + 1], out_gain[:, :],
                                         ALU.mult, ALU.mult).then_inc(out_ready, 1)


_INS = ["x", "norm_mix_g", "w_in", "pool_w", "pool_scale", "hgrn_norm_g", "w_out", "norm_mlp_g", "w_up", "w_down",
        "final_norm_g", "norm1_g_2", "w_in_2", "b_in_2", "rpb_2", "w_na_out_2", "conv_dw_w_2", "conv_dw_b_2",
        "conv_ln_g_2", "conv_ln_b_2", "w_conv_out_2", "w_out_2", "norm2_g_2", "w_up_2", "ffn_dw_w_2", "ffn_dw_b_2",
        "w_down_2", "norm_f_g_2"]


def _constants():
    import numpy as np

    s, t = np.arange(CHUNK)[:, None], np.arange(CHUNK)[None, :]
    masks = [(((s >> (l + 1)) == (t >> (l + 1))) & ((s >> l) & 1 == 0))[:, (t[0] >> l) & 1 == 1] for l in range(LEVELS)]
    masks.append(s == t)
    tokens = np.arange(1, SEQ + 1)
    windows = np.repeat(np.array(POOL_WINDOWS), POOL_W // len(POOL_WINDOWS))
    inv = 1.0 / np.minimum(tokens[None, :], windows[:, None])
    c = np.arange(P)[:, None] % GRID_W
    k = np.arange(GRID_W)[None, :]
    first = np.clip(c - KW // 2, 0, GRID_W - KW)
    return {
        "c_ident": np.eye(P, dtype=np.float32),
        "c_pair_mask": np.concatenate(masks, axis=1).astype(np.float32),
        "c_pool_inv": np.ascontiguousarray(inv.reshape(2, P, SEQ).transpose(1, 0, 2)).astype(np.float32),
        "c_col_mask": np.where((k >= first) & (k < first + KW), 0.0, NEG).astype(np.float32),
    }


def kernel(**inputs):
    import numpy as np
    import concourse.bacc as bacc
    from concourse.bass_utils import run_bass_kernel_spmd as run

    nc = bacc.Bacc("TRN2", target_bir_lowering=False, num_devices=1)
    arrays, dram = {}, {}
    given = {name: np.ascontiguousarray(inputs[name]) for name in _INS} | _constants()
    for name, a in given.items():
        if name not in ("x", "final_norm_g", "norm_f_g_2") and not name.startswith("c_"):
            a = a[0]
        arrays[f"in_{name}"] = a
        dram[name] = nc.dram_tensor(f"in_{name}", a.shape, mybir.dt.from_np(a.dtype), kind="ExternalInput").ap()
    out = nc.dram_tensor("out", (1, SEQ, D), F32, kind="ExternalOutput").ap()
    two_blocks(nc, dram, out)
    return run(nc, [arrays], core_ids=[0]).results[0]["out"]
```

```python
import concourse.bass as bass
from concourse import mybir
from contextlib import ExitStack

F32 = mybir.dt.float32
F32R = mybir.dt.float32r
U32 = mybir.dt.uint32
ACT = mybir.ActivationFunctionType
ALU = mybir.AluOpType

P = 128
SEQ = 1024
D = 1024
KT = D // P
HALF = 512
QUARTER = 256
BANKS = 8
SPILLS = 4
SQ_SLOTS = 4
POOL_W = 256
POOL_WINDOWS = (2, 4, 8, 16)
POOL_PAD = 16
HEADS = 6
HG_W = HEADS * P
CHUNK = 128
NC = SEQ // CHUNK
LEVELS = 7
MASK_W = LEVELS * CHUNK // 2 + CHUNK
D_FF = 4096
GRID_W = 64
ROWS = SEQ // GRID_W
NA_HEADS = 8
DH = 64
D_ATTN = NA_HEADS * DH
KH, KW = 8, 16
PAIRS = NA_HEADS // 2
GROUP_W = 8
GROUPS = GRID_W // GROUP_W
UNITS = 2 * GROUPS
WIN = 3 * P
RPB_H, RPB_W = 2 * KH - 1, 2 * KW - 1
RPB_PAD = ROWS - KH
SHIFTS = 3 * GROUP_W
SHIFT_ROWS = 2 * ROWS - 1
NEG = -1e30
CONV_CH = 512
CT = CONV_CH // P
CONV_K = 31
CONV_PAD = CONV_K // 2
POOL_TAPS = 8
DVE_TAPS = CONV_K - POOL_TAPS
TAIL_TAPS = 8
CONV_STEPS = DVE_TAPS + 1
D_FF2 = 2816
FT2 = D_FF2 // P
MLP_CHUNKS = D_FF // (2 * P)
FFN_CHUNKS = FT2 // 2
EPS1, EPS2 = 1e-5, 1e-6

Q1, F1, I1, G1 = POOL_W, POOL_W + HG_W, POOL_W + 2 * HG_W, POOL_W + 3 * HG_W
Q2, K2, V2 = 0, D_ATTN, 2 * D_ATTN
CA2, CB2 = 3 * D_ATTN, 3 * D_ATTN + CONV_CH
GA2, GB2 = 3 * D_ATTN + 2 * CONV_CH, 3 * D_ATTN + 2 * CONV_CH + D
D_IN2 = GB2 + D

VECTORS = [
    [("norm_mix_g", 8), ("pool_scale", 2), ("hgrn_norm_g", 6), ("norm_mlp_g", 8), ("final_norm_g", 8),
     ("norm1_g_2", 8), ("b_in_2", D_IN2 // P), ("norm2_g_2", 8), ("norm_f_g_2", 8), ("conv_dw_b_2", CT),
     ("conv_ln_g_2", CT), ("conv_ln_b_2", CT)],
    [("ffn_dw_b_2", 2 * FT2), ("ffn_dw_w_2/0", 2 * FT2)],
    [("ffn_dw_w_2/1", 2 * FT2), ("ffn_dw_w_2/2", 2 * FT2)],
    [("conv_dw_w_2", CONV_K * CT)],
]
COL = {}
for _s, _stack in enumerate(VECTORS):
    _at = _s * P
    for _name, _n in _stack:
        COL[_name] = _at
        _at += _n

NEXT_AFTER = {3: [0], UNITS: [1, 2], UNITS + 1: [3, 4], UNITS + 2: [5, 6], UNITS + 3: [7]}

T_POOL = 0
T_HEADS = T_POOL + POOL_W // P
T_OUT1 = T_HEADS + 4 * HEADS
T_MLP = T_OUT1 + KT
T_CB = T_MLP + 4 * MLP_CHUNKS
T_PAIRS = T_CB + CT
T_MERGE = T_PAIRS + 4 * PAIRS
T_OUT2 = T_MERGE + 3 * KT
T_FFN = T_OUT2 + KT
T_END = T_FFN + 6 * FFN_CHUNKS

H_MIX1 = 0
H_MLP = H_MIX1 + 4 * KT
H_MIX2 = H_MLP + 2 * KT
H_FFN = H_MIX2 + KT
HALVES_AHEAD = [(d, 0) for d in range(KT - 1)]
HALVES_BEHIND = [(0, 1), (1, 1), (KT - 1, 0)] + [(d, 1) for d in range(2, KT)]
HALVES = HALVES_AHEAD + HALVES_BEHIND
SUMS_MIX1 = 0
SUMS_MLP = SUMS_MIX1 + 2 * (KT - 1)
SUMS_MIX2 = SUMS_MLP + KT - 1
SUMS_FFN = SUMS_MIX2 + 2 * KT - 1
SUMS_OUT = SUMS_FFN + KT - 1

BASE = 16512
KB = 1024
A_X = BASE
A_HI = A_X + 32 * KB
A_LO = A_HI + 32 * KB
A_RAW = A_LO + 32 * KB
A_WHI = A_RAW + 8 * KB
A_WLO = A_WHI + 8 * KB
A_CONST = A_WLO + 8 * KB
A_ARENA = A_CONST + 9 * KB
A_END = 229344


def two_blocks(nc, dram, out):
    ctx = ExitStack()
    with ctx:
        def sem(name):
            return ctx.enter_context(nc.semaphore(name))

        def at(name, shape, address, dtype=F32):
            return nc.alloc_sbuf_tensor_at(name, shape, dtype, offset=address)

        x_t = at("x_t", [P, KT, SEQ], A_X)
        mix1 = at("mix1", [P, KT, SEQ], A_X)
        h_hi = at("h_hi", [P, KT, SEQ], A_HI, F32R)
        h_lo = at("h_lo", [P, KT, SEQ], A_LO, F32R)
        w_raw = at("w_raw", [P, 2, 1024], A_RAW)
        w_hi = at("w_hi", [P, 2, 1024], A_WHI, F32R)
        w_lo = at("w_lo", [P, 2, 1024], A_WLO, F32R)

        ident = at("ident", [P, P], A_CONST)
        ones = at("ones", [P, P], A_CONST + 512)
        cols = at("cols", [P, 4 * P], A_CONST + 1024)
        eps1, eps2, row_max, neg_max, row_sum, row_inv = (
            at(name, [P, n], A_CONST + 4096 + 32 * j) for j, (name, n) in enumerate(
                (("eps1", 1), ("eps2", 1), ("row_max", 2), ("neg_max", 2),
                 ("row_sum", 2), ("row_inv", 2))))
        gain_both, gain_sq, q_bias, out_inv = (
            at(name, [P, 8], A_CONST + 4608 + 32 * j)
            for j, name in enumerate(("gain_both", "gain_sq", "q_bias", "out_inv")))
        first_gain = at("first_gain", [P, KT], A_CONST + 4800)
        rinv = at("rinv", [P, SEQ], A_CONST + 5 * KB)

        def arena(*shapes):
            got, a = [], A_ARENA
            for name, shape, dtype in shapes:
                size = 4
                for n in shape[1:]:
                    size *= n
                got.append(at(name, shape, a, dtype))
                a += -(-size // 32) * 32
            assert a <= A_END, a
            return got

        x_in, = arena(("x_in", [P, KT, D], F32))
        A_NORM = (A_END - 28 * KB) // 32 * 32
        rinv1 = at("rinv1", [P, SEQ], A_NORM)
        sq_sum_gain = at("sq_sum_gain", [P, SEQ], A_NORM + 4 * KB)
        sq = at("sq", [P, SQ_SLOTS, SEQ], A_NORM + 8 * KB)
        stack_rows = at("stack_rows", [P, 4, P], A_NORM + 4 * KB)
        gain_rows = at("gain_rows", [KT, P], A_NORM + 6 * KB)
        rpb_zeros = at("rpb_zeros", [RPB_PAD, RPB_W], A_NORM + 7 * KB)
        sq_sum = at("sq_sum", [P, SEQ], A_NORM + 24 * KB)
        (zf, zq, zv, zg, decays, k_t, kd_t, q_t, qd_t, sg_t, v_tok, e_t, s_t, kd_tok, states, pool_w,
         pair_mask) = arena(
            ("zf", [P, SEQ], F32), ("zq", [P, SEQ], F32), ("zv", [P, SEQ], F32), ("zg", [P, SEQ], F32),
            ("decays", [P, 2 * SEQ], F32), ("k_t", [P, SEQ], F32), ("kd_t", [P, SEQ], F32),
            ("q_t", [P, SEQ], F32), ("qd_t", [P, SEQ], F32), ("sg_t", [P, SEQ], F32),
            ("v_tok", [P, NC, P], F32), ("e_t", [P, 2, SEQ], F32), ("s_t", [P, SEQ], F32),
            ("kd_tok", [P, NC, P], F32), ("states", [P, NC, P], F32), ("pool_w", [P, 2, P], F32),
            ("pair_mask", [P, MASK_W], F32))
        w_hi_first = at("w_hi_first", [P, 1024], A_ARENA + 4 * KB, F32R)
        w_lo_first = at("w_lo_first", [P, 1024], A_ARENA + 8 * KB, F32R)
        w_out_parts = [[at(f"w_out_{part}_{j}", [P, 1024], A_ARENA + (8 * j + 4 * i) * KB, F32R)[:, :]
                        for i, part in enumerate(("hi", "lo"))] for j in range(2)]
        PADDED = POOL_PAD + SEQ
        A_POOL = A_ARENA + 20 * KB
        pool_u = at("pool_u", [P, 2, PADDED], A_POOL)
        pool_a = at("pool_a", [P, PADDED], A_POOL + 2 * 4 * PADDED)
        pool_b = at("pool_b", [P, PADDED], A_POOL + 3 * 4 * PADDED)
        pool_inv = at("pool_inv", [P, 2, SEQ], A_POOL + 4 * 4 * PADDED)
        pool_p = at("pool_p", [P, 2, SEQ], A_POOL + 4 * 4 * PADDED + 8 * KB)
        assert A_POOL + 4 * 4 * PADDED + 16 * KB <= A_ARENA + 68 * KB
        mlp_a, mlp_hi, mlp_lo, mlp_hi_last, mlp_lo_last = arena(
            ("mlp_a", [P, 2, SEQ], F32), ("mlp_hi", [P, 2, SEQ], F32R), ("mlp_lo", [P, 2, SEQ], F32R),
            ("mlp_hi_last", [P, 2, SEQ], F32R), ("mlp_lo_last", [P, 2, SEQ], F32R))
        ffn_z, ffn_gate, ffn_val, ffn_a, ffn_hi, ffn_lo, ffn_hi_last, ffn_lo_last = arena(
            ("ffn_z", [P, 2, SEQ], F32),
            ("ffn_gate", [P, SEQ], F32), ("ffn_val", [P, SEQ], F32), ("ffn_a", [P, 2, SEQ], F32),
            ("ffn_hi", [P, 2, SEQ], F32R), ("ffn_lo", [P, 2, SEQ], F32R),
            ("ffn_hi_last", [P, 2, SEQ], F32R), ("ffn_lo_last", [P, 2, SEQ], F32R))
        conv_t = at("conv_t", [P, CT, SEQ], A_X)
        att_t = at("att_t", [P, PAIRS, SEQ], A_X + 16 * KB)
        conv_lo = at("conv_lo", [P, CT, SEQ], A_X, F32R)
        att_lo = at("att_lo", [P, PAIRS, SEQ], A_X + 16 * KB, F32R)
        U_PAD = CONV_PAD + SEQ + CONV_PAD
        (sig_cb, q_hi, q_lo, k_hi, k_lo, v_t, v_keys, bias_raw, prob_t, bias, near_mask, prob, u_t, qk32,
         conv_pool) = arena(
            ("sig_cb", [P, CT, SEQ], F32), ("q_hi", [P, SEQ], F32R), ("q_lo", [P, SEQ], F32R),
            ("k_hi", [P, SEQ], F32R), ("k_lo", [P, SEQ], F32R), ("v_t", [P, SEQ], F32),
            ("v_keys", [P, GROUPS, P], F32), ("bias_raw", [P, 2, 3, P], F32), ("prob_t", [P, 2, WIN], F32),
            ("bias", [P, 2, 5, P], F32), ("near_mask", [P, 3, P], F32), ("prob", [P, 3, WIN], F32),
            ("u_t", [P, U_PAD], F32), ("qk32", [P, SEQ], F32), ("conv_pool", [P, SEQ], F32))
        tap_product = sig_cb[:, 0, :]
        conv_hi, att_hi, mix2, sig_a, sig_b = arena(
            ("conv_hi", [P, CT, SEQ], F32R), ("att_hi", [P, PAIRS, SEQ], F32R), ("mix2", [P, KT, SEQ], F32),
            ("sig_a", [P, 2, SEQ], F32), ("sig_b", [P, SEQ], F32))
        A_LN = A_ARENA + 32 * KB
        ln_mean = at("ln_mean", [P, SEQ], A_LN)
        ln_sq = at("ln_sq", [P, CT, SEQ], A_LN + 4 * KB)
        ln_inv = at("ln_inv", [P, SEQ], A_LN + 20 * KB)
        y_tok = at("y_tok", [P, KT, D], A_HI)
        out_gain = at("out_gain", [P, D], A_LO)
        w_hi_last = at("w_hi_last", [P, 1024], A_LO + 4 * KB, F32R)
        w_lo_last = at("w_lo_last", [P, 1024], A_LO + 8 * KB, F32R)

        psum = ctx.enter_context(nc.psum_tensor("psum", [P, BANKS, HALF], F32))

        def banks(b, n=2):
            return psum[:, b:b + n, :].rearrange("p b t -> p (b t)")

        v_bias = cols[:, COL["b_in_2"] + V2 // P:COL["b_in_2"] + V2 // P + PAIRS]

        def col(name, k=0):
            c = COL[name] + k
            return cols[:, bass.ds(c, 1)] if not isinstance(c, int) else cols[:, c:c + 1]

        x_spill = nc.dram_tensor("x_spill", (P, KT * SEQ), F32, kind="Internal").ap()
        rpb_rows = nc.dram_tensor("rpb_rows", (NA_HEADS * RPB_H + 2 * RPB_PAD, RPB_W), F32, kind="Internal").ap()
        shifted = nc.dram_tensor("shifted", (NA_HEADS, SHIFTS, SHIFT_ROWS, GROUP_W), F32, kind="Internal").ap()
        bias_rows = nc.dram_tensor("bias_rows", (PAIRS, P, 2, 3, P), F32, kind="Internal").ap()

        def by_row(tile):
            return tile.rearrange("p (r g c) -> p r g c", g=GROUPS, c=GROUP_W)

        def by_group(tile):
            return tile.rearrange("p (g r c) -> p r g c", g=GROUPS, c=GROUP_W)

        weight_loaded = [sem("weight_loaded_0"), sem("weight_loaded_1")]
        weight_split = sem("weight_split")
        weight_hi = sem("weight_hi")
        tile_done = sem("tile_done")
        sp_passed, pool_passed, dve_passed = (sem(f"{e}_passed") for e in ("sp", "pool", "dve"))
        consts_loaded = sem("consts_loaded")
        gain_loaded = sem("gain_loaded")
        gain_turned = sem("gain_turned")
        gain_ready = sem("gain_ready")
        x_loaded = [sem(f"x_loaded_{t}") for t in range(KT)]
        rows_loaded = sem("rows_loaded")
        rows_zeroed = sem("rows_zeroed")
        rpb_zeroed = sem("rpb_zeroed")
        rpb_stored = sem("rpb_stored")
        shifted_stored = sem("shifted_stored")
        mask_loaded = sem("mask_loaded")
        bias_stored = sem("bias_stored")
        memsets = sem("memsets")
        cols_turned = sem("cols_turned")
        cols_ready = sem("cols_ready")
        x_turned = sem("x_turned")
        x_copied = sem("x_copied")
        x_copied_rest = sem("x_copied_rest")
        x_spilled = sem("x_spilled")
        x_back = sem("x_back")
        x_ready = sem("x_ready")
        sq_ready = sem("sq_ready")
        sq_summed = sem("sq_summed")
        norm_summed = sem("norm_summed")
        mean_log = sem("mean_log")
        rinv_ready = sem("rinv_ready")
        block_rinv1 = sem("block_rinv1")
        block_mean = sem("block_mean")
        h_hi_ready = sem("h_hi_ready")
        h_ready = sem("h_ready")
        mix_hi_ready = sem("mix_hi_ready")
        mix_split = sem("mix_split")
        out_half_done = sem("out_half_done")
        x_added = sem("x_added")
        pool_w_zeroed = sem("pool_w_zeroed")
        pool_loaded = sem("pool_loaded")
        pool_inv_loaded = sem("pool_inv_loaded")
        pool_u_ready = sem("pool_u_ready")
        pool_step = sem("pool_step")
        pool_p_ready = sem("pool_p_ready")
        pool_mixed = sem("pool_mixed")
        pool_ready = sem("pool_ready")
        zf_ready, zq_ready, zv_ready, zg_ready = (sem(f"z{n}_ready") for n in "fqvg")
        q_gate = sem("q_gate")
        f_ready = sem("f_ready")
        kd_start = sem("kd_start")
        k_ready = sem("k_ready")
        g_gate = sem("g_gate")
        q_ready = sem("q_ready")
        qd_start = sem("qd_start")
        sg_ready = sem("sg_ready")
        level_ready = sem("level_ready")
        level_done = sem("level_done")
        level_moved = sem("level_moved")
        level_merged = sem("level_merged")
        v_turned = sem("v_turned")
        v_ready = sem("v_ready")
        kd_turned = sem("kd_turned")
        kd_tok_ready = sem("kd_tok_ready")
        update_done = sem("update_done")
        state_ready = sem("state_ready")
        o_done = sem("o_done")
        o_sq = sem("o_sq")
        o_mean = sem("o_mean")
        o_log = sem("o_log")
        o_inv = sem("o_inv")
        o_scaled = sem("o_scaled")
        y_ready = sem("y_ready")
        x_back_last = sem("x_back_last")
        up_read = sem("up_read")
        act_ready = sem("act_ready")
        act_hi_ready = sem("act_hi_ready")
        act_split = sem("act_split")
        down_done = sem("down_done")
        down_added = sem("down_added")
        ffn_read = sem("ffn_read")
        ffn_mid = sem("ffn_mid")
        ffn_left = sem("ffn_left")
        ffn_right = sem("ffn_right")
        ffn_gelu = sem("ffn_gelu")
        cb_read = sem("cb_read")
        cb_ready = sem("cb_ready")
        u_zeroed = sem("u_zeroed")
        bias_loaded = sem("bias_loaded")
        bias_ready = sem("bias_ready")
        v_read = sem("v_read")
        v_tiles_turned = sem("v_tiles_turned")
        v_tiles_ready = sem("v_tiles_ready")
        q_read = sem("q_read")
        q32_ready = sem("q32_ready")
        q_hi_ready = sem("q_hi_ready")
        q_split = sem("q_split")
        k_read = sem("k_read")
        k32_ready = sem("k32_ready")
        k_hi_ready = sem("k_hi_ready")
        k_split = sem("k_split")
        u_read = sem("u_read")
        u_ready = sem("u_ready")
        conv_step = sem("conv_step")
        tap_ready = sem("tap_ready")
        tap_added = sem("tap_added")
        scores_done = sem("scores_done")
        scores_max = sem("scores_max")
        neg_max_ready = sem("neg_max_ready")
        prob_exp = sem("prob_exp")
        inv_ready = sem("inv_ready")
        prob_ready = sem("prob_ready")
        prob_turned = sem("prob_turned")
        prob_t_ready = sem("prob_t_ready")
        prob_t_used = sem("prob_t_used")
        att_ready = sem("att_ready")
        ln_added = sem("ln_added")
        ln_summed = sem("ln_summed")
        ln_mean_ready = sem("ln_mean_ready")
        ln_centred = sem("ln_centred")
        ln_sq_ready = sem("ln_sq_ready")
        ln_var = sem("ln_var")
        ln_log = sem("ln_log")
        ln_inv_ready = sem("ln_inv_ready")
        ln_scaled = sem("ln_scaled")
        ln_silu = sem("ln_silu")
        branch_hi = sem("branch_hi")
        branch_split = sem("branch_split")
        gate_a_read = sem("gate_a_read")
        gate_b_read = sem("gate_b_read")
        gate_a_ready = sem("gate_a_ready")
        gate_b_ready = sem("gate_b_ready")
        branch_a = sem("branch_a")
        branch_b = sem("branch_b")
        merged = sem("merged")
        y_turned = sem("y_turned")
        y_copied = sem("y_copied")
        out_gain_loaded = sem("out_gain_loaded")
        out_inv_ready = sem("out_inv_ready")
        out_ready = sem("out_ready")
        stored = sem("stored")

        block = ctx.enter_context(nc.Block())

        def columns(w, first):
            v = w.rearrange("(k p) n -> p k n", p=P)
            c = slice(first, first + P) if isinstance(first, int) else bass.ds(first, P)
            return [v[:, 0:4, c], v[:, 4:8, c]]

        def rows(w, first, left):
            r = [slice(first + P * k, first + P * k + P) if isinstance(first, int)
                 else bass.ds(first + P * k, P) for k in range(2)]
            return [w[r[k], left:left + HALF] for k in range(2)]

        def branches(first):
            c = slice(first, first + P) if isinstance(first, int) else bass.ds(first, P)
            return [dram[n].rearrange("(k p) n -> p k n", p=P)[:, :, c] for n in ("w_na_out_2", "w_conv_out_2")]

        w_in, w_in2 = dram["w_in"], dram["w_in_2"]

        def head_tiles(h):
            return [columns(w_in, c + h * P) for c in (F1, Q1, I1, G1)]

        def mlp_up(c):
            return [columns(dram["w_up"], c * 2 * P + j * P) for j in range(2)]

        def mlp_down(c):
            return [rows(dram["w_down"], c * 2 * P, j * HALF) for j in range(2)]

        def pair_tiles(p):
            return [columns(w_in2, c + p * P) for c in (CA2, Q2, K2, V2)]

        def gate_tiles(d):
            return [columns(w_in2, GA2 + d * P), columns(w_in2, GB2 + d * P)]

        def merge_tiles(d):
            return gate_tiles(d + 1) + [branches(d * P)]

        def ffn_up(c):
            return [columns(dram["w_up_2"], part + c * 2 * P + j * P) for j in range(2) for part in (0, D_FF2)]

        def ffn_down(c):
            return [rows(dram["w_down_2"], c * 2 * P, j * HALF) for j in range(2)]

        pool_tiles = [columns(w_in, j * P) for j in range(POOL_W // P)]

        def weight_stream(eng, step, begun=0, between=lambda n, i, j: None):
            last_gates = gate_tiles(KT - 1)
            parts = [
                ((pool_tiles + head_tiles(0))[begun:], HEADS - 1, lambda i: head_tiles(i + 1), []),
                ([columns(dram["w_out"], j * P) for j in range(4)], KT // 2 - 2,
                 lambda i: [columns(dram["w_out"], (i + 2) * 2 * P + j * P) for j in range(2)], []),
                (mlp_up(0), MLP_CHUNKS - 1, lambda i: mlp_up(i + 1) + mlp_down(i), mlp_down(MLP_CHUNKS - 1)),
                ([], CT // 2, lambda i: [columns(w_in2, CB2 + i * 2 * P + j * P) for j in range(2)], []),
                (pair_tiles(0)[0:2], PAIRS - 1, lambda p: pair_tiles(p)[2:4] + pair_tiles(p + 1)[0:2],
                 pair_tiles(PAIRS - 1)[2:4] + gate_tiles(0)),
                ([], KT // 2 - 1, lambda i: merge_tiles(i * 2) + merge_tiles(i * 2 + 1),
                 [last_gates[0], branches((KT - 2) * P), last_gates[1], branches((KT - 1) * P)]),
                ([], KT // 2, lambda i: [columns(dram["w_out_2"], i * 2 * P + j * P) for j in range(2)], []),
                (ffn_up(0), FFN_CHUNKS - 1, lambda i: ffn_up(i + 1) + ffn_down(i), ffn_down(FFN_CHUNKS - 1)),
            ]
            n = begun
            for ahead, count, body, behind in parts:
                for halves in ahead:
                    step(n, n % 2, halves)
                    n += 1
                if count:
                    size = len(body(0))
                    assert size % 2 == 0 and n % 2 == 0
                    with eng.Fori(0, count) as i:
                        for j, halves in enumerate(body(i)):
                            step(i * size + (n + j), j % 2, halves)
                            between(n, i, j)
                    n += count * size
                for j, halves in enumerate(behind):
                    step(n, n % 2, halves)
                    between(n - count * size - j, count, j)
                    n += 1
            assert n == T_END

        def arrived(n, slot):
            return (n - slot) * 16 + 32

        @block.sync
        def _(sp):
            def load(n, slot, halves):
                if not isinstance(n, int) or n >= 2:
                    sp.wait_ge(weight_split, n - 1)
                    sp.sem_inc(sp_passed, 1)
                for j, half in enumerate(halves):
                    dst = w_raw[:, slot, j * HALF:(j + 1) * HALF]
                    if len(half.shape) == 3:
                        dst = dst.rearrange("p (k n) -> p k n", n=P)
                    sp.dma_start(dst, half).then_inc(weight_loaded[slot], 16)

            for t in range(KT):
                if t in (1, 3):
                    load(t // 2, t // 2, pool_tiles[t // 2])
                sp.dma_start(x_in[:, t, :], dram["x"][0, t * P:(t + 1) * P, :]).then_inc(x_loaded[t], 16)
            for j in range(2):
                load(T_HEADS + j, j, head_tiles(0)[j])
            sp.dma_start(pool_inv[:, :, :], dram["c_pool_inv"]).then_inc(pool_inv_loaded, 16)
            sp.wait_ge(rows_zeroed, 1)
            for s, stack in enumerate(VECTORS):
                r = 0
                for name, n in stack:
                    if "/" in name:
                        name, tap = name.split("/")
                        src = dram[name][int(tap), :].rearrange("(n c) -> n c", c=P)
                    elif name == "conv_dw_w_2":
                        src = dram[name].rearrange("k (n c) -> n k c", c=P)
                    else:
                        src = dram[name].rearrange("(n c) -> n c", c=P)
                    if len(src.shape) == 3:
                        for t in range(CT):
                            sp.dma_start(stack_rows[t * CONV_K:(t + 1) * CONV_K, s, :], src[t]).then_inc(rows_loaded, 16)
                    else:
                        sp.dma_start(stack_rows[r:r + n, s, :], src).then_inc(rows_loaded, 16)
                    r += n
            weight_stream(sp, load, begun=T_HEADS + 2)

            for t in range(KT):
                sp.wait_ge(out_ready, t + 1)
                sp.dma_start(out[0, t * P:(t + 1) * P, :], y_tok[:, t, :]).then_inc(stored, 16)
            sp.wait_ge(stored, 16 * KT)

        @block.gpsimd
        def _(pool):
            pool.memset(stack_rows[:, :, :], 0.0).then_inc(rows_zeroed, 1)
            pool.memset(rpb_zeros[:, :], 0.0).then_inc(rpb_zeroed, 1)
            pool.memset(ones[:, :], 1.0).then_inc(memsets, 1)
            pool.memset(eps1[:, :], EPS1).then_inc(memsets, 1)
            pool.memset(eps2[:, :], EPS2).then_inc(memsets, 1)

            def split(n, slot, _):
                pool.wait_ge(weight_loaded[slot], arrived(n, slot))
                hi, lo = w_hi[:, slot, :], w_lo[:, slot, :]
                if isinstance(n, int) and n == T_END - 1:
                    pool.wait_ge(tile_done, T_END - 4)
                    hi, lo = w_hi_last[:, :], w_lo_last[:, :]
                elif isinstance(n, int) and n == T_HEADS:
                    pool.wait_ge(x_turned, 2 * KT)
                    hi, lo = w_hi_first[:, :], w_lo_first[:, :]
                elif isinstance(n, int) and n in (T_OUT1 + 2, T_OUT1 + 3):
                    for read in ((k_ready, q_ready), (v_turned, sg_ready))[n - T_OUT1 - 2]:
                        pool.wait_ge(read, HEADS)
                    hi, lo = w_out_parts[n - T_OUT1 - 2]
                elif not isinstance(n, int) or n >= 2:
                    pool.wait_ge(tile_done, n - 1)
                pool.sem_inc(pool_passed, 1)
                pool.tensor_copy(hi, w_raw[:, slot, :]).then_inc(weight_hi, 1)
                pool.wait_ge(weight_hi, n + 1)
                pool.tensor_tensor(lo, w_raw[:, slot, :], hi.bitcast(F32), ALU.subtract).then_inc(weight_split, 1)

            def add_taps(p, taps):
                for k in taps:
                    pool.wait_ge(tap_ready, p * POOL_TAPS + (k + 1))
                    if k >= 2:
                        pool.wait_ge(tap_added, p * (POOL_TAPS - 1) + (k - 1))
                    pool.sem_inc(pool_passed, 1)
                    pool.tensor_tensor(conv_pool[:, :], conv_pool[:, :], tap_product, ALU.add).then_inc(tap_added, 1)

            tap_ends = [1, 2, 3, 4, POOL_TAPS]

            def between(n, i, j):
                if n == T_PAIRS + 2:
                    add_taps(i, range(tap_ends[j], tap_ends[j + 1]))

            weight_stream(pool, split, between=between)

            for t in range(2):
                for d in range(1, KT - 1):
                    half = slice(t * HALF, (t + 1) * HALF)
                    pool.wait_ge(sq_ready, (5 + t) * KT + d + 1)
                    if d >= 2:
                        pool.wait_ge(sq_summed, SUMS_OUT + (KT - 2) * t + d - 1)
                    pool.tensor_tensor(sq_sum[:, half], sq_sum[:, half], sq[:, d % SQ_SLOTS, half], ALU.add)\
                        .then_inc(sq_summed, 1)

        def key_groups(g):
            first, last = max(g - 1, 0), min(g + 1, GROUPS - 1)
            return first, last - first + 1

        def level_parts(tile, level):
            return tile.rearrange("p (n two s) -> p n two s", two=2, s=1 << level)

        @block.tensor
        def _(pe):
            def product(n, slot, first_bank, hi, lo, part=range(KT), split=None, halves=range(2), weights=None):
                w_tile_hi, w_tile_lo = weights or (w_hi[:, slot, :], w_lo[:, slot, :])
                pe.wait_ge(weight_split, n + 1)
                for k in part:
                    if split is not None:
                        pe.wait_ge(*split(k))
                    wh, wl = w_tile_hi[:, k * P:(k + 1) * P], w_tile_lo[:, k * P:(k + 1) * P]
                    for j, (w, a) in enumerate(((wh, hi), (wh, lo), (wl, hi))):
                        for t in halves:
                            last = pe.matmul(psum[:, first_bank + t, :], w, a[:, k, t * HALF:(t + 1) * HALF],
                                             start=(k == 0 and j == 0), stop=(k == KT - 1 and j == 2))
                if part[-1] == KT - 1 and halves[-1] == 1:
                    last.then_inc(tile_done, 1)
                return last

            def down(n, slot, first_group, hi, lo):
                pe.wait_ge(weight_split, n + 1)
                for g in range(8):
                    pe.wait_ge(down_added, first_group + (g + 1))
                    d, t = g // 2, g % 2
                    for k in range(2):
                        at_d = slice(k * HALF + d * P, k * HALF + (d + 1) * P)
                        wh, wl = w_hi[:, slot, at_d], w_lo[:, slot, at_d]
                        for j, (w, a) in enumerate(((wh, hi), (wh, lo), (wl, hi))):
                            last = pe.matmul(psum[:, 4 + g % 4, :], w, a[:, k, t * HALF:(t + 1) * HALF],
                                             start=(k == 0 and j == 0), stop=(k == 1 and j == 2))
                    last.then_inc(down_done if g < 7 else tile_done, 1)

            def sum_features(src, summed, first_bank):
                pe.wait_ge(sq_summed, summed)
                for t in range(2):
                    last = pe.matmul(psum[:, first_bank + t, :], ones[:, :], src[:, t * HALF:(t + 1) * HALF],
                                     start=True, stop=True)
                last.then_inc(norm_summed, 1)

            def normed(first):
                return lambda k: (h_ready, first + k + 1)

            def turn(src, dst_bank, tiles, done):
                for c, block_in in enumerate(tiles):
                    last = pe.transpose(psum[:, dst_bank + c // 4, (c % 4) * P:(c % 4 + 1) * P],
                                        block_in, ident[:, :])
                last.then_inc(done, 1)

            def turn_x(t, bank):
                pe.wait_ge(x_loaded[t], 16)
                for d in range(0, KT, 4):
                    turn(x_in, bank + d // 4, [x_in[:, t, (d + c) * P:(d + c + 1) * P] for c in range(4)], x_turned)

            def x_in_sbuf(t):
                pe.wait_ge(x_copied, t + 1)
                pe.wait_ge(x_copied_rest, t + 1)

            def pool_product(j, q):
                pe.wait_ge(weight_split, T_POOL + j + 1)
                tokens = slice(q * QUARTER, (q + 1) * QUARTER)
                dst = psum[:, 2 * j + q // 2, (q % 2) * QUARTER:(q % 2 + 1) * QUARTER]
                for k in range(KT):
                    pe.wait_ge(h_ready, H_MIX1 + KT * q + k + 1)
                    wh, wl = w_hi[:, j, k * P:(k + 1) * P], w_lo[:, j, k * P:(k + 1) * P]
                    for i, (w, a) in enumerate(((wh, h_hi), (wh, h_lo), (wl, h_hi))):
                        last = pe.matmul(dst, w, a[:, k, tokens], start=(k == 0 and i == 0), stop=(k == KT - 1 and i == 2))
                if q == SEQ // QUARTER - 1:
                    last.then_inc(tile_done, 1)

            pe.wait_ge(consts_loaded, 16)
            pe.wait_ge(gain_loaded, 16)
            pe.transpose(psum[:, 7, 0:KT], gain_rows[:, :], ident[0:KT, 0:KT]).then_inc(gain_turned, 1)
            for t in range(4):
                if t == 3:
                    pe.wait_ge(gain_ready, 1)
                turn_x(t, 2 * t)
            x_in_sbuf(0)
            pool_product(0, 0)
            for t in range(4, KT):
                x_in_sbuf(t - 2)
                turn_x(t, 4 + 2 * (t % 2))
                if t == 5:
                    pool_product(0, 1)
                    pool_product(1, 0)
            pool_product(1, 1)
            for q in range(2, 4):
                for j in range(2):
                    pool_product(j, q)

            def project_f(h):
                pe.wait_ge(zv_ready, h)
                product(h * 4 + T_HEADS, 0, 0, h_hi, h_lo)

            def project_q(h, part=range(KT)):
                pe.wait_ge(zg_ready, h)
                product(h * 4 + (T_HEADS + 1), 1, 2, h_hi, h_lo, part)

            def project_i(h, part=range(KT)):
                pe.wait_ge(zf_ready, h + 1)
                product(h * 4 + (T_HEADS + 2), 0, 0, h_hi, h_lo, part)

            def project_g(h):
                pe.wait_ge(zq_ready, h + 1)
                product(h * 4 + (T_HEADS + 3), 1, 2, h_hi, h_lo)

            first_half, second_half = range(KT // 2), range(KT // 2, KT)

            def head(h, meanwhile):
                def level(l, bank):
                    pe.wait_ge(level_ready, h * LEVELS + (l + 1))
                    keys = CHUNK if l < LEVELS - 1 else CHUNK // 2
                    for c in range(NC):
                        e = e_t[:, l % 2, c * CHUNK:(c + 1) * CHUNK]
                        last = pe.matmul(psum[0:keys, bank, c * (CHUNK // 2):(c + 1) * (CHUNK // 2)], e[:, 0:keys],
                                         level_parts(e, l)[:, :, 1, :], start=True, stop=True)
                    last.then_inc(level_done, 1)

                def merged_up_to(l):
                    pe.wait_ge(level_merged, h * (LEVELS + 1) + (l + 2))

                meanwhile[0]()
                pe.wait_ge(o_scaled, h + 1)
                pe.wait_ge(k_ready, h + 1)
                pe.wait_ge(q_ready, h + 1)
                for c in range(NC):
                    last = pe.matmul(psum[:, 6 + c // 4, (c % 4) * P:(c % 4 + 1) * P],
                                     k_t[:, c * CHUNK:(c + 1) * CHUNK], q_t[:, c * CHUNK:(c + 1) * CHUNK],
                                     start=True, stop=True)
                last.then_inc(level_done, 1)
                pe.wait_ge(o_log, h + 1)
                level(0, 4)
                level(1, 5)
                meanwhile[1]()
                pe.wait_ge(zv_ready, h + 1)
                merged_up_to(-1)
                turn(zv, 6, [zv[:, c * P:(c + 1) * P] for c in range(NC)], v_turned)
                merged_up_to(0)
                level(2, 4)
                merged_up_to(1)
                level(3, 5)
                meanwhile[2]()
                pe.wait_ge(v_ready, h + 1)
                level(4, 6)
                merged_up_to(2)
                level(5, 4)
                meanwhile[3]()
                merged_up_to(3)
                level(6, 5)
                pe.wait_ge(level_moved, h * LEVELS + LEVELS)
                merged_up_to(4)
                turn(kd_t, 6, [kd_t[:, c * P:(c + 1) * P] for c in range(NC)], kd_turned)
                meanwhile[4]()
                pe.wait_ge(kd_tok_ready, h + 1)
                merged_up_to(6)
                for c in range(NC - 1):
                    last = pe.matmul(psum[:, 4 + c // 4, (c % 4) * P:(c % 4 + 1) * P], kd_tok[:, c, :],
                                     v_tok[:, c, :], start=True, stop=True)
                last.then_inc(update_done, 1)
                meanwhile[5]()
                pe.wait_ge(state_ready, h * (NC - 1) + (NC - 1))
                for c in range(NC):
                    o = psum[:, 6 + c // 4, (c % 4) * P:(c % 4 + 1) * P]
                    tokens = slice(c * CHUNK, (c + 1) * CHUNK)
                    last = pe.matmul(o, v_tok[:, c, :], s_t[:, tokens], start=True, stop=(c == 0))
                    if c >= 1:
                        last = pe.matmul(o, states[:, c, :], qd_t[:, tokens], start=False, stop=True)
                last.then_inc(o_done, 1)
                meanwhile[6]()
                pe.wait_ge(o_sq, h + 1)
                for t in range(2):
                    last = pe.matmul(psum[:, 4 + t, :], ones[:, :], e_t[:, 1, t * HALF:(t + 1) * HALF],
                                     start=True, stop=True)
                last.then_inc(o_mean, 1)
                meanwhile[7]()

            def between_steps(h):
                return [lambda: project_g(h), lambda: project_f(h + 1),
                        lambda: project_q(h + 1, first_half), lambda: project_q(h + 1, second_half),
                        lambda: project_i(h + 1, range(0, 3)), lambda: project_i(h + 1, range(3, 6)),
                        lambda: project_i(h + 1, [6]), lambda: project_i(h + 1, [7])]

            first_weights = w_hi_first[:, :], w_lo_first[:, :]
            product(T_HEADS, 0, 6, h_hi, h_lo, first_half, weights=first_weights)
            pe.wait_ge(memsets, 3)
            sum_features(sq_sum, SUMS_MIX1 + 2 * (KT - 1), 4)
            product(T_HEADS, 0, 6, h_hi, h_lo, second_half, weights=first_weights)
            pe.wait_ge(mean_log, 1)
            product(T_HEADS + 1, 1, 4, h_hi, h_lo)
            pe.wait_ge(rows_loaded, 16 * (sum(len(stack) for stack in VECTORS) + CT - 1))
            pe.wait_ge(pool_u_ready, 2)
            turn(stack_rows, 2, [stack_rows[:, s, :] for s in range(4)], cols_turned)
            project_i(0)
            pe.wait_ge(pool_loaded, 16 * 5)
            pe.wait_ge(zf_ready, 1)
            pe.wait_ge(zq_ready, 1)
            pe.wait_ge(cols_ready, 1)
            for j in range(2):
                pe.wait_ge(pool_p_ready, j + 1)
                for t in range(2):
                    last = pe.matmul(psum[:, 4 + 2 * j + t, :], pool_w[:, j, :],
                                     pool_p[:, j, t * HALF:(t + 1) * HALF], start=True, stop=True)
                last.then_inc(pool_mixed, 1)
            pe.wait_ge(pool_ready, 2)
            with pe.Fori(0, HEADS - 1) as i:
                head(i, between_steps(i))

            def out_tile(t, part):
                product(T_OUT1 + t, t % 2, 2 * t, h_hi, h_lo, part, split=lambda k: (mix_split, k + 1),
                        weights=None if t < 2 else w_out_parts[t - 2])

            def begin_out(t, part):
                pe.wait_ge(*((zv_ready, HEADS), (zg_ready, HEADS), (o_log, HEADS + 1))[t])
                out_tile(t, part)

            def begin_rest():
                begin_out(1, range(5, 7))
                begin_out(2, range(7))

            head(HEADS - 1, [lambda: project_g(HEADS - 1), lambda: begin_out(0, range(0, 4)),
                             lambda: begin_out(0, range(4, 7)), lambda: begin_out(1, [0]), lambda: begin_out(1, [1]),
                             lambda: begin_out(1, [2, 3]), lambda: begin_out(1, [4]), begin_rest])
            for t in range(3):
                out_tile(t, [KT - 1])
            pe.wait_ge(o_scaled, HEADS + 1)
            out_tile(3, range(KT))

            def project_out(count, first_tile, first_added):
                def tile(i, s, halves):
                    pe.wait_ge(x_added, i * 2 + (first_added + s + 1))
                    return product(i * 2 + (first_tile + s), s, 2 * s, h_hi, h_lo, halves=halves)

                with pe.Fori(0, count - 1) as i:
                    for s in range(2):
                        tile(i, s, range(2))
                tile(count - 1, 0, range(2))
                tile(count - 1, 1, [0]).then_inc(out_half_done, 1)
                tile(count - 1, 1, [1])

            def product_by_halves(n, first_h):
                for t in range(2):
                    product(n, 0, 0, h_hi, h_lo, halves=[t],
                            split=lambda k: (h_ready, first_h + HALVES.index((k, t)) + 1))

            project_out(KT // 2 - 2, T_OUT1 + 4, 4)

            def up_product(n, slot, tile, read, first_bank):
                pe.wait_ge(read, tile + 1)
                product(n, slot, first_bank, h_hi, h_lo)

            def mlp_up_part(c, n):
                for j in range(2):
                    up_product(n + j, j, c * 2 + j, up_read, 2 * j)

            def mlp_down_part(c, n, hi=mlp_hi, lo=mlp_lo):
                pe.wait_ge(act_split, c * 2 + 4)
                for j in range(2):
                    down(n + j, j, c * 16 + 8 * j, hi, lo)

            product_by_halves(T_MLP, H_MLP)
            sum_features(sq_sum, SUMS_MLP + KT - 1, 4)
            product(T_MLP + 1, 1, 2, h_hi, h_lo)
            with pe.Fori(0, MLP_CHUNKS - 2) as i:
                mlp_up_part(i + 1, i * 4 + (T_MLP + 2))
                mlp_down_part(i, i * 4 + (T_MLP + 4))
            mlp_up_part(MLP_CHUNKS - 1, T_CB - 6)
            mlp_down_part(MLP_CHUNKS - 2, T_CB - 4)
            mlp_down_part(MLP_CHUNKS - 1, T_CB - 2, mlp_hi_last, mlp_lo_last)

            product(T_CB, 0, 0, h_hi, h_lo, split=normed(H_MIX2))
            product(T_CB + 1, 1, 2, h_hi, h_lo, range(KT // 2))
            sum_features(sq_sum, SUMS_MIX2 + KT + 3, 4)
            product(T_CB + 1, 1, 2, h_hi, h_lo, range(KT // 2, KT))
            sum_features(sq_sum_gain, SUMS_MIX2 + 2 * KT - 1, 6)
            pe.wait_ge(mean_log, 3)
            product(T_CB + 2, 0, 4, h_hi, h_lo)
            pe.wait_ge(block_mean, 1)
            product(T_CB + 3, 1, 6, h_hi, h_lo)

            def scores(p, s):
                g, head_rows = s // 2, slice(DH * (s % 2), DH * (s % 2 + 1))
                first, n = key_groups(g)
                pe.wait_ge(scores_max, p * UNITS + (s + 1))
                for j, (q, k) in enumerate(((q_hi, k_hi), (q_hi, k_lo), (q_lo, k_hi))):
                    last = pe.matmul(psum[:, 4 + s % 2, 0:n * P], q[head_rows, g * P:(g + 1) * P],
                                     k[head_rows, first * P:(first + n) * P], start=(j == 0), stop=(j == 2))
                last.then_inc(scores_done, 1)

            def turn_probabilities(p, s):
                pe.wait_ge(prob_ready, p * UNITS + (s + 1))
                pe.wait_ge(prob_t_ready, p * UNITS + (s + 1))
                _, n = key_groups(s // 2)
                turn(prob, 6 + s % 2, [prob[:, s % 3, c * P:(c + 1) * P] for c in range(n)], prob_turned)

            def weigh_values(p, s):
                first, n = key_groups(s // 2)
                pe.wait_ge(prob_t_ready, p * UNITS + (s + 3))
                pe.wait_ge(att_ready, p * 4 + (s // 4 + 3))
                for c in range(n):
                    last = pe.matmul(psum[:, (s // 4) % 2, (s % 4) * P:(s % 4 + 1) * P], v_keys[:, first + c, :],
                                     prob_t[:, s % 2, c * P:(c + 1) * P], start=(c == 0), stop=(c == n - 1))
                last.then_inc(prob_t_used, 1)

            pe.wait_ge(cb_read, 2)
            product(T_PAIRS, 0, 2, h_hi, h_lo)
            with pe.Fori(0, PAIRS) as p:
                pe.wait_ge(att_ready, p * 4 + 4)
                product(p * 4 + (T_PAIRS + 1), 1, 0, h_hi, h_lo)
                pe.wait_ge(u_read, p + 1)
                product(p * 4 + (T_PAIRS + 2), 0, 2, h_hi, h_lo)
                pe.wait_ge(q_read, p + 1)
                product(p * 4 + (T_PAIRS + 3), 1, 0, h_hi, h_lo, range(KT - 2))
                pe.wait_ge(cb_read, CT)
                pe.wait_ge(q_split, p + 1)
                pe.wait_ge(k_split, p + 1)
                for s in range(2):
                    scores(p, s)
                product(p * 4 + (T_PAIRS + 3), 1, 0, h_hi, h_lo, range(KT - 2, KT))
                for s in range(2, UNITS + 4):
                    if s < UNITS:
                        scores(p, s)
                    if s < UNITS + 2:
                        turn_probabilities(p, s - 2)
                    if s == 2:
                        pe.wait_ge(k_read, p + 1)
                        pe.wait_ge(v_read, p + 1)
                        turn(v_t, 0, [v_t[:, g * P:(g + 1) * P] for g in range(GROUPS)], v_tiles_turned)
                    if s == 4:
                        pe.wait_ge(v_tiles_ready, p + 1)
                    if s >= 4:
                        weigh_values(p, s - 4)
                    if s in NEXT_AFTER:
                        product(p * 4 + (T_PAIRS + 4), 0, 2, h_hi, h_lo, NEXT_AFTER[s])

            def gate_a(d, n, slot, part=range(KT)):
                pe.wait_ge(gate_a_read, d)
                product(n, slot, 2, h_hi, h_lo, part)

            def gate_b(d, n, slot, part=range(KT)):
                if not isinstance(d, int) or d >= 1:
                    pe.wait_ge(gate_b_read, d)
                product(n, slot, 0, h_hi, h_lo, part)

            def both_branches(d, n, slot):
                pe.wait_ge(weight_split, n + 1)
                for branch, split, read, bank, hi, lo in ((0, PAIRS, branch_a, 4, att_hi, att_lo),
                                                          (1, PAIRS + CT, branch_b, 6, conv_hi, conv_lo)):
                    pe.wait_ge(branch_split, split)
                    pe.wait_ge(read, d + 1)
                    for k in range(4):
                        at_k = slice((4 * branch + k) * P, (4 * branch + k + 1) * P)
                        wh, wl = w_hi[:, slot, at_k], w_lo[:, slot, at_k]
                        for j, (w, a) in enumerate(((wh, hi), (wh, lo), (wl, hi))):
                            for t in range(2):
                                last = pe.matmul(psum[:, bank + t, :], w, a[:, k, t * HALF:(t + 1) * HALF],
                                                 start=(k == 0 and j == 0), stop=(k == 3 and j == 2))
                last.then_inc(tile_done, 1)

            def merge_step(d, n, slot):
                gate_a(d + 1, n, slot)
                gate_b(d + 1, n + 1, 1 - slot)
                both_branches(d, n + 2, slot)

            pe.wait_ge(att_ready, 4 + 4 * PAIRS)
            def sum_channels(src, added, first_bank, done):
                pe.wait_ge(ln_added, added)
                for t in range(2):
                    last = pe.matmul(psum[:, first_bank + t, :], ones[:, :], src[:, t * HALF:(t + 1) * HALF],
                                     start=True, stop=True)
                last.then_inc(done, 1)

            gate_b(0, T_MERGE + 1, 1)
            sum_channels(ln_inv, CT - 1, 4, ln_summed)
            gate_a(1, T_MERGE + 2, 0)
            sum_channels(ln_sq[:, 0, :], 2 * (CT - 1), 6, ln_var)
            gate_b(1, T_MERGE + 3, 1)
            both_branches(0, T_MERGE + 4, 0)
            merge_step(1, T_MERGE + 5, 1)
            with pe.Fori(1, KT // 2 - 1) as i:
                for s in range(2):
                    merge_step(i * 2 + s, i * 6 + (T_MERGE + 2 + 3 * s), s)
            gate_a(KT - 1, T_OUT2 - 4, 0)
            both_branches(KT - 2, T_OUT2 - 3, 1)
            gate_b(KT - 1, T_OUT2 - 2, 0)
            both_branches(KT - 1, T_OUT2 - 1, 1)

            pe.wait_ge(gate_b_read, KT)
            product(T_OUT2, 0, 0, h_hi, h_lo, split=lambda k: (mix_split, KT + k + 1))
            product(T_OUT2 + 1, 1, 2, h_hi, h_lo)
            project_out(KT // 2 - 1, T_OUT2 + 2, KT + 2)

            def ffn_up_part(c, n):
                for j in range(4):
                    up_product(n + j, j % 2, c * 4 + j, ffn_read, 2 * (j % 2))

            def ffn_down_part(c, n):
                pe.wait_ge(act_split, c * 2 + (2 * MLP_CHUNKS + 4))
                for j in range(2):
                    down(n + j, j, c * 16 + (16 * MLP_CHUNKS + 8 * j), ffn_hi, ffn_lo)

            product_by_halves(T_FFN, H_FFN)
            sum_features(sq_sum, SUMS_FFN + KT - 1, 4)
            product(T_FFN + 1, 1, 2, h_hi, h_lo)
            for j in range(2, 4):
                up_product(T_FFN + j, j % 2, j, ffn_read, 2 * (j % 2))
            with pe.Fori(0, FFN_CHUNKS - 2) as i:
                ffn_up_part(i + 1, i * 6 + (T_FFN + 4))
                ffn_down_part(i, i * 6 + (T_FFN + 8))
            ffn_up_part(FFN_CHUNKS - 1, T_END - 8)
            ffn_down_part(FFN_CHUNKS - 2, T_END - 4)

            last_groups = 16 * (MLP_CHUNKS + FFN_CHUNKS - 1)

            def turn_back(i):
                pe.wait_ge(down_added, 4 + last_groups + i + 1)
                if i >= 3:
                    pe.wait_ge(y_copied, i - 2)
                d, t = i % KT, i // KT
                turn(x_t, i % 3, [x_t[:, d, t * HALF + c * P:t * HALF + (c + 1) * P] for c in range(4)], y_turned)

            def sum_tokens(t):
                pe.wait_ge(sq_summed, SUMS_OUT + (KT - 2) * (t + 1))
                pe.wait_ge(sq_ready, (5 + t) * KT + KT)
                for c in range(4 * t, 4 * t + 4):
                    tokens = slice(c * P, (c + 1) * P)
                    pe.matmul(psum[:, 3, c:c + 1], sq_sum[:, tokens], ones[:, 0:1], start=True, stop=False)
                    last = pe.matmul(psum[:, 3, c:c + 1], sq[:, (KT - 1) % SQ_SLOTS, tokens], ones[:, 0:1],
                                     start=False, stop=True)
                last.then_inc(norm_summed, 1)

            pe.wait_ge(act_split, 2 * (MLP_CHUNKS + FFN_CHUNKS) + 2)
            for i in range(2 * KT):
                d, t = i % KT, i // KT
                pe.wait_ge(weight_split, T_END if i >= 4 else T_END - 1)
                pe.wait_ge(down_added, last_groups + i + 1)
                for k in range(2):
                    at_d = slice(k * HALF + d % 4 * P, k * HALF + (d % 4 + 1) * P)
                    wh, wl = (w_hi[:, 0, at_d], w_lo[:, 0, at_d]) if d < 4 else (w_hi_last[:, at_d], w_lo_last[:, at_d])
                    for j, (w, a) in enumerate(((wh, ffn_hi_last), (wh, ffn_lo_last), (wl, ffn_hi_last))):
                        last = pe.matmul(psum[:, 4 + i % 4, :], w, a[:, k, t * HALF:(t + 1) * HALF],
                                         start=(k == 0 and j == 0), stop=(k == 1 and j == 2))
                last.then_inc(down_done, 1)
                if i >= 2:
                    turn_back(i - 2)
                if i == KT + 2:
                    sum_tokens(0)
            turn_back(2 * KT - 2)
            turn_back(2 * KT - 1)
            sum_tokens(1)

        @block.scalar
        def _(act):
            def square(d, first_sum, part=slice(0, SEQ)):
                if d > SQ_SLOTS:
                    act.wait_ge(sq_summed, first_sum + d - SQ_SLOTS)
                dst = sq[:, d % SQ_SLOTS, part] if d else sq_sum[:, part]
                act.activation(dst, x_t[:, d, part], ACT.Square).then_inc(sq_ready, 1)

            def inverse(m, norm, eps):
                act.wait_ge(norm_summed, norm)
                act.activation(rinv[:, :], banks(4), ACT.Ln, scale=1.0 / D, bias=eps[:, :]).then_inc(mean_log, 1)
                act.wait_ge(mean_log, m + 1)
                act.activation(rinv[:, :], rinv[:, :], ACT.Exp, scale=-0.5).then_inc(rinv_ready, 1)

            def hi_part(d, gain, part=slice(0, SEQ)):
                act.activation(h_hi[:, d, part], x_t[:, d, part], ACT.Copy, scale=gain).then_inc(h_hi_ready, 1)

            act.dma_start(ident[:, :], dram["c_ident"]).then_inc(consts_loaded, 16)
            act.dma_start(gain_rows[:, :], dram["norm_mix_g"].rearrange("(k p) -> k p", p=P)).then_inc(gain_loaded, 16)
            act.dma_start(rpb_rows[RPB_PAD:RPB_PAD + NA_HEADS * RPB_H, :],
                          dram["rpb_2"].rearrange("h r c -> (h r) c")).then_inc(rpb_stored, 16)

            def x_bank(t):
                return 2 * t if t < 4 else 4 + 2 * (t % 2)

            def take_x(t):
                act.wait_ge(x_turned, 2 * t + 1)
                act.activation(x_t[:, 0:4, t * P:(t + 1) * P],
                               psum[:, x_bank(t), :].rearrange("p (d t) -> p d t", t=P), ACT.Copy).then_inc(x_copied, 1)

            def split_x(q):
                act.wait_ge(x_copied, 2 * q + 2)
                act.wait_ge(x_copied_rest, 2 * q + 2)
                for d in range(KT):
                    hi_part(d, first_gain[:, d:d + 1], slice(q * QUARTER, (q + 1) * QUARTER))

            act.wait_ge(gain_turned, 1)
            act.activation(first_gain[:, :], psum[:, 7, 0:KT], ACT.Copy).then_inc(gain_ready, 1)
            act.wait_ge(gain_ready, 1)
            for q in range(4):
                take_x(2 * q)
                take_x(2 * q + 1)
                split_x(q)
                if q == 2:
                    for d in range(4):
                        square(d, SUMS_MIX1, slice(0, HALF))
            for d in range(4, KT):
                square(d, SUMS_MIX1, slice(0, HALF))
            for d in range(KT):
                square(d, SUMS_MIX1 + KT - 1, slice(HALF, SEQ))
            act.wait_ge(rpb_zeroed, 1)
            for r in (0, RPB_PAD + NA_HEADS * RPB_H):
                act.dma_start(rpb_rows[r:r + RPB_PAD, :], rpb_zeros[:, :]).then_inc(rpb_stored, 16)
            act.dma_start(x_spill, x_t[:, :, :].rearrange("p d t -> p (d t)")).then_inc(x_spilled, 16)
            inverse(0, 1, eps1)
            act.wait_ge(pool_w_zeroed, 1)
            for g in range(4):
                half = slice(64 * (g % 2), 64 * (g % 2) + 64)
                act.dma_start(pool_w[half, g // 2, half], dram["pool_w"][g, :, :]).then_inc(pool_loaded, 16)
            act.dma_start(pair_mask[:, :], dram["c_pair_mask"]).then_inc(pool_loaded, 16)

            act.wait_ge(rpb_stored, 16 * 3)
            for h in range(NA_HEADS):
                by_distance = bass.AP(rpb_rows.tensor, h * RPB_H * RPB_W + SHIFTS - 1,
                                      [[RPB_W, SHIFT_ROWS], [-1, SHIFTS], [1, GROUP_W]])
                act.dma_start(shifted[h, :, :, :].rearrange("i r c -> r i c"), by_distance).then_inc(shifted_stored, 16)

            act.wait_ge(cols_turned, 1)
            act.activation(cols[:, :], psum[:, 2, :], ACT.Copy).then_inc(cols_ready, 1)
            act.wait_ge(x_spilled, 16)
            for j in range(2):
                act.wait_ge(pool_mixed, j + 1)
                act.activation(mix1[:, j, :], banks(4 + 2 * j), ACT.Copy,
                               scale=col("pool_scale", j)).then_inc(pool_ready, 1)

            def mix_hi(d, mix, ready):
                act.wait_ge(*ready)
                act.activation(h_hi[:, d, :], mix[:, d, :], ACT.Copy).then_inc(mix_hi_ready, 1)

            def mix1_hi(d):
                mix_hi(d, mix1, (pool_ready, d + 1) if d < 2 else (y_ready, d))

            def head(h, last):
                def level(l):
                    if l == 0:
                        act.wait_ge(qd_start, h + 1)
                    else:
                        act.wait_ge(level_moved, h * LEVELS + l)
                    if l >= 2:
                        act.wait_ge(level_done, h * (LEVELS + 1) + l)
                    e = level_parts(e_t[:, l % 2, :], l)
                    act.activation(e[:, :, 0, :], level_parts(kd_t[:, :], l)[:, :, 0, :], ACT.Copy)
                    act.activation(e[:, :, 1, :], level_parts(qd_t[:, :], l)[:, :, 1, :], ACT.Copy)\
                       .then_inc(level_ready, 1)

                def begin_mix(*tiles):
                    if last:
                        for d in tiles:
                            mix1_hi(d)

                act.wait_ge(zq_ready, h + 1)
                act.activation(q_t[:, :], zq[:, :], ACT.Sigmoid).then_inc(q_gate, 1)
                act.wait_ge(zf_ready, h + 1)
                act.activation(decays[:, 0:SEQ], zf[:, :], ACT.Sigmoid).then_inc(f_ready, 1)
                act.activation(kd_t[:, :], zf[:, :], ACT.Sigmoid, scale=-1.0).then_inc(kd_start, 1)
                act.activation(k_t[:, :], zf[:, :], ACT.Sigmoid, scale=-1.0).then_inc(k_ready, 1)
                act.wait_ge(kd_start, h + 1)
                level(0)
                level(1)
                act.wait_ge(y_ready, h + 1)
                act.wait_ge(zg_ready, h + 1)
                act.activation(sg_t[:, :], zg[:, :], ACT.Sigmoid).then_inc(g_gate, 1)
                if last:
                    act.wait_ge(tile_done, T_OUT1)
                begin_mix(0, 1)
                level(2)
                begin_mix(2, 3, 4, 5, 6)
                level(3)
                act.wait_ge(v_turned, h + 1)
                act.activation(v_tok[:, :, :].rearrange("p c v -> p (c v)"), banks(6), ACT.Copy).then_inc(v_ready, 1)
                if last:
                    act.wait_ge(mix_split, KT - 1)
                    act.dma_start(x_t[:, 0:KT - 1, :].rearrange("p d t -> p (d t)"),
                                  x_spill[:, 0:(KT - 1) * SEQ]).then_inc(x_back, 16)
                level(4)
                level(5)
                level(6)
                act.wait_ge(kd_turned, h + 1)
                act.activation(kd_tok[:, :, :].rearrange("p c k -> p (c k)"), banks(6), ACT.Copy)\
                   .then_inc(kd_tok_ready, 1)
                act.wait_ge(o_done, h + 1)
                act.activation(e_t[:, 1, :], banks(6), ACT.Square).then_inc(o_sq, 1)
                act.wait_ge(o_mean, h + 1)
                act.activation(e_t[:, 0, :], banks(4), ACT.Ln, scale=1.0 / P, bias=eps1[:, :]).then_inc(o_log, 1)
                act.wait_ge(o_log, h + 2)
                act.activation(e_t[:, 0, :], e_t[:, 0, :], ACT.Exp, scale=-0.5).then_inc(o_inv, 1)

            with act.Fori(0, HEADS - 1) as i:
                head(i, False)
            head(HEADS - 1, True)
            mix1_hi(KT - 1)
            act.wait_ge(mix_split, KT)
            act.dma_start(x_t[:, KT - 1, :], x_spill[:, (KT - 1) * SEQ:]).then_inc(x_back_last, 16)

            def split_activations(a, hi, first, after):
                if after is not None:
                    act.wait_ge(tile_done, after)
                for j in range(2):
                    act.wait_ge(act_ready, first + (j + 1))
                    act.activation(hi[:, j, :], a[:, j, :], ACT.Copy).then_inc(act_hi_ready, 1)

            def mlp_square(c):
                for j in range(2):
                    act.wait_ge(up_read, c * 2 + (2 + j + 1))
                    act.activation(mlp_a[:, j, :], mlp_a[:, j, :], ACT.Square).then_inc(act_ready, 1)

            def next_norm(m, norm, first_added, first_sum, halves_done, last_use, gain, eps):
                for d in range(KT - 1):
                    act.wait_ge(x_added, first_added + d + 1)
                    square(d, first_sum)
                def hi_half(d, t):
                    if d == KT - 1:
                        act.wait_ge(x_added, first_added + KT)
                    hi_part(d, col(gain, d), slice(t * HALF, (t + 1) * HALF))

                act.wait_ge(out_half_done, halves_done)
                for d, t in HALVES_AHEAD:
                    hi_half(d, t)
                act.wait_ge(tile_done, last_use)
                for d, t in HALVES_BEHIND:
                    hi_half(d, t)
                square(KT - 1, first_sum)
                inverse(m, norm, eps)

            next_norm(1, 2, 2, SUMS_MLP, 1, T_MLP, "norm_mlp_g", eps1)
            mlp_square(0)
            split_activations(mlp_a, mlp_hi, 0, None)
            act.wait_ge(shifted_stored, 16 * NA_HEADS)
            step = SHIFT_ROWS * GROUP_W
            for h in range(NA_HEADS):
                for m in range(3):
                    near = bass.AP(shifted.tensor, ((h + 1) * SHIFTS - GROUP_W * (m + 1)) * step + (ROWS - 1) * GROUP_W,
                                   [[step, GROUP_W], [-GROUP_W, ROWS], [1, P]])
                    act.dma_start(bias_rows[h // 2, :, h % 2, m, :].rearrange("(r c) k -> c r k", c=GROUP_W), near)\
                       .then_inc(bias_stored, 16)
            with act.Fori(0, MLP_CHUNKS - 2) as i:
                mlp_square(i + 1)
                split_activations(mlp_a, mlp_hi, i * 2 + 2, i * 4 + (T_MLP + 6))
            mlp_square(MLP_CHUNKS - 1)
            split_activations(mlp_a, mlp_hi_last, 2 * MLP_CHUNKS - 2, None)

            def down_x(d):
                act.wait_ge(down_added, 4 + 16 * (MLP_CHUNKS - 1) + 2 * (d + 1))

            act.wait_ge(tile_done, T_CB - 2)
            for d in range(4):
                down_x(d)
                hi_part(d, gain_both[:, d:d + 1])
                square(d, SUMS_MIX2)
            for d in range(4, KT):
                down_x(d)
                hi_part(d, gain_both[:, d:d + 1])
            for d in range(4, KT):
                square(d, SUMS_MIX2 + d - SQ_SLOTS - 1)
            act.wait_ge(norm_summed, 3)
            act.activation(rinv1[:, :], banks(4), ACT.Ln, scale=1.0 / D, bias=eps1[:, :]).then_inc(mean_log, 1)
            act.wait_ge(mean_log, 3)
            act.activation(rinv[:, :], rinv1[:, :], ACT.Exp, scale=-1.0)
            act.activation(rinv1[:, :], rinv1[:, :], ACT.Exp, scale=-0.5).then_inc(block_rinv1, 1)
            act.wait_ge(block_mean, 1)
            act.activation(rinv[:, :], rinv[:, :], ACT.Ln, scale=1.0 / D, bias=eps2[:, :]).then_inc(mean_log, 1)
            act.wait_ge(mean_log, 4)
            act.activation(rinv[:, :], rinv[:, :], ACT.Exp, scale=-0.5).then_inc(rinv_ready, 1)

            for c in range(CT):
                act.wait_ge(cb_read, c + 1)
                act.activation(sig_cb[:, c, :], sig_cb[:, c, :], ACT.Sigmoid, bias=col("b_in_2", CB2 // P + c))\
                   .then_inc(cb_ready, 1)
                if c == 1:
                    for d in range(0, KT, KT // SPILLS):
                        act.wait_ge(x_ready, d + KT // SPILLS)
                        act.dma_start(x_spill[:, d * SEQ:(d + KT // SPILLS) * SEQ],
                                      x_t[:, d:d + KT // SPILLS, :].rearrange("p d t -> p (d t)")).then_inc(x_spilled, 16)

            act.wait_ge(bias_stored, 16 * 3 * NA_HEADS)
            act.dma_start(near_mask[:, :, :], dram["c_near_mask"]).then_inc(mask_loaded, 16)
            with act.Fori(0, PAIRS) as p:
                act.wait_ge(scores_max, p * UNITS + 2)
                act.dma_start(bias_raw[:, :, :, :].rearrange("p j m k -> p (j m k)"),
                              bias_rows[bass.ds(p, 1), :, :, :, :].rearrange("a q j m k -> (a q) (j m k)"))\
                   .then_inc(bias_loaded, 16)
                def tap_products(taps):
                    for k in taps:
                        if k == 0:
                            act.wait_ge(u_ready, p + 1)
                        elif k >= 2:
                            act.wait_ge(tap_added, p * (POOL_TAPS - 1) + (k - 1))
                        act.activation(tap_product if k else conv_pool[:, :], u_t[:, DVE_TAPS + k:DVE_TAPS + k + SEQ],
                                       ACT.Copy, scale=col("conv_dw_w_2", p * CONV_K + (DVE_TAPS + k)))\
                           .then_inc(tap_ready, 1)

                tap_products([0, 1])
                act.wait_ge(q_read, p + 1)
                act.activation(qk32[:, :], qk32[:, :], ACT.Identity, scale=DH ** -0.5, bias=q_bias[:, bass.ds(p, 1)])\
                   .then_inc(q32_ready, 1)
                act.wait_ge(q32_ready, p + 1)
                act.activation(q_hi[:, :], qk32[:, :], ACT.Copy).then_inc(q_hi_ready, 1)
                tap_products([2])
                act.wait_ge(k_read, p + 1)
                act.activation(qk32[:, :], qk32[:, :], ACT.Identity, bias=col("b_in_2", p + K2 // P))\
                   .then_inc(k32_ready, 1)
                act.wait_ge(k32_ready, p + 1)
                act.activation(k_hi[:, :], qk32[:, :], ACT.Copy).then_inc(k_hi_ready, 1)
                tap_products([3])
                for s in range(UNITS + 5):
                    if s < UNITS:
                        act.wait_ge(neg_max_ready, p * UNITS + (s + 1))
                        exponents = prob[:, s % 3, 0:key_groups(s // 2)[1] * P]
                        act.activation(exponents, exponents, ACT.Exp, bias=neg_max[:, s % 2:s % 2 + 1],
                                       accum_out=row_sum[:, s % 2:s % 2 + 1]).then_inc(prob_exp, 1)
                    if 2 <= s < UNITS + 2:
                        u = s - 2
                        act.wait_ge(prob_turned, p * UNITS + (u + 1))
                        act.wait_ge(prob_t_used, p * UNITS + (u + 1))
                        n = key_groups(u // 2)[1] * P
                        act.activation(prob_t[:, u % 2, 0:n], psum[:, 6 + u % 2, 0:n], ACT.Copy).then_inc(prob_t_ready, 1)
                    if s == 2:
                        act.wait_ge(v_tiles_turned, p + 1)
                        act.activation(v_keys[:, :, :].rearrange("p g v -> p (g v)"), banks(0), ACT.Copy)\
                           .then_inc(v_tiles_ready, 1)
                    if s in (4, 7, 10, 13):
                        tap_products([4 + (s - 4) // 3])
                    if s >= 5 and (s - 5) % 4 == 3:
                        b = (s - 5) // 4
                        act.wait_ge(x_spilled, 16 * (1 + SPILLS))
                        act.wait_ge(prob_t_used, p * UNITS + (2 + 4 * b + 4))
                        for j in range(2):
                            half = slice(DH * j, DH * (j + 1))
                            dst = att_t[half, bass.ds(p, 1), :].rearrange("p a (r g c) -> p g (a r) c", g=GROUPS, c=GROUP_W)
                            src = psum[half, b % 2, :].rearrange("p (g j r c) -> p g j r c", g=2, j=2, c=GROUP_W)
                            last = act.activation(dst[:, 2 * b:2 * b + 2, :, :], src[:, :, j, :, :], ACT.Identity,
                                                  bias=v_bias[half, bass.ds(p, 1)])
                        last.then_inc(att_ready, 1)

            act.wait_ge(att_ready, 4 + 4 * PAIRS)
            act.wait_ge(scores_done, UNITS * PAIRS)
            def gate_a(d, slot):
                act.wait_ge(gate_a_read, d + 1)
                act.activation(sig_a[:, slot, :], sig_a[:, slot, :], ACT.Sigmoid, bias=col("b_in_2", d + GA2 // P))\
                   .then_inc(gate_a_ready, 1)

            def gate_b(d):
                act.wait_ge(gate_b_read, d + 1)
                act.activation(sig_b[:, :], sig_b[:, :], ACT.Sigmoid, bias=col("b_in_2", d + GB2 // P))\
                   .then_inc(gate_b_ready, 1)

            for c in range(PAIRS):
                act.activation(att_hi[:, c, :], att_t[:, c, :], ACT.Copy).then_inc(branch_hi, 1)
            act.wait_ge(ln_summed, 1)
            act.activation(ln_mean[:, :], banks(4), ACT.Copy, scale=1.0 / CONV_CH).then_inc(ln_mean_ready, 1)
            for c in range(CT):
                act.wait_ge(ln_centred, c + 1)
                act.activation(ln_sq[:, c, :], conv_t[:, c, :], ACT.Square).then_inc(ln_sq_ready, 1)
            gate_a(0, 0)
            gate_b(0)
            act.wait_ge(ln_var, 1)
            act.activation(ln_inv[:, :], banks(6), ACT.Ln, scale=1.0 / CONV_CH, bias=eps2[:, :]).then_inc(ln_log, 1)
            act.wait_ge(ln_log, 1)
            act.activation(ln_inv[:, :], ln_inv[:, :], ACT.Exp, scale=-0.5).then_inc(ln_inv_ready, 1)
            for c in range(CT):
                act.wait_ge(ln_scaled, c + 1)
                act.activation(conv_t[:, c, :], conv_t[:, c, :], ACT.Silu, scale=col("conv_ln_g_2", c),
                               bias=col("conv_ln_b_2", c)).then_inc(ln_silu, 1)
                act.wait_ge(ln_silu, c + 1)
                act.activation(conv_hi[:, c, :], conv_t[:, c, :], ACT.Copy).then_inc(branch_hi, 1)

            with act.Fori(0, KT // 2 - 1) as i:
                for s in range(2):
                    gate_a(i * 2 + (s + 1), (s + 1) % 2)
                    gate_b(i * 2 + (s + 1))
            gate_a(KT - 1, 1)
            act.wait_ge(tile_done, T_OUT2 - 1)
            mix_hi(0, mix2, (merged, 2))
            gate_b(KT - 1)
            for d in range(1, KT - 1):
                mix_hi(d, mix2, (merged, d + 2))
            act.wait_ge(tile_done, T_OUT2)
            act.dma_start(x_t[:, :, :].rearrange("p d t -> p (d t)"), x_spill).then_inc(x_back, 16)
            mix_hi(KT - 1, mix2, (merged, KT + 1))

            def ffn_middle(c):
                for j in range(2):
                    for part, buf in enumerate((ffn_gate, ffn_val)):
                        act.wait_ge(ffn_read, c * 4 + (2 + 2 * j + part + 1))
                        act.wait_ge(act_ready, c * 2 + (2 * MLP_CHUNKS + j))
                        k = c * 2 + (part * FT2 + j)
                        act.activation(buf[:, :], ffn_z[:, part, :], ACT.Identity, scale=col("ffn_dw_w_2/1", k),
                                       bias=col("ffn_dw_b_2", k)).then_inc(ffn_mid, 1)
                    act.wait_ge(ffn_right, c * 4 + (2 * j + 1))
                    act.activation(ffn_gate[:, :], ffn_gate[:, :], ACT.Gelu).then_inc(ffn_gelu, 1)

            next_norm(4, 5, 2 + KT, SUMS_FFN, 2, T_FFN, "norm2_g_2", eps2)
            ffn_middle(0)
            split_activations(ffn_a, ffn_hi, 2 * MLP_CHUNKS, None)
            with act.Fori(0, FFN_CHUNKS - 2) as i:
                ffn_middle(i + 1)
                split_activations(ffn_a, ffn_hi, i * 2 + (2 * MLP_CHUNKS + 2), i * 6 + (T_FFN + 10))
            ffn_middle(FFN_CHUNKS - 1)
            split_activations(ffn_a, ffn_hi_last, 2 * (MLP_CHUNKS + FFN_CHUNKS) - 2, None)

            act.wait_ge(tile_done, T_END - 2)
            act.dma_start(out_gain[:, :], bass.AP(dram["norm_f_g_2"].tensor, 0, [[0, P], [1, D]]))\
               .then_inc(out_gain_loaded, 16)

            def take_back(i):
                d, t = i % KT, i // KT
                act.wait_ge(y_turned, i + 1)
                act.activation(y_tok[:, 4 * t:4 * t + 4, d * P:(d + 1) * P],
                               psum[:, i % 3, :].rearrange("p (t f) -> p t f", f=P), ACT.Copy).then_inc(y_copied, 1)

            def log_out(t):
                part = slice(4 * t, 4 * t + 4)
                act.wait_ge(norm_summed, 6 + t)
                act.activation(out_inv[:, part], psum[:, 3, part], ACT.Ln, scale=1.0 / D, bias=eps2[:, :])\
                   .then_inc(mean_log, 1)

            def inverse_out(t):
                part = slice(4 * t, 4 * t + 4)
                act.wait_ge(mean_log, 6 + t)
                act.activation(out_inv[:, part], out_inv[:, part], ACT.Exp, scale=-0.5).then_inc(out_inv_ready, 1)

            for i in range(2 * KT):
                d, t = i % KT, i // KT
                act.wait_ge(down_added, 4 + 16 * (MLP_CHUNKS + FFN_CHUNKS - 1) + i + 1)
                square(d, SUMS_OUT + (KT - 2) * t, slice(t * HALF, (t + 1) * HALF))
                if i >= 2:
                    take_back(i - 2)
                if i == KT + 3:
                    log_out(0)
                if i == KT + 4:
                    inverse_out(0)
            take_back(2 * KT - 2)
            take_back(2 * KT - 1)
            log_out(1)
            inverse_out(1)

        @block.vector
        def _(dve):
            dve.sem_inc(down_added, 4)
            dve.sem_inc(x_added, 2)
            dve.sem_inc(o_log, 1)
            dve.sem_inc(o_scaled, 1)
            dve.sem_inc(y_ready, 1)
            dve.sem_inc(up_read, 2)
            dve.sem_inc(act_split, 2)
            dve.sem_inc(att_ready, 4)
            dve.sem_inc(scores_max, 2)
            dve.sem_inc(prob_t_ready, 2)
            dve.sem_inc(prob_t_used, 2)
            for free in (branch_a, branch_b, merged):
                dve.sem_inc(free, 1)
            dve.sem_inc(ffn_read, 2)

            def add_square(d, first_sum, first_ready, part=slice(0, SEQ)):
                dve.wait_ge(sq_ready, first_ready + d + 1)
                if d >= 2:
                    dve.wait_ge(sq_summed, first_sum + d - 1)
                dve.tensor_tensor(sq_sum[:, part], sq_sum[:, part], sq[:, d % SQ_SLOTS, part], ALU.add).then_inc(sq_summed, 1)

            def lo_part(d, gain, first, part=slice(0, SEQ), nth=None):
                dve.wait_ge(h_hi_ready, first + (d if nth is None else nth) + 1)
                dve.scalar_tensor_tensor(h_lo[:, d, part], x_t[:, d, part], gain, h_hi[:, d, part].bitcast(F32),
                                         ALU.mult, ALU.subtract).then_inc(h_ready, 1)

            def take_x(t):
                dve.wait_ge(x_turned, 2 * t + 2)
                bank = 2 * t + 1 if t < 4 else 5 + 2 * (t % 2)
                dve.tensor_copy(x_t[:, 4:8, t * P:(t + 1) * P], psum[:, bank, :].rearrange("p (d t) -> p d t", t=P))\
                   .then_inc(x_copied_rest, 1)

            def split_x(q):
                dve.wait_ge(x_copied_rest, 2 * q + 2)
                for d in range(KT):
                    lo_part(d, first_gain[:, d:d + 1], H_MIX1 + KT * q, slice(q * QUARTER, (q + 1) * QUARTER))

            for q in range(4):
                take_x(2 * q)
                take_x(2 * q + 1)
                if q == 0:
                    dve.wait_ge(gain_ready, 1)
                split_x(q)
                if q == 2:
                    for d in range(1, 4):
                        add_square(d, SUMS_MIX1, 0, slice(0, HALF))
            for d in range(4, KT):
                add_square(d, SUMS_MIX1, 0, slice(0, HALF))
            for d in range(1, KT):
                add_square(d, SUMS_MIX1 + KT - 1, KT, slice(HALF, SEQ))
            def take(z, n, bank, ready):
                dve.wait_ge(tile_done, n + 1)
                dve.tensor_tensor(z[:, :], banks(bank), rinv[:, :], ALU.mult).then_inc(ready, 1)

            def take_f(h):
                take(zf, h * 4 + T_HEADS, 6 if isinstance(h, int) and h == 0 else 0, zf_ready)

            def take_q(h):
                take(zq, h * 4 + (T_HEADS + 1), 4 if isinstance(h, int) and h == 0 else 2, zq_ready)

            def take_i(h):
                take(zv, h * 4 + (T_HEADS + 2), 0, zv_ready)

            def take_g(h):
                take(zg, h * 4 + (T_HEADS + 3), 2, zg_ready)

            dve.memset(pool_u[:, :, 0:POOL_PAD], 0.0)
            dve.wait_ge(rinv_ready, 1)
            for j in range(2):
                dve.wait_ge(tile_done, T_POOL + j + 1)
                dve.tensor_tensor(pool_u[:, j, POOL_PAD:], banks(2 * j), rinv[:, :], ALU.mult).then_inc(pool_u_ready, 1)
            dve.memset(pool_w[:, :, :], 0.0).then_inc(pool_w_zeroed, 1)
            take_f(0)
            dve.memset(pool_a[:, 0:POOL_PAD], 0.0)
            dve.memset(pool_b[:, 0:POOL_PAD], 0.0).then_inc(pool_step, 1)
            steps = 1
            dve.wait_ge(pool_inv_loaded, 16)
            for j in range(2):
                dve.wait_ge(pool_u_ready, j + 1)
                src, sums, shift = pool_u[:, j, :], [], 1
                spare = [pool_a, pool_b]
                for n in range(2 * j + 2):
                    dst = spare[n % 2][:, :]
                    dve.wait_ge(pool_step, steps)
                    dve.tensor_tensor(dst[:, POOL_PAD:], src[:, POOL_PAD:], src[:, POOL_PAD - shift:PADDED - shift],
                                      ALU.add).then_inc(pool_step, 1)
                    steps += 1
                    sums.append(dst)
                    src, shift = dst, 2 * shift
                dve.wait_ge(pool_step, steps)
                for half, window_sum in ((slice(0, 64), sums[-2]), (slice(64, P), sums[-1])):
                    dve.tensor_tensor(pool_p[half, j, :], window_sum[half, POOL_PAD:], pool_inv[half, j, :],
                                      ALU.mult).then_inc(pool_step, 1)
                    steps += 1
                dve.wait_ge(pool_step, steps)
                dve.tensor_tensor(pool_p[:, j, :], pool_p[:, j, :], pool_u[:, j, POOL_PAD:], ALU.subtract)\
                   .then_inc(pool_p_ready, 1)

            take_q(0)
            take_i(0)
            dve.wait_ge(cols_ready, 1)
            both, g1, b = COL["final_norm_g"], COL["norm1_g_2"], COL["b_in_2"] + Q2 // P
            dve.tensor_tensor(gain_both[:, :], cols[:, both:both + KT], cols[:, g1:g1 + KT], ALU.mult)
            dve.tensor_tensor(gain_sq[:, :], cols[:, both:both + KT], cols[:, both:both + KT], ALU.mult)
            dve.tensor_scalar(q_bias[:, 0:PAIRS], cols[:, b:b + PAIRS], DH ** -0.5, None, ALU.mult)
            dve.wait_ge(x_spilled, 16)
            dve.wait_ge(pool_ready, 2)
            dve.wait_ge(cols_turned, 1)
            dve.wait_ge(rpb_stored, 16 * 3)
            dve.memset(s_t[:, :], 0.0).then_inc(pool_step, 1)
            steps += 1
            dve.wait_ge(pool_step, steps)

            def mix_lo(m, d, mix):
                dve.wait_ge(mix_hi_ready, KT * m + d + 1)
                dve.tensor_tensor(h_lo[:, d, :], mix[:, d, :], h_hi[:, d, :].bitcast(F32),
                                  ALU.subtract).then_inc(mix_split, 1)

            def head(h, last):
                def decay_of(l):
                    first = 2 * SEQ - (2 * SEQ >> l)
                    return decays[:, first:first + (SEQ >> l)].rearrange("p (n two) -> p n two", two=2)

                def move(l):
                    n, s = SEQ >> (l + 1), 1 << l
                    decay, twice = decay_of(l), 2 * SEQ - (2 * SEQ >> (l + 1))
                    q, k = level_parts(qd_t[:, :], l)[:, :, 1, :], level_parts(kd_t[:, :], l)[:, :, 0, :]
                    dve.wait_ge(level_ready, h * LEVELS + (l + 1))
                    dve.tensor_tensor(q, q, decay[:, :, 0:1].to_broadcast([P, n, s]), ALU.mult)
                    dve.tensor_tensor(k, k, decay[:, :, 1:2].to_broadcast([P, n, s]), ALU.mult)
                    dve.tensor_tensor(decays[:, twice:twice + n], decay[:, :, 0], decay[:, :, 1], ALU.mult)\
                       .then_inc(level_moved, 1)

                def merge_diagonal():
                    dve.wait_ge(level_done, h * (LEVELS + 1) + 1)
                    dve.sem_inc(dve_passed, 1)
                    mask = pair_mask[:, LEVELS * CHUNK // 2:].bitcast(U32).unsqueeze(1).to_broadcast([P, NC, CHUNK])
                    dve.copy_predicated(s_t[:, :].rearrange("p (c t) -> p c t", t=CHUNK), mask,
                                        banks(6).rearrange("p (c t) -> p c t", t=CHUNK)).then_inc(level_merged, 1)

                def merge(l, bank):
                    n, s = CHUNK >> (l + 1), 1 << l
                    dve.wait_ge(level_merged, h * (LEVELS + 1) + (l + 1))
                    dve.wait_ge(level_done, h * (LEVELS + 1) + (l + 2))
                    dve.sem_inc(dve_passed, 1)
                    keys = CHUNK if l < LEVELS - 1 else CHUNK // 2
                    mask = pair_mask[0:keys, l * CHUNK // 2:(l + 1) * CHUNK // 2].bitcast(U32)\
                        .rearrange("p (n s) -> p n s", s=s).unsqueeze(1).to_broadcast([keys, NC, n, s])
                    right = s_t[0:keys, :].rearrange("p (c n two s) -> p c n two s", c=NC, two=2, s=s)[:, :, :, 1, :]
                    dve.copy_predicated(right, mask, psum[0:keys, bank, :].rearrange("p (c n s) -> p c n s", c=NC, s=s))\
                       .then_inc(level_merged, 1)

                def begin_mix(*tiles):
                    if last:
                        for d in tiles:
                            mix_lo(0, d, mix1)

                dve.wait_ge(q_gate, h + 1)
                dve.tensor_tensor(q_t[:, :], zq[:, :], q_t[:, :], ALU.mult).then_inc(q_ready, 1)
                dve.wait_ge(q_ready, h + 1)
                dve.wait_ge(f_ready, h + 1)
                dve.tensor_tensor(qd_t[:, :], q_t[:, :], decays[:, 0:SEQ], ALU.mult).then_inc(qd_start, 1)
                move(0)
                move(1)
                take_g(h)
                merge_diagonal()
                merge(0, 4)
                begin_mix(0)
                move(2)
                begin_mix(1)
                merge(1, 5)
                begin_mix(2, 3)
                dve.wait_ge(g_gate, h + 1)
                dve.tensor_tensor(sg_t[:, :], zg[:, :], sg_t[:, :], ALU.mult).then_inc(sg_ready, 1)
                move(3)
                begin_mix(4, 5, 6)
                if not last:
                    dve.wait_ge(k_ready, h + 1)
                    take_f(h + 1)
                merge(2, 4)
                move(4)
                merge(3, 5)
                move(5)
                merge(4, 6)
                move(6)
                merge(5, 4)
                if not last:
                    take_q(h + 1)
                merge(6, 5)
                chunk_decay = 2 * SEQ - (2 * SEQ >> LEVELS)
                dve.wait_ge(level_moved, h * LEVELS + LEVELS)
                dve.wait_ge(update_done, h + 1)
                for c in range(NC - 1):
                    update = psum[:, 4 + c // 4, (c % 4) * P:(c % 4 + 1) * P]
                    if c == 0:
                        dve.tensor_copy(states[:, 1, :], update).then_inc(state_ready, 1)
                    else:
                        dve.wait_ge(state_ready, h * (NC - 1) + c)
                        dve.scalar_tensor_tensor(states[:, c + 1, :], states[:, c, :],
                                                 decays[:, chunk_decay + c:chunk_decay + c + 1], update,
                                                 ALU.mult, ALU.add).then_inc(state_ready, 1)
                if not last:
                    dve.wait_ge(v_turned, h + 1)
                    take_i(h + 1)
                dve.wait_ge(o_inv, h + 1)
                dve.tensor_tensor(e_t[:, 1, :], banks(6), e_t[:, 0, :], ALU.mult).then_inc(o_scaled, 1)
                dve.wait_ge(o_scaled, h + 2)
                dve.wait_ge(sg_ready, h + 1)
                y = mix1[:, h + 2, :] if isinstance(h, int) else \
                    mix1[:, bass.ds(h + 2, 1), :].rearrange("p a t -> p (a t)")
                dve.scalar_tensor_tensor(y, e_t[:, 1, :], col("hgrn_norm_g", h), sg_t[:, :], ALU.mult, ALU.mult)\
                   .then_inc(y_ready, 1)

            with dve.Fori(0, HEADS - 1) as i:
                head(i, False)
            head(HEADS - 1, True)
            mix_lo(0, KT - 1, mix1)

            def add_out(first_tile, first_banks, first_sum, first_ready, gain, first_h):
                def lo_halves(halves):
                    for d, t in halves:
                        lo_part(d, col(gain, d), first_h, slice(t * HALF, (t + 1) * HALF), HALVES.index((d, t)))

                for d in range(KT):
                    if d == KT - 1:
                        lo_halves(HALVES_AHEAD)
                        dve.wait_ge(x_back_last, 16)
                    dve.wait_ge(tile_done, first_tile + d + 1)
                    dve.tensor_tensor(x_t[:, d, :], x_t[:, d, :], banks(2 * d if d < first_banks else 2 * (d % 2)),
                                      ALU.add).then_inc(x_added, 1)
                    if 2 <= d < KT - 1:
                        add_square(d - 1, first_sum, first_ready)
                lo_halves(HALVES_BEHIND)
                for d in range(KT - 2, KT):
                    add_square(d, first_sum, first_ready)

            dve.wait_ge(x_back, 16)
            add_out(T_OUT1, 4, SUMS_MLP, 2 * KT, "norm_mlp_g", H_MLP)

            def add_down(c, n, first_chunk, after_group=lambda g: None):
                for part in range(2):
                    for g in range(8):
                        if g < 7:
                            dve.wait_ge(down_done, c * 14 + (14 * first_chunk + 7 * part + g + 1))
                        else:
                            dve.wait_ge(tile_done, n + (part + 1))
                        x_d = x_t[:, 4 * part + g // 2, (g % 2) * HALF:(g % 2 + 1) * HALF]
                        dve.tensor_tensor(x_d, x_d, psum[:, 4 + g % 4, :], ALU.add).then_inc(down_added, 1)
                        after_group(8 * part + g)

            def lo_activations(a, hi, lo, first):
                for j in range(2):
                    dve.wait_ge(act_hi_ready, first + (j + 1))
                    dve.tensor_tensor(lo[:, j, :], a[:, j, :], hi[:, j, :].bitcast(F32),
                                      ALU.subtract).then_inc(act_split, 1)

            def mlp_relu(c, n):
                for j in range(2):
                    dve.wait_ge(tile_done, n + (j + 1))
                    dve.wait_ge(act_split, c * 2 + (j + 1))
                    dve.scalar_tensor_tensor(mlp_a[:, j, :], banks(2 * j), 0.0, rinv[:, :], ALU.max, ALU.mult)\
                       .then_inc(up_read, 1)

            dve.wait_ge(rinv_ready, 2)
            mlp_relu(0, T_MLP)
            lo_activations(mlp_a, mlp_hi, mlp_lo, 0)
            with dve.Fori(0, MLP_CHUNKS - 2) as i:
                mlp_relu(i + 1, i * 4 + (T_MLP + 2))
                add_down(i, i * 4 + (T_MLP + 4), 0)
                lo_activations(mlp_a, mlp_hi, mlp_lo, i * 2 + 2)
            mlp_relu(MLP_CHUNKS - 1, T_CB - 6)
            add_down(MLP_CHUNKS - 2, T_CB - 4, 0, lambda g: lo_activations(
                mlp_a, mlp_hi_last, mlp_lo_last, 2 * MLP_CHUNKS - 2) if g == 5 else None)

            def block_lo(d):
                lo_part(d, gain_both[:, d:d + 1], H_MIX2)

            def sum_plain(d, done):
                dve.wait_ge(sq_ready, 3 * KT + d + 1)
                dve.wait_ge(sq_summed, SUMS_MIX2 + done)
                dve.tensor_tensor(sq_sum[:, :], sq_sum[:, :], sq[:, d % SQ_SLOTS, :], ALU.add).then_inc(sq_summed, 1)

            def sum_gained(d, done):
                dve.wait_ge(sq_ready, 3 * KT + d + 1)
                if d == 0:
                    dve.tensor_scalar(sq_sum_gain[:, :], sq_sum[:, :], gain_sq[:, 0:1], None, ALU.mult)\
                       .then_inc(sq_summed, 1)
                else:
                    dve.wait_ge(sq_summed, SUMS_MIX2 + done)
                    dve.scalar_tensor_tensor(sq_sum_gain[:, :], sq[:, d % SQ_SLOTS, :], gain_sq[:, d:d + 1],
                                             sq_sum_gain[:, :], ALU.mult, ALU.add).then_inc(sq_summed, 1)

            between_adds = [(block_lo, 0), (sum_gained, 0, 0)]
            for d in range(1, 4):
                between_adds += [(block_lo, d), (sum_plain, d, 2 * d - 1), (sum_gained, d, 2 * d)]

            def after_group(g):
                if 3 <= g < 3 + len(between_adds):
                    step, *arguments = between_adds[g - 3]
                    step(*arguments)

            add_down(MLP_CHUNKS - 1, T_CB - 2, 0, after_group)
            for d in range(4, KT):
                block_lo(d)
            for d in range(4, KT):
                sum_plain(d, d + 3)
            for d in range(4, KT):
                sum_gained(d, d + KT - 1)
            dve.wait_ge(block_rinv1, 1)
            dve.wait_ge(norm_summed, 4)
            dve.tensor_tensor(rinv[:, :], rinv[:, :], banks(6), ALU.mult).then_inc(block_mean, 1)
            dve.wait_ge(rinv_ready, 3)
            dve.tensor_tensor(rinv[:, :], rinv[:, :], rinv1[:, :], ALU.mult).then_inc(rinv_ready, 1)
            dve.wait_ge(rinv_ready, 4)

            for c in range(CT):
                dve.wait_ge(tile_done, T_CB + c + 1)
                dve.tensor_tensor(sig_cb[:, c, :], banks(2 * c), rinv[:, :], ALU.mult).then_inc(cb_read, 1)
                if c == 1:
                    for d in range(KT):
                        dve.scalar_tensor_tensor(x_t[:, d, :], x_t[:, d, :], col("final_norm_g", d), rinv1[:, :],
                                                 ALU.mult, ALU.mult).then_inc(x_ready, 1)
            dve.wait_ge(x_ready, KT)

            dve.memset(u_t[:, 0:CONV_PAD], 0.0)
            dve.memset(u_t[:, CONV_PAD + SEQ:], 0.0).then_inc(u_zeroed, 1)
            dve.wait_ge(u_zeroed, 1)

            with dve.Fori(0, PAIRS) as p:
                def convolve(taps):
                    acc = conv_t[:, bass.ds(p, 1), :].rearrange("p a t -> p (a t)")
                    for tap in taps:
                        w = col("conv_dw_w_2", p * CONV_K + tap)
                        if tap == 0:
                            dve.tensor_scalar(acc, u_t[:, 0:SEQ], w, col("conv_dw_b_2", p), ALU.mult, ALU.add)\
                               .then_inc(conv_step, 1)
                        else:
                            dve.wait_ge(conv_step, p * CONV_STEPS + tap)
                            dve.scalar_tensor_tensor(acc, u_t[:, tap:tap + SEQ], w, acc, ALU.mult, ALU.add)\
                               .then_inc(conv_step, 1)

                u = u_t[:, CONV_PAD:CONV_PAD + SEQ]
                dve.wait_ge(tile_done, p * 4 + (T_PAIRS + 1))
                dve.tensor_tensor(u, banks(2), rinv[:, :], ALU.mult).then_inc(u_read, 1)
                dve.wait_ge(u_read, p + 1)
                dve.wait_ge(cb_ready, CT)
                dve.scalar_tensor_tensor(u, u, col("b_in_2", p + CA2 // P),
                                         sig_cb[:, bass.ds(p, 1), :].rearrange("p a t -> p (a t)"),
                                         ALU.add, ALU.mult).then_inc(u_ready, 1)
                dve.wait_ge(u_ready, p + 1)
                dve.wait_ge(x_spilled, 16 * (1 + SPILLS))
                convolve(range(0, 5))
                dve.wait_ge(tile_done, p * 4 + (T_PAIRS + 2))
                dve.tensor_tensor(by_group(qk32[:, :]), by_row(banks(0)), by_row(rinv[:, :]), ALU.mult)\
                   .then_inc(q_read, 1)
                dve.wait_ge(mask_loaded, 16)
                dve.wait_ge(bias_loaded, p * 16 + 16)
                dve.tensor_tensor(bias[:, :, 0:5:2, :], bias_raw[:, :, :, :],
                                  near_mask[:, 0:1, :].unsqueeze(1).to_broadcast([P, 2, 3, P]), ALU.add)
                dve.tensor_tensor(bias[:, :, 1:4:2, :], bias_raw[:, :, 0:3:2, :],
                                  near_mask[:, 1:3, :].unsqueeze(1).to_broadcast([P, 2, 2, P]),
                                  ALU.add).then_inc(bias_ready, 1)
                convolve(range(5, 7))
                dve.wait_ge(q_hi_ready, p + 1)
                dve.tensor_tensor(q_lo[:, :], qk32[:, :], q_hi[:, :].bitcast(F32), ALU.subtract).then_inc(q_split, 1)
                convolve(range(7, 11))
                dve.wait_ge(q_split, p + 1)
                dve.wait_ge(tile_done, p * 4 + (T_PAIRS + 3))
                dve.tensor_tensor(by_group(qk32[:, :]), by_row(banks(2)), by_row(rinv[:, :]), ALU.mult)\
                   .then_inc(k_read, 1)
                convolve(range(11, 13))
                dve.wait_ge(k_hi_ready, p + 1)
                dve.tensor_tensor(k_lo[:, :], qk32[:, :], k_hi[:, :].bitcast(F32), ALU.subtract).then_inc(k_split, 1)
                convolve(range(13, DVE_TAPS - TAIL_TAPS))
                dve.wait_ge(bias_ready, p + 1)
                for s in range(UNITS + 1):
                    if s < UNITS:
                        dve.wait_ge(scores_done, p * UNITS + (s + 1))
                        dve.sem_inc(dve_passed, 1)
                        g, j = s // 2, s % 2
                        first, n = key_groups(g)
                        at_b, step = {0: (2, 2), GROUPS - 1: (0, 2)}.get(g, (1, 1))
                        dve.tensor_tensor_reduce(
                            out=prob[:, s % 3, 0:n * P].rearrange("p (m k) -> p m k", k=P),
                            in0=psum[:, 4 + s % 2, 0:n * P].rearrange("p (m k) -> p m k", k=P),
                            in1=bias[:, j, at_b:at_b + step * (n - 1) + 1:step, :], scale=1.0, scalar=3 * NEG,
                            op0=ALU.add, op1=ALU.max, accum_out=row_max[:, s % 2:s % 2 + 1]).then_inc(scores_max, 1)
                        dve.wait_ge(scores_max, p * UNITS + (s + 3))
                        dve.tensor_scalar(neg_max[:, s % 2:s % 2 + 1], row_max[:, s % 2:s % 2 + 1], -1.0, None,
                                          ALU.mult).then_inc(neg_max_ready, 1)
                    if s >= 1:
                        u = s - 1
                        n = key_groups(u // 2)[1] * P
                        dve.wait_ge(prob_exp, p * UNITS + (u + 1))
                        dve.reciprocal(row_inv[:, u % 2:u % 2 + 1], row_sum[:, u % 2:u % 2 + 1]).then_inc(inv_ready, 1)
                        dve.wait_ge(inv_ready, p * UNITS + (u + 1))
                        dve.tensor_scalar(prob[:, u % 3, 0:n], prob[:, u % 3, 0:n], row_inv[:, u % 2:u % 2 + 1], None,
                                          ALU.mult).then_inc(prob_ready, 1)
                    if s == 1:
                        dve.wait_ge(tile_done, p * 4 + (T_PAIRS + 4))
                        dve.tensor_tensor(by_group(v_t[:, :]), by_row(banks(0)), by_row(rinv[:, :]), ALU.mult)\
                           .then_inc(v_read, 1)
                convolve(range(DVE_TAPS - TAIL_TAPS, DVE_TAPS))
                dve.wait_ge(conv_step, p * CONV_STEPS + DVE_TAPS)
                dve.wait_ge(tap_added, p * (POOL_TAPS - 1) + (POOL_TAPS - 1))
                acc = conv_t[:, bass.ds(p, 1), :].rearrange("p a t -> p (a t)")
                dve.tensor_tensor(acc, acc, conv_pool[:, :], ALU.add).then_inc(conv_step, 1)

            dve.wait_ge(conv_step, CONV_STEPS * CT)
            dve.wait_ge(prob_turned, UNITS * PAIRS)
            for c in range(1, CT):
                if c >= 2:
                    dve.wait_ge(ln_added, c - 1)
                dve.tensor_tensor(ln_inv[:, :], conv_t[:, 0, :] if c == 1 else ln_inv[:, :], conv_t[:, c, :],
                                  ALU.add).then_inc(ln_added, 1)

            def gate_a(d, n, slot):
                dve.wait_ge(tile_done, n + 1)
                dve.wait_ge(merged, d if not isinstance(d, int) or d >= 1 else 1)
                dve.tensor_tensor(sig_a[:, slot, :], banks(2), rinv[:, :], ALU.mult).then_inc(gate_a_read, 1)

            def gate_b(d, n):
                dve.wait_ge(tile_done, n + 1)
                dve.wait_ge(merged, d + 1)
                dve.tensor_tensor(sig_b[:, :], banks(0), rinv[:, :], ALU.mult).then_inc(gate_b_read, 1)

            gate_a(0, T_MERGE, 0)
            for c in range(PAIRS):
                dve.wait_ge(branch_hi, c + 1)
                dve.tensor_tensor(att_lo[:, c, :], att_t[:, c, :], att_hi[:, c, :].bitcast(F32), ALU.subtract)\
                   .then_inc(branch_split, 1)
            dve.wait_ge(ln_mean_ready, 1)
            for c in range(CT):
                dve.tensor_tensor(conv_t[:, c, :], conv_t[:, c, :], ln_mean[:, :], ALU.subtract).then_inc(ln_centred, 1)
            for c in range(1, CT):
                dve.wait_ge(ln_sq_ready, c + 1)
                if c >= 2:
                    dve.wait_ge(ln_added, CT - 1 + c - 1)
                dve.tensor_tensor(ln_sq[:, 0, :], ln_sq[:, 0, :], ln_sq[:, c, :], ALU.add).then_inc(ln_added, 1)
            gate_b(0, T_MERGE + 1)
            dve.wait_ge(ln_inv_ready, 1)
            for c in range(CT):
                dve.tensor_tensor(conv_t[:, c, :], conv_t[:, c, :], ln_inv[:, :], ALU.mult).then_inc(ln_scaled, 1)
            for c in range(CT):
                dve.wait_ge(branch_hi, PAIRS + c + 1)
                dve.tensor_tensor(conv_lo[:, c, :], conv_t[:, c, :], conv_hi[:, c, :].bitcast(F32), ALU.subtract)\
                   .then_inc(branch_split, 1)

            def merge(d, n, slot):
                dve.wait_ge(tile_done, n + 1)
                dve.wait_ge(gate_a_ready, d + 1)
                dve.tensor_tensor(sig_a[:, slot, :], sig_a[:, slot, :], banks(4), ALU.mult).then_inc(branch_a, 1)
                dve.wait_ge(gate_b_ready, d + 1)
                dve.tensor_tensor(sig_b[:, :], sig_b[:, :], banks(6), ALU.mult).then_inc(branch_b, 1)
                dve.wait_ge(branch_a, d + 2)
                dve.wait_ge(branch_b, d + 2)
                dst = mix2[:, d, :] if isinstance(d, int) else \
                    mix2[:, bass.ds(d, 1), :].rearrange("p a t -> p (a t)")
                dve.tensor_tensor(dst, sig_a[:, slot, :], sig_b[:, :], ALU.add).then_inc(merged, 1)

            def merge_step(d, n, slot):
                gate_a(d + 1, n, 1 - slot)
                merge(d, n + 2, slot)
                gate_b(d + 1, n + 1)

            with dve.Fori(0, KT // 2 - 1) as i:
                for s in range(2):
                    merge_step(i * 2 + s, i * 6 + (T_MERGE + 2 + 3 * s), s)
            gate_a(KT - 1, T_OUT2 - 4, 1)
            merge(KT - 2, T_OUT2 - 3, 0)
            gate_b(KT - 1, T_OUT2 - 2)
            for d in range(KT - 1):
                mix_lo(1, d, mix2)
            merge(KT - 1, T_OUT2 - 1, 1)
            mix_lo(1, KT - 1, mix2)
            dve.wait_ge(x_back, 32)
            add_out(T_OUT2, 2, SUMS_FFN, 4 * KT, "norm2_g_2", H_FFN)

            def ffn_read_out(c, n, j):
                for part in range(2):
                    tile = c * 4 + (2 * j + part)
                    dve.wait_ge(tile_done, n + (2 * j + part + 1))
                    if not isinstance(c, int) or j == 1:
                        dve.wait_ge(ffn_right, tile - 1)
                    dve.tensor_tensor(ffn_z[:, part, :], banks(2 * part), rinv[:, :], ALU.mult).then_inc(ffn_read, 1)

            def ffn_steps(c, j):
                def tap(part, buf, left):
                    tile, k = c * 4 + (2 * j + part), c * 2 + (part * FT2 + j)
                    if left:
                        dve.wait_ge(ffn_mid, tile + 1)
                        dve.scalar_tensor_tensor(buf[:, 1:], ffn_z[:, part, 0:SEQ - 1], col("ffn_dw_w_2/0", k),
                                                 buf[:, 1:], ALU.mult, ALU.add).then_inc(ffn_left, 1)
                    else:
                        dve.wait_ge(ffn_left, tile + 1)
                        dve.scalar_tensor_tensor(buf[:, 0:SEQ - 1], ffn_z[:, part, 1:], col("ffn_dw_w_2/2", k),
                                                 buf[:, 0:SEQ - 1], ALU.mult, ALU.add).then_inc(ffn_right, 1)

                def gate():
                    dve.wait_ge(ffn_gelu, c * 2 + (j + 1))
                    dve.wait_ge(ffn_right, c * 4 + (2 * j + 2))
                    dve.tensor_tensor(ffn_a[:, j, :], ffn_gate[:, :], ffn_val[:, :], ALU.mult).then_inc(act_ready, 1)

                return [lambda: tap(0, ffn_gate, True), lambda: tap(0, ffn_gate, False),
                        lambda: tap(1, ffn_val, True), lambda: tap(1, ffn_val, False), gate]

            def ffn_first(c, n):
                ffn_read_out(c, n, 0)
                for step in ffn_steps(c, 0):
                    step()
                ffn_read_out(c, n, 1)

            dve.wait_ge(rinv_ready, 5)
            ffn_first(0, T_FFN)
            for step in ffn_steps(0, 1):
                step()
            lo_activations(ffn_a, ffn_hi, ffn_lo, 2 * MLP_CHUNKS)
            def ffn_second(c, n, more=None):
                steps = ffn_steps(c + 1, 1)
                if more is not None:
                    steps += [lambda: None, more]
                add_down(c, n, MLP_CHUNKS, lambda g: steps[g]() if g < len(steps) else None)

            with dve.Fori(0, FFN_CHUNKS - 2) as i:
                ffn_first(i + 1, i * 6 + (T_FFN + 4))
                ffn_second(i, i * 6 + (T_FFN + 8))
                lo_activations(ffn_a, ffn_hi, ffn_lo, i * 2 + (2 * MLP_CHUNKS + 2))
            ffn_first(FFN_CHUNKS - 1, T_END - 8)
            ffn_second(FFN_CHUNKS - 2, T_END - 4, lambda: lo_activations(
                ffn_a, ffn_hi_last, ffn_lo_last, 2 * (MLP_CHUNKS + FFN_CHUNKS) - 2))

            def scale_out(t):
                dve.wait_ge(y_copied, KT * (t // 4 + 1))
                dve.wait_ge(out_inv_ready, t // 4 + 1)
                dve.scalar_tensor_tensor(y_tok[:, t, :], y_tok[:, t, :], out_inv[:, t:t + 1], out_gain[:, :],
                                         ALU.mult, ALU.mult).then_inc(out_ready, 1)

            for i in range(2 * KT):
                d, t = i % KT, i // KT
                dve.wait_ge(down_done, 14 * (MLP_CHUNKS + FFN_CHUNKS - 1) + i + 1)
                x_d = x_t[:, d, t * HALF:(t + 1) * HALF]
                dve.tensor_tensor(x_d, x_d, psum[:, 4 + i % 4, :], ALU.add).then_inc(down_added, 1)
                if i == KT + 5:
                    dve.wait_ge(out_gain_loaded, 16)
                if i >= KT + 5:
                    scale_out(i - KT - 5)
            for t in range(3, KT):
                scale_out(t)


_INS = ["x", "norm_mix_g", "w_in", "pool_w", "pool_scale", "hgrn_norm_g", "w_out", "norm_mlp_g", "w_up", "w_down",
        "final_norm_g", "norm1_g_2", "w_in_2", "b_in_2", "rpb_2", "w_na_out_2", "conv_dw_w_2", "conv_dw_b_2",
        "conv_ln_g_2", "conv_ln_b_2", "w_conv_out_2", "w_out_2", "norm2_g_2", "w_up_2", "ffn_dw_w_2", "ffn_dw_b_2",
        "w_down_2", "norm_f_g_2"]


def _constants():
    import numpy as np

    s, t = np.arange(CHUNK)[:, None], np.arange(CHUNK)[None, :]
    masks = [(((s >> (l + 1)) == (t >> (l + 1))) & ((s >> l) & 1 == 0))[:, (t[0] >> l) & 1 == 1] for l in range(LEVELS)]
    masks.append(s == t)
    tokens = np.arange(1, SEQ + 1)
    windows = np.repeat(np.array(POOL_WINDOWS), POOL_W // len(POOL_WINDOWS))
    inv = 1.0 / np.minimum(tokens[None, :], windows[:, None])
    row, c = np.arange(P) // GROUP_W, np.arange(P) % GROUP_W
    first = np.clip(row - KH // 2, 0, ROWS - KH)[:, None]
    seen = (row[None, :] >= first) & (row[None, :] < first + KH)
    near = np.stack([seen, seen & (c[None, :] >= c[:, None]), seen & (c[None, :] < c[:, None])], axis=1)
    return {
        "c_ident": np.eye(P, dtype=np.float32),
        "c_pair_mask": np.concatenate(masks, axis=1).astype(np.float32),
        "c_pool_inv": np.ascontiguousarray(inv.reshape(2, P, SEQ).transpose(1, 0, 2)).astype(np.float32),
        "c_near_mask": np.where(near, 0.0, NEG).astype(np.float32),
    }


def kernel(**inputs):
    import numpy as np
    import concourse.bacc as bacc
    from concourse.bass_utils import run_bass_kernel_spmd as run

    nc = bacc.Bacc("TRN2", target_bir_lowering=False, num_devices=1)
    arrays, dram = {}, {}
    given = {name: np.ascontiguousarray(inputs[name]) for name in _INS} | _constants()
    for name, a in given.items():
        if name not in ("x", "final_norm_g", "norm_f_g_2") and not name.startswith("c_"):
            a = a[0]
        arrays[f"in_{name}"] = a
        dram[name] = nc.dram_tensor(f"in_{name}", a.shape, mybir.dt.from_np(a.dtype), kind="ExternalInput").ap()
    out = nc.dram_tensor("out", (1, SEQ, D), F32, kind="ExternalOutput").ap()
    two_blocks(nc, dram, out)
    return run(nc, [arrays], core_ids=[0]).results[0]["out"]
```
